# Optimizing a Trainium2 kernel written in Bass

```python
import jax
import jax.numpy as jnp
from jax import lax
import numpy as np

D_MODEL = 1024
BATCH = 1
SEQ = 256
DEPTH = 2

POOL_WIDTH = D_MODEL // 4
POOL_GROUPS = 4
POOL_GROUP_WIDTH = POOL_WIDTH // POOL_GROUPS
POOL_WINDOWS = (2, 4, 8, 16)
LRU_WIDTH = D_MODEL // 4
LRU_BLOCKS = 4
LRU_BLOCK_WIDTH = LRU_WIDTH // LRU_BLOCKS
CONV_WIDTH = 4
LRU_C = 8.0
HEAD_DIM = 64
ATTN_WIDTH = D_MODEL - POOL_WIDTH - LRU_WIDTH
N_ATTN_HEADS = ATTN_WIDTH // HEAD_DIM
DILATED_PATTERNS = ((128, 1), (512, 4), (2048, 16))
ATTN_BLOCK = 128
ROPE_THETA = 10000.0
IN_WIDTH = POOL_WIDTH + 2 * LRU_WIDTH + 3 * ATTN_WIDTH
N_EXPERTS = 32
TOP_K = 4
EXPERT_FF = D_MODEL // 4
MOE_BLOCK = 512
SWIGLU_LIMIT = 7.0
SWIGLU_ALPHA = 1.702
NORM_EPS = 1e-6
NEG_INF = -1e30

kernel_name = 'hybrid_pool_rglru_dilated_attn_moe'

def _rms_norm(x, g):
    x32 = x.astype(jnp.float32)
    y = x32 * lax.rsqrt(jnp.mean(x32 * x32, axis=-1, keepdims=True) + NORM_EPS)
    return (y * g.astype(jnp.float32)).astype(x.dtype)

def _rope_tables(seq_len):
    pos = jnp.arange(seq_len, dtype=jnp.float32)
    inv_freq = ROPE_THETA ** (-jnp.arange(0, HEAD_DIM, 2, dtype=jnp.float32) / HEAD_DIM)
    ang = pos[:, None] * inv_freq[None, :]
    return jnp.cos(ang)[None, :, None, :], jnp.sin(ang)[None, :, None, :]

def _rope(x, cos, sin):
    half = HEAD_DIM // 2
    x1, x2 = x[..., :half], x[..., half:]
    return jnp.concatenate([x1 * cos - x2 * sin, x2 * cos + x1 * sin], axis=-1)

def _pool_mixer(u, pool_w, pool_scale):
    b, s, _ = u.shape
    u32 = u.astype(jnp.float32).reshape(b, s, POOL_GROUPS, POOL_GROUP_WIDTH)
    csum = lax.cumsum(u32, axis=1)
    count = jnp.arange(1, s + 1, dtype=jnp.float32)[None, :, None]
    means = []
    for g, w in enumerate(POOL_WINDOWS):
        cg = csum[:, :, g]
        lagged = jnp.pad(cg, ((0, 0), (w, 0), (0, 0)))[:, :s]
        means.append((cg - lagged) / jnp.minimum(count, float(w)))
    pooled = jnp.stack(means, axis=2) - u32
    y = jnp.einsum('bsgc,gce->bsge', pooled, pool_w.astype(jnp.float32)).reshape(b, s, POOL_WIDTH)
    return y * pool_scale.astype(jnp.float32)

def _lru_combine(left, right):
    a1, b1 = left
    a2, b2 = right
    return a1 * a2, a2 * b1 + b2

def _rglru_mixer(u, gate_in, conv_w, conv_b, wa, ba, wx, bx, lam):
    b, s, _ = u.shape
    up = jnp.pad(u, ((0, 0), (CONV_WIDTH - 1, 0), (0, 0)))
    xc = conv_b.astype(jnp.float32)
    for j in range(CONV_WIDTH):
        xc = xc + conv_w[j].astype(jnp.float32) * up[:, j:j + s].astype(jnp.float32)
    xblk = xc.reshape(b, s, LRU_BLOCKS, LRU_BLOCK_WIDTH)
    r = jax.nn.sigmoid(jnp.einsum('bsnc,nce->bsne', xblk, wa.astype(jnp.float32)).reshape(b, s, LRU_WIDTH) + ba)
    i = jax.nn.sigmoid(jnp.einsum('bsnc,nce->bsne', xblk, wx.astype(jnp.float32)).reshape(b, s, LRU_WIDTH) + bx)
    log_a = -LRU_C * r * jax.nn.softplus(-lam.astype(jnp.float32))
    a = jnp.exp(log_a)
    mult = jnp.sqrt(-jnp.expm1(2.0 * log_a))
    mult = mult.at[:, 0].set(1.0)
    _, h = lax.associative_scan(_lru_combine, (a, mult * (i * xc)), axis=1)
    return h * jax.nn.gelu(gate_in.astype(jnp.float32))

def _dilated_branch(q, k, v, window, dilation):
    b, s, h, dh = q.shape
    span = window // dilation
    sub = s // dilation
    n_blk = -(-sub // ATTN_BLOCK)
    pad = n_blk * ATTN_BLOCK - sub

    def to_blocks(t):
        t = t.reshape(b, sub, dilation, h, dh)
        t = jnp.pad(t, ((0, 0), (0, pad), (0, 0), (0, 0), (0, 0)))
        return t.reshape(b, n_blk, ATTN_BLOCK, dilation, h, dh)

    def with_previous(t):
        prev = jnp.pad(t, ((0, 0), (1, 0), (0, 0), (0, 0), (0, 0), (0, 0)))[:, :n_blk]
        return jnp.concatenate([prev, t], axis=2)

    qb = to_blocks(q)
    kb = with_previous(to_blocks(k))
    vb = with_previous(to_blocks(v))
    scores = jnp.einsum('bnqrhd,bnkrhd->bnrhqk', qb, kb) * (HEAD_DIM ** -0.5)
    qi = jnp.arange(ATTN_BLOCK)[:, None]
    kj = jnp.arange(2 * ATTN_BLOCK)[None, :]
    dist = qi + ATTN_BLOCK - kj
    band = (dist >= 0) & (dist <= span)
    valid = band[None] & ((jnp.arange(n_blk)[:, None, None] > 0) | (kj[None] >= ATTN_BLOCK))
    scores = jnp.where(valid[None, :, None, None], scores, NEG_INF)
    row_max = jnp.max(scores, axis=-1)
    p = jnp.exp(scores - row_max[..., None])
    den = jnp.sum(p, axis=-1)
    num = jnp.einsum('bnrhqk,bnkrhd->bnqrhd', p, vb)

    def from_blocks(t):
        t1 = t.reshape((b, n_blk * ATTN_BLOCK) + t.shape[3:])[:, :sub]
        return t1.reshape((b, s) + t1.shape[3:])

    return (from_blocks(num),
            from_blocks(den.transpose(0, 1, 4, 2, 3)),
            from_blocks(row_max.transpose(0, 1, 4, 2, 3)))

def _attention_mixer(q, k, v, q_norm_g, k_norm_g, cos, sin):
    b, s, _ = q.shape
    q = _rope(_rms_norm(q.reshape(b, s, N_ATTN_HEADS, HEAD_DIM), q_norm_g).astype(jnp.float32), cos, sin)
    k = _rope(_rms_norm(k.reshape(b, s, N_ATTN_HEADS, HEAD_DIM), k_norm_g).astype(jnp.float32), cos, sin)
    v = v.reshape(b, s, N_ATTN_HEADS, HEAD_DIM).astype(jnp.float32)
    branches = [_dilated_branch(q, k, v, w, d) for (w, d) in DILATED_PATTERNS]
    m_ref = branches[0][2]
    for br in branches[1:]:
        m_ref = jnp.maximum(m_ref, br[2])
    num = jnp.zeros_like(q)
    den = jnp.zeros_like(m_ref)
    for n_g, d_g, m_g in branches:
        wgt = jnp.exp(m_g - m_ref)
        num = num + wgt[..., None] * n_g
        den = den + wgt * d_g
    return (num / den[..., None]).reshape(b, s, ATTN_WIDTH)

def _moe(h, router_w, router_b, w_gate_up, b_gate_up, w_down, b_down):
    b, s, d = h.shape
    n_tok = b * s
    n_assign = n_tok * TOP_K
    n_blocks = -(-n_assign // MOE_BLOCK) + N_EXPERTS
    t = h.reshape(n_tok, d)
    logits = t.astype(jnp.float32) @ router_w.astype(jnp.float32) + router_b.astype(jnp.float32)
    top_val, top_idx = lax.top_k(logits, TOP_K)
    gates = jax.nn.softmax(top_val, axis=-1)
    flat_e = top_idx.reshape(-1).astype(jnp.int32)
    order = jnp.argsort(flat_e)
    e_sorted = flat_e[order]
    sizes = jnp.bincount(flat_e, length=N_EXPERTS).astype(jnp.int32)
    start = jnp.cumsum(sizes) - sizes
    pad_sizes = (sizes + MOE_BLOCK - 1) // MOE_BLOCK * MOE_BLOCK
    pad_end = jnp.cumsum(pad_sizes)
    pad_start = pad_end - pad_sizes
    dest_sorted = pad_start[e_sorted] + jnp.arange(n_assign, dtype=jnp.int32) - start[e_sorted]
    dest = jnp.zeros((n_assign,), jnp.int32).at[order].set(dest_sorted.astype(jnp.int32))
    row_tok = jnp.zeros((n_blocks * MOE_BLOCK,), jnp.int32).at[dest].set(
        jnp.arange(n_assign, dtype=jnp.int32) // TOP_K)
    block_e = jnp.minimum(jnp.searchsorted(pad_end, jnp.arange(n_blocks, dtype=jnp.int32) * MOE_BLOCK,
                                           side='right'), N_EXPERTS - 1)
    xb = t[row_tok].reshape(n_blocks, MOE_BLOCK, d)
    gu = jnp.einsum('nrd,ndf->nrf', xb, w_gate_up[block_e]) + b_gate_up[block_e][:, None, :]
    gate = jnp.minimum(gu[..., :EXPERT_FF], SWIGLU_LIMIT)
    up = jnp.clip(gu[..., EXPERT_FF:], -SWIGLU_LIMIT, SWIGLU_LIMIT)
    act = (up + 1.0) * gate * jax.nn.sigmoid(SWIGLU_ALPHA * gate)
    y = jnp.einsum('nrf,nfd->nrd', act, w_down[block_e]) + b_down[block_e][:, None, :]
    y_assign = y.reshape(n_blocks * MOE_BLOCK, d)[dest].reshape(n_tok, TOP_K, d)
    out = jnp.einsum('tkd,tk->td', y_assign, gates.astype(y.dtype))
    return out.reshape(b, s, d)

def setup_inputs(seed: int = 0) -> dict:
    key = jax.random.key(seed)
    ks = jax.random.split(key, 24)
    f32 = jnp.float32

    def nrm(k, shape, scale):
        return jax.random.normal(k, shape, f32) * scale

    lam_u = jax.random.uniform(ks[11], (DEPTH, LRU_WIDTH), f32, 0.9, 0.999)
    lam_s = lam_u ** (1.0 / LRU_C)
    return {
        'x': nrm(ks[0], (BATCH, SEQ, D_MODEL), 1.0),
        'norm1_g': 1.0 + nrm(ks[1], (DEPTH, D_MODEL), 0.02),
        'w_in': nrm(ks[2], (DEPTH, D_MODEL, IN_WIDTH), D_MODEL ** -0.5),
        'pool_w': nrm(ks[3], (DEPTH, POOL_GROUPS, POOL_GROUP_WIDTH, POOL_GROUP_WIDTH), POOL_GROUP_WIDTH ** -0.5),
        'pool_scale': 1.0 + nrm(ks[4], (DEPTH, POOL_WIDTH), 0.02),
        'conv_w': nrm(ks[5], (DEPTH, CONV_WIDTH, LRU_WIDTH), CONV_WIDTH ** -0.5),
        'conv_b': nrm(ks[6], (DEPTH, LRU_WIDTH), 0.01),
        'lru_wa': nrm(ks[7], (DEPTH, LRU_BLOCKS, LRU_BLOCK_WIDTH, LRU_BLOCK_WIDTH), LRU_BLOCK_WIDTH ** -0.5),
        'lru_ba': nrm(ks[8], (DEPTH, LRU_WIDTH), 0.01),
        'lru_wx': nrm(ks[9], (DEPTH, LRU_BLOCKS, LRU_BLOCK_WIDTH, LRU_BLOCK_WIDTH), LRU_BLOCK_WIDTH ** -0.5),
        'lru_bx': nrm(ks[10], (DEPTH, LRU_WIDTH), 0.01),
        'lru_lambda': jnp.log(lam_s) - jnp.log1p(-lam_s),
        'q_norm_g': 1.0 + nrm(ks[12], (DEPTH, HEAD_DIM), 0.02),
        'k_norm_g': 1.0 + nrm(ks[13], (DEPTH, HEAD_DIM), 0.02),
        'out_norm_g': 1.0 + nrm(ks[14], (DEPTH, D_MODEL), 0.02),
        'w_out': nrm(ks[15], (DEPTH, D_MODEL, D_MODEL), D_MODEL ** -0.5),
        'norm2_g': 1.0 + nrm(ks[16], (DEPTH, D_MODEL), 0.02),
        'router_w': nrm(ks[17], (DEPTH, D_MODEL, N_EXPERTS), D_MODEL ** -0.5),
        'router_b': nrm(ks[18], (DEPTH, N_EXPERTS), 0.01),
        'w_gate_up': nrm(ks[19], (DEPTH, N_EXPERTS, D_MODEL, 2 * EXPERT_FF), D_MODEL ** -0.5),
        'b_gate_up': nrm(ks[20], (DEPTH, N_EXPERTS, 2 * EXPERT_FF), 0.01),
        'w_down': nrm(ks[21], (DEPTH, N_EXPERTS, EXPERT_FF, D_MODEL), EXPERT_FF ** -0.5),
        'b_down': nrm(ks[22], (DEPTH, N_EXPERTS, D_MODEL), 0.01),
    }

def reference(x, norm1_g, w_in, pool_w, pool_scale, conv_w, conv_b, lru_wa, lru_ba, lru_wx, lru_bx,
              lru_lambda, q_norm_g, k_norm_g, out_norm_g, w_out, norm2_g, router_w, router_b,
              w_gate_up, b_gate_up, w_down, b_down):
    cos, sin = _rope_tables(x.shape[1])
    c0 = POOL_WIDTH
    c1 = c0 + LRU_WIDTH
    c2 = c1 + LRU_WIDTH
    c3 = c2 + ATTN_WIDTH
    c4 = c3 + ATTN_WIDTH
    a_end = POOL_WIDTH
    b_end = POOL_WIDTH + LRU_WIDTH
    for l in range(DEPTH):
        h = _rms_norm(x, norm1_g[l])
        proj = h @ w_in[l]
        y_pool = _pool_mixer(proj[..., :c0], pool_w[l], pool_scale[l])
        y_lru = _rglru_mixer(proj[..., c0:c1], proj[..., c1:c2], conv_w[l], conv_b[l],
                             lru_wa[l], lru_ba[l], lru_wx[l], lru_bx[l], lru_lambda[l])
        y_attn = _attention_mixer(proj[..., c2:c3], proj[..., c3:c4], proj[..., c4:],
                                  q_norm_g[l], k_norm_g[l], cos, sin)
        og = out_norm_g[l]
        mix = jnp.concatenate([_rms_norm(y_pool, og[:a_end]),
                               _rms_norm(y_lru, og[a_end:b_end]),
                               _rms_norm(y_attn, og[b_end:])], axis=-1).astype(x.dtype)
        x = x + mix @ w_out[l]
        x = x + _moe(_rms_norm(x, norm2_g[l]), router_w[l], router_b[l],
                     w_gate_up[l], b_gate_up[l], w_down[l], b_down[l])
    return x


_drawn_inputs = setup_inputs


def setup_inputs(seed=0):
    import zlib

    import numpy as np

    out = dict(_drawn_inputs(seed))
    spreads = {}
    factors = {'lru_ba': 8.0, 'lru_bx': 3.607, 'b_gate_up': 7.089, 'b_down': 4.698}
    for name, (base, spread) in spreads.items():
        noise = np.random.default_rng([zlib.crc32(name.encode()), seed]).standard_normal(out[name].shape)
        drawn = base * np.exp(spread * noise) if base else spread * noise
        out[name] = jnp.asarray(drawn.astype(out[name].dtype))
    for name, factor in factors.items():
        out[name] = (out[name] * factor).astype(out[name].dtype)
    return out
```

```python
from contextlib import ExitStack

import concourse.bass as bass
from concourse import mybir

P = 128
F32 = mybir.dt.float32
U32 = mybir.dt.uint32
ALU = mybir.AluOpType
ACT = mybir.ActivationFunctionType
AX = mybir.AxisListType

DEPTH, SEQ, D = 2, 256, 1024
TT = SEQ // P
KD = D // P
IN_W = 2304
HEADS, DH = 8, 64
ATT = HEADS * DH
E, FF, TOPK = 32, 256, 4
CONV = 4
PAD = 16
KEYS = P + 2 * P
EPS = 1e-6
LIMIT, ALPHA = 7.0, 1.702
GU = KD * 2 * FF
DN = (FF // P) * D
SLOT = GU + DN
RING = 4
G1, OG, PS, CW, CB, BA, BX, LAM, BD, QG, KG = 0, 8, 16, 18, 26, 28, 30, 32, 34, 802, 866
NA = 930
G2, RW, BGU, RB = 0, 8, 264, 392
NB = 393
ATANH_TERMS = 9


class Counter:

    def __init__(self, sem, per, base=0):
        self.sem, self.per, self.base = sem, per, base

    def at(self, layer, k):
        return self.sem, layer * self.per + k + self.base


def build(nc, x_in, small_a, small_b, w_in, w_out, experts, b_down, consts, out):
    with ExitStack() as ctx:
        def sb(name, *shape, dt=F32):
            return ctx.enter_context(nc.sbuf_tensor(name, [P, *shape], dt))

        def counter(name, per, base=0):
            return Counter(ctx.enter_context(nc.semaphore(name)), per, base)

        bank = [ctx.enter_context(nc.psum_tensor(f"bank{i}", [P, 512], F32)) for i in range(8)]

        x = sb("x", TT, D)
        ring = sb("ring", RING, SLOT)
        wout = sb("wout", KD, D)
        cst = sb("cst", consts.shape[1])
        pa = sb("pa", NA)
        pb = sb("pb", NB)
        xn = sb("xn", TT, D)
        ysq = xn[:, :, :].rearrange("p t d -> p (t d)").rearrange("p (k s) -> p k s", k=KD)
        hT = sb("hT", KD, SEQ)
        yT = hT
        ms = sb("ms", 8)
        rstd = sb("rstd", 8)
        vt = sb("vt", TT, ATT)
        tmp = sb("tmp", ATT)
        rot = sb("rot", 2, TT, ATT)
        cg = sb("cg", 2, 2, TT, DH)
        hs = sb("hs", 4, 16)
        qkT = sb("qkT", 2, 4, SEQ)
        probs = sb("probs", 4, KEYS)
        prob, probT = probs[:, 0:2, :], probs[:, 2:4, :]
        before = probs[:, :, :].rearrange("p a b -> p (a b)")
        sq, swp = before[:, 0:ATT], before[:, ATT:2 * ATT]
        nmax = sb("nmax", 16)
        den = sb("den", 16)
        rden = sb("rden", 16)
        gstat = sb("gstat", 8)
        grs = sb("grs", 8)
        up = sb("up", 2, CONV - 1 + SEQ)
        gt = sb("gt", 2, SEQ)
        gl = sb("gl", 2, SEQ)
        hb = sb("hb", 4)
        sp = sb("sp", 12, 2)
        pp = sb("pp", 2, PAD + SEQ)
        ps = sb("ps", 2, 2, PAD + SEQ)
        p2, p4 = ps[:, 0], ps[:, 1]
        pooled = cg[:, :, :, :, :].rearrange("p a b t d -> p (a b t d)").rearrange("p (c s) -> p c s", c=2)

        def two(ap):
            return ap.rearrange("p (c s) -> p c s", c=2)
        th_r, th_i, la, tn = (two(rot[:, n, t, :]) for n in range(2) for t in range(TT))
        ea = th_r
        xc = two(tmp[:, :])
        rec = two(sq[:, :])
        pflat = ps[:, :, :, :].rearrange("p a b c -> p (a b c)")
        lgT = pflat[:, 0:SEQ]
        gT = pflat[:, SEQ:2 * SEQ]
        hot = pflat[:, 2 * SEQ:2 * SEQ + TT * TOPK * E].rearrange("p (t k e) -> p t k e", t=TT, k=TOPK)
        bdn = probs[:, :, :].rearrange("p a b -> p (a b)")[:, 0:D]
        lg = sb("lg", TT, E)
        top = sb("top", TT, 8)
        tix = sb("tix", TT, 8, dt=U32)
        tif = sb("tif", TT, 8)
        ntop = sb("ntop", TT)
        ptop = sb("ptop", TT, TOPK)
        psum4 = sb("psum4", TT)
        rp4 = sb("rp4", TT)
        gates = sb("gates", TT, E)

        def by_parity(ap):
            return ap.rearrange("p c s -> p (c s)").rearrange("p (q f s) -> p q f s", q=2, f=2)
        g, u = by_parity(qkT[:, 0, :, :]), by_parity(qkT[:, 1, :, :])
        th, act_t = by_parity(rot[:, 0, :, :]), by_parity(rot[:, 1, :, :])

        ident = cst[:, 0:128]
        cos_t = cst[:, 128:256].rearrange("p (t d) -> p t d", t=TT)
        sin_t = cst[:, 256:384].rearrange("p (t d) -> p t d", t=TT)
        mask = cst[:, 384:768]
        invc = cst[:, 768:1280].rearrange("p (t s) -> p t s", t=2)
        iota_e = cst[:, 1280:1312]
        half = cst[:, 1312:1328]
        ones = cst[:, 1328:1329]
        win = ring[:, 0:3, :].rearrange("p r c -> p (r c)").rearrange("p (k c) -> p k c", k=KD)

        passed = counter("waits_passed", 0)
        once, zeroed = counter("once_landed", 0), counter("pads_zeroed", 0)
        pa_in, pb_in = counter("params_a_landed", 16), counter("params_b_landed", 16)
        bdn_in = counter("b_down_landed", 16)
        win_in = [counter(f"w_in_{n}_landed", 16) for n in range(4)]
        wout_in = counter("w_out_landed", 16)
        slot_in = [counter(f"expert_slot{j}_landed", 16 * (E // RING)) for j in range(RING)]
        ms_ok = counter("squares_summed", 4)
        rstd_ok = counter("rstd_ready", 4)
        rstd_mid = counter("rstd_half", 4)
        xn_ok = counter("tokens_normalised", 4)
        tr_ok = counter("h_transposed", 8)
        hT_act, hT_dve = counter("hT_by_act", 8), counter("hT_by_dve", 8)
        proj_ok = counter("projected", 9)
        proj_free = counter("projection_copied", 5)
        sq_ok = counter("qk_squared", 4)
        hsum_ok = counter("qk_head_sums", 4)
        hr_mid, hr_ok = counter("qk_rstd_half", 4), counter("qk_rstd_ready", 4)
        rope = counter("rope_steps", 24)
        qkT_ps, qkT_ok = counter("qk_transposed", 4), counter("qkT_ready", 4)
        sp_dve, sp_act = counter("softplus_steps", 19), counter("softplus_exp", 1)
        conv_ok = counter("conv_steps", 8)
        lru_ps = counter("lru_gates_product", 2)
        lru_a = counter("lru_activations", 7)
        lru_d = counter("lru_steps", 14)
        gelu_p, gelu_a = counter("gelu_steps", 5), counter("gelu_tanh", 1)
        pool_p, pool_ps, pool_ok = counter("pool_steps", 9), counter("pool_product", 1), counter("pool_out", 2)
        ysq_pl, ysq_at = counter("y_squares", 4), counter("attention_squares", 4)
        st_ps, st_ok = counter("group_sums", 2), counter("group_sums_copied", 2)
        gr_mid, gr_ok = counter("group_rstd_half", 2), counter("group_rstd_ready", 2)
        s_ps, s_ok, e_ok = counter("scores", 8), counter("scores_masked", 16), counter("exp_done", 16)
        rd_ok, pn_ok = counter("den_reciprocal", 8), counter("probs_normalised", 8)
        pt_ps, pt_ok = counter("probs_transposed", 8), counter("probsT_copied", 8)
        o_ps, o_ok = counter("attention_out", 4), counter("attention_yT", 4)
        wo_ps, wo_ok = counter("w_out_product", 12), counter("w_out_added", 12)
        lgT_ps, lgT_ok = counter("logitsT", 1), counter("logitsT_copied", 1)
        lg_ps, rt = counter("logits", 1), counter("router_steps", 40)
        rt_act = counter("router_exp", 2)
        gT_ps, gT_ok = counter("gates_transposed", 1), counter("gatesT_copied", 1)
        gu_ps = counter("gate_up_product", E)
        gu_rd = counter("gate_up_read", E, base=1)
        sg_ok, am_ok, act_ok = counter("tanh_done", E), counter("swiglu_half", E), counter("swiglu_done", E, base=1)
        gclip = counter("gate_up_clipped", 2 * E)
        y_ps, y_ok = counter("down_product", 2 * (E + 1), base=1), counter("down_added", 4 * (E + 1), base=1)
        stored = counter("out_stored", 0)

        def alone(eng, sem, value):
            eng.wait_ge(sem, value)
            eng.sem_inc(passed.sem, 1)

        block = ctx.enter_context(nc.Block())
        WIN_COLS = [(768, 1280), (1280, 1792), (0, 768), (1792, 2304)]

        @block.sync
        def _(sp_):
            sp_.dma_start(x[:, :, :], x_in).then_inc(once.sem, 16)
            sp_.dma_start(cst[:, :], consts).then_inc(once.sem, 16)
            with sp_.Fori(0, DEPTH) as l:
                sp_.wait_ge(*y_ps.at(l, 0))
                sp_.dma_start(pa[:, :], small_a[bass.ds(l, 1)].rearrange("o p c -> (o p) c")).then_inc(pa_in.sem, 16)
                for n, (a, b) in enumerate(WIN_COLS):
                    sp_.dma_start(win[:, :, a:b], w_in[bass.ds(l, 1), :, :, a:b].rearrange("o p k c -> (o p) k c")
                                  ).then_inc(win_in[n].sem, 16)
                sp_.wait_ge(*y_ok.at(l, 0))
                sp_.dma_start(pb[:, :], small_b[bass.ds(l, 1)].rearrange("o p c -> (o p) c")).then_inc(pb_in.sem, 16)
                sp_.dma_start(wout[:, :, :], w_out[bass.ds(l, 1)].rearrange("o p k c -> (o p) k c")
                              ).then_inc(wout_in.sem, 16)
                for j in (3, 0, 1, 2):
                    if j == 0:
                        sp_.wait_ge(*proj_ok.at(l, 9))
                    sp_.dma_start(ring[:, j, :], experts[bass.ds(l * E + j, 1)].rearrange("o p c -> (o p) c")
                                  ).then_inc(slot_in[j].sem, 16)
                sp_.wait_ge(*o_ps.at(l, 4))
                sp_.dma_start(bdn[0:E, :], b_down[bass.ds(l, 1)].rearrange("o e d -> (o e) d")).then_inc(bdn_in.sem, 16)
                with sp_.Fori(1, E // RING) as i:
                    for j in range(RING):
                        sp_.wait_ge(*y_ps.at(l, 2 * (RING * i + j - RING + 2)))
                        sp_.dma_start(ring[:, j, :], experts[bass.ds(l * E + RING * i + j, 1)].rearrange("o p c -> (o p) c")
                                      ).then_inc(slot_in[j].sem, 16)
            sp_.wait_ge(*y_ok.at(DEPTH, 0))
            sp_.dma_start(out, x[:, :, :]).then_inc(stored.sem, 16)
            sp_.wait_ge(stored.sem, 16)

        @block.tensor
        def _(pe):
            pe.sem_inc(y_ps.sem, 1)
            pe.wait_ge(once.sem, 32)
            with pe.Fori(0, DEPTH) as l:
                def transpose_tokens(c):
                    pe.wait_ge(*xn_ok.at(l, 2 * c + 2))
                    for b in range(4):
                        for dt in range(2):
                            for t in range(TT):
                                k = 2 * b + dt
                                mm = pe.transpose(bank[b][:, dt * SEQ + t * P:dt * SEQ + t * P + P],
                                                  xn[:, t, k * P:k * P + P], ident)
                        mm.then_inc(tr_ok.sem, 1)

                pe.wait_ge(*gu_rd.at(l, 0))
                transpose_tokens(0)

                pe.wait_ge(*y_ok.at(l, 0))
                pe.wait_ge(*hT_act.at(l, 4))
                pe.wait_ge(*hT_dve.at(l, 4))
                for n in range(2):
                    pe.wait_ge(*win_in[n].at(l, 16))
                    for t in range(TT):
                        for k in range(KD):
                            mm = pe.matmul(bank[4 + 2 * n + t][:, :], hT[:, k, t * P:t * P + P],
                                           win[:, k, 768 + 512 * n:1280 + 512 * n], start=(k == 0), stop=(k == KD - 1))
                        mm.then_inc(proj_ok.sem, 1)
                pe.wait_ge(*win_in[2].at(l, 16))
                for b, c0 in enumerate((256, 512, 0)):
                    for c in range(2):
                        for k in range(KD):
                            mm = pe.matmul(bank[b][:, c * SEQ:c * SEQ + SEQ], win[:, k, c0 + c * P:c0 + c * P + P],
                                           hT[:, k, :], start=(k == 0), stop=(k == KD - 1))
                    mm.then_inc(proj_ok.sem, 1)
                for n in range(2):
                    for t in range(TT):
                        pe.wait_ge(*rope.at(l, 6 * (2 * n + t + 1)))
                        for c in range(4):
                            mm = pe.transpose(bank[4 + 2 * n + t][:, c * P:c * P + P], rot[:, n, t, c * P:c * P + P], ident)
                        mm.then_inc(qkT_ps.sem, 1)
                pe.wait_ge(*win_in[3].at(l, 16))

                def project_v(t):
                    for k in range(KD):
                        mm = pe.matmul(bank[3][:, :], hT[:, k, t * P:t * P + P], win[:, k, 1792:2304],
                                       start=(k == 0), stop=(k == KD - 1))
                    mm.then_inc(proj_ok.sem, 1)
                project_v(0)
                pe.wait_ge(*conv_ok.at(l, 8))
                pe.wait_ge(*proj_free.at(l, 2))
                for b in range(2):
                    for c in range(2):
                        w = pa[:, BD + (2 * b + c) * P:BD + (2 * b + c + 1) * P]
                        mm = pe.matmul(bank[b][:, c * SEQ:c * SEQ + SEQ], w, xc[:, c, :], start=True, stop=True)
                    mm.then_inc(lru_ps.sem, 1)
                pe.wait_ge(*proj_free.at(l, 4))
                project_v(1)
                pe.wait_ge(*pool_p.at(l, 9))
                pe.wait_ge(*proj_free.at(l, 3))
                for c in range(2):
                    mm = pe.matmul(bank[2][:, c * SEQ:c * SEQ + SEQ], pa[:, BD + (4 + c) * P:BD + (5 + c) * P],
                                   pooled[:, c, :], start=True, stop=True)
                mm.then_inc(pool_ps.sem, 1)

                def scores(h):
                    if h == 0:
                        pe.wait_ge(*qkT_ok.at(l, 4))
                    if h >= 2:
                        pe.wait_ge(*s_ok.at(l, 2 * h - 2))
                    s, r = bank[4 + h % 2], slice(DH * (h % 2), DH * (h % 2) + DH)
                    pe.matmul(s[:, 0:P], qkT[r, 0, h // 2, 0:P], qkT[r, 1, h // 2, 0:P], start=True, stop=True)
                    pe.matmul(s[:, P:KEYS], qkT[r, 0, h // 2, P:SEQ], qkT[r, 1, h // 2, :], start=True,
                              stop=True).then_inc(s_ps.sem, 1)

                def turn_probs(h):
                    pe.wait_ge(*pn_ok.at(l, h + 1))
                    if h == 0:
                        pe.wait_ge(*qkT_ok.at(l, 4))
                    if h >= 2:
                        pe.wait_ge(*pt_ok.at(l, h - 1))
                    for c in range(3):
                        mm = pe.transpose(bank[6 + h % 2][:, c * P:c * P + P], prob[:, h % 2, c * P:c * P + P], ident)
                    mm.then_inc(pt_ps.sem, 1)

                def values(h):
                    pr = h // 2
                    pe.wait_ge(*pt_ok.at(l, h + 1))
                    if h == 0:
                        pe.wait_ge(*proj_free.at(l, 5))
                        pe.wait_ge(*st_ok.at(l, 1))
                    if h == 2:
                        pe.wait_ge(*lru_a.at(l, 4))
                    if h >= 4 and h % 2 == 0:
                        pe.wait_ge(*o_ok.at(l, pr - 1))
                    o = bank[pr % 2][DH * (h % 2):DH * (h % 2) + DH, :]
                    pe.matmul(o[:, 0:SEQ], vt[:, 0, h * DH:h * DH + DH], probT[:, h % 2, 0:SEQ],
                              start=True, stop=False)
                    mm = pe.matmul(o[:, P:SEQ], vt[:, 1, h * DH:h * DH + DH], probT[:, h % 2, SEQ:KEYS],
                                   start=False, stop=True)
                    if h % 2:
                        mm.then_inc(o_ps.sem, 1)

                def group_sums(b, groups):
                    for n, (k0, k1) in enumerate(groups):
                        for t in range(TT):
                            c = SEQ + 2 * n + t
                            for k in range(k0, k1):
                                mm = pe.matmul(bank[b][:, c:c + 1], ysq[:, k, t * P:t * P + P], ones,
                                               start=(k == k0), stop=(k == k1 - 1))
                    mm.then_inc(st_ps.sem, 1)

                def out_unit(n, k0, k1):
                    t, c = (n // 2) % 2, n % 2
                    if n == 0:
                        pe.wait_ge(*wout_in.at(l, 16))
                        pe.wait_ge(*pool_ok.at(l, 2))
                    if n == 1:
                        pe.wait_ge(*proj_free.at(l, 5))
                    if n >= 2:
                        pe.wait_ge(*wo_ok.at(l, n - 1))
                    for k in range(k0, k1):
                        mm = pe.matmul(bank[2 + n % 2][:, :], yT[:, k, t * P:t * P + P], wout[:, k, c * 512:c * 512 + 512],
                                       start=(k == k0), stop=(k == k1 - 1))
                    mm.then_inc(wo_ps.sem, 1)

                for h in range(HEADS + 2):
                    if h < HEADS:
                        scores(h)
                    if h == 1:
                        pe.wait_ge(*ysq_pl.at(l, 4))
                        pe.wait_ge(*lru_a.at(l, 2))
                        group_sums(0, ((0, 2), (2, 4)))
                    if 1 <= h < HEADS + 1:
                        turn_probs(h - 1)
                    if h >= 2:
                        values(h - 2)
                        if h - 2 < 4:
                            out_unit(h - 2, 0, 2)
                        else:
                            if h - 2 == 4:
                                pe.wait_ge(*lru_d.at(l, 14))
                            out_unit(h - 2, 2, 4)
                pe.wait_ge(*ysq_at.at(l, 4))
                pe.wait_ge(*o_ok.at(l, 4))
                group_sums(0, ((4, 8),))
                for n in range(8, 12):
                    out_unit(n, 4, 8)

                pe.wait_ge(*st_ok.at(l, 2))
                pe.wait_ge(*wo_ok.at(l, 12))
                transpose_tokens(1)
                pe.wait_ge(*pb_in.at(l, 16))
                pe.wait_ge(*hT_act.at(l, 8))
                pe.wait_ge(*hT_dve.at(l, 8))
                for k in range(KD):
                    mm = pe.matmul(bank[4][0:E, 0:SEQ], pb[:, RW + k * E:RW + k * E + E], hT[:, k, :],
                                   start=(k == 0), stop=(k == KD - 1))
                mm.then_inc(lgT_ps.sem, 1)

                def gate_up(e, j, parity, first):
                    if first:
                        pe.wait_ge(*slot_in[j].at(l, 16))
                    else:
                        pe.wait_ge(*slot_in[j].at(l, (e - j) * (16 // RING) + 16))
                        pe.wait_ge(*gu_rd.at(l, e - 1))
                    for c in range(4):
                        for k in range(KD):
                            mm = pe.matmul(bank[2 * parity + c // 2][:, (c % 2) * SEQ:(c % 2) * SEQ + SEQ],
                                           ring[:, j, k * 2 * FF + c * P:k * 2 * FF + c * P + P], hT[:, k, :],
                                           start=(k == 0), stop=(k == KD - 1))
                    mm.then_inc(gu_ps.sem, 1)

                def down(e, j):
                    pe.wait_ge(*act_ok.at(l, e + 1))
                    for t in range(TT):
                        for c in range(2):
                            pe.wait_ge(*y_ok.at(l, 4 * e + 2 * t + c + 1))
                            for k in range(2):
                                mm = pe.matmul(bank[4 + 2 * t + c][:, :], act_t[:, j % 2, k, t * P:t * P + P],
                                               ring[:, j, GU + k * D + c * 512:GU + k * D + c * 512 + 512],
                                               start=(k == 0), stop=(k == 1))
                        mm.then_inc(y_ps.sem, 1)

                pe.wait_ge(*tr_ok.at(l, 8))
                gate_up(0, 0, 0, True)
                alone(pe, *lgT_ok.at(l, 1))
                for t in range(TT):
                    mm = pe.transpose(bank[5][:, t * E:t * E + E], lgT[0:E, t * P:t * P + P], ident[0:E, 0:E])
                mm.then_inc(lg_ps.sem, 1)
                gate_up(1, 1, 1, True)
                alone(pe, *rt.at(l, 40))
                for t in range(TT):
                    mm = pe.transpose(bank[6][0:E, t * P:t * P + P], gates[:, t, :], ident)
                mm.then_inc(gT_ps.sem, 1)
                pe.wait_ge(*gT_ok.at(l, 1))
                pe.wait_ge(*bdn_in.at(l, 16))
                for t in range(TT):
                    for c in range(2):
                        mm = pe.matmul(bank[4 + 2 * t + c][:, :], gT[0:E, t * P:t * P + P], bdn[0:E, c * 512:c * 512 + 512],
                                       start=True, stop=True)
                    mm.then_inc(y_ps.sem, 1)
                down(0, 0)
                gate_up(2, 2, 0, False)
                down(1, 1)
                gate_up(3, 3, 1, False)
                with pe.Fori(0, E // RING - 1) as i:
                    for j in range(RING):
                        down(RING * i + 2 + j, (2 + j) % RING)
                        gate_up(RING * i + RING + j, j, j % 2, False)
                for e in (E - 2, E - 1):
                    down(e, e % RING)

        @block.vector
        def _(dve):
            for c in (gu_rd, act_ok, y_ok):
                dve.sem_inc(c.sem, 1)
            dve.memset(up[:, :, 0:CONV - 1], 0.0)
            dve.memset(pp[:, :, 0:PAD], 0.0).then_inc(zeroed.sem, 1)
            dve.wait_ge(once.sem, 32)
            dve.wait_ge(zeroed.sem, 1)
            with dve.Fori(0, DEPTH) as l:
                def normalise(c):
                    for t in range(TT):
                        dve.wait_ge(*rstd_ok.at(l, 2 * c + t + 1))
                        dve.tensor_scalar(xn[:, t, :], x[:, t, :], rstd[:, 2 * c + t:2 * c + t + 1], None, ALU.mult
                                          ).then_inc(xn_ok.sem, 1)

                def turned(c, gain):
                    for b in (1, 3):
                        dve.wait_ge(*tr_ok.at(l, 4 * c + b + 1))
                        for dt in range(2):
                            k = 2 * b + dt
                            dve.tensor_scalar(hT[:, k, :], bank[b][:, dt * SEQ:dt * SEQ + SEQ], gain[:, k:k + 1], None,
                                              ALU.mult).then_inc(hT_dve.sem, 1)

                normalise(0)
                dve.wait_ge(*pa_in.at(l, 16))
                turned(0, pa[:, G1:G1 + KD])

                steps = [0]

                def tiny(ins):
                    ins.then_inc(sp_dve.sem, 1)
                    steps[0] += 1
                    dve.wait_ge(*sp_dve.at(l, steps[0]))
                lam = pa[:, LAM:LAM + 2]
                tiny(dve.tensor_scalar(sp[:, 0, :], lam, -1.0, None, ALU.mult))
                tiny(dve.tensor_tensor(sp[:, 1, :], lam, sp[:, 0, :], ALU.max))
                tiny(dve.tensor_scalar(hb[:, :], pa[:, BA:BA + 4], 0.5, None, ALU.mult))
                dve.wait_ge(*sp_act.at(l, 1))
                tiny(dve.tensor_scalar(sp[:, 3, :], sp[:, 2, :], 2.0, None, ALU.add))
                tiny(dve.reciprocal(sp[:, 4, :], sp[:, 3, :]))
                tiny(dve.tensor_tensor(sp[:, 5, :], sp[:, 2, :], sp[:, 4, :], ALU.mult))
                tiny(dve.tensor_tensor(sp[:, 6, :], sp[:, 5, :], sp[:, 5, :], ALU.mult))
                tiny(dve.tensor_scalar(sp[:, 7, :], sp[:, 6, :], 1.0 / (2 * ATANH_TERMS - 1), None, ALU.mult))
                for k in range(ATANH_TERMS - 2, 0, -1):
                    tiny(dve.scalar_tensor_tensor(sp[:, 7, :], sp[:, 7, :], 1.0 / (2 * k + 1), sp[:, 6, :], ALU.add, ALU.mult))
                tiny(dve.scalar_tensor_tensor(sp[:, 8, :], sp[:, 7, :], 1.0, sp[:, 5, :], ALU.add, ALU.mult))
                tiny(dve.tensor_scalar(sp[:, 9, :], sp[:, 0, :], 0.0, -4.0, ALU.max, ALU.mult))
                tiny(dve.scalar_tensor_tensor(sp[:, 10, :], sp[:, 8, :], -8.0, sp[:, 9, :], ALU.mult, ALU.add))
                for n, (g0, scale) in enumerate(((QG, DH ** -0.5), (KG, 1.0))):
                    gain = pa[:, g0:g0 + DH].unsqueeze(1).broadcast_to([P, TT, DH])
                    dve.scalar_tensor_tensor(cg[:, n, 0, :, :], cos_t, scale, gain, ALU.mult, ALU.mult)
                    for a, b in ((0, 32), (32, 0)):
                        gs = pa[:, g0 + b:g0 + b + 32].unsqueeze(1).broadcast_to([P, TT, 32])
                        ins = dve.scalar_tensor_tensor(cg[:, n, 1, :, a:a + 32], sin_t[:, :, a:a + 32], scale, gs,
                                                       ALU.mult, ALU.mult)
                tiny(ins)
                assert steps[0] == 19

                def rope_unit(n, t):
                    w = 2 * n + t
                    b3 = bank[4 + w][:, :].rearrange("p (h d) -> p h d", h=HEADS)
                    dve.wait_ge(*sq_ok.at(l, w + 1))
                    dve.tensor_reduce(hs[:, w, 0:8], sq[:, :].rearrange("p (h d) -> p h d", h=HEADS), AX.X, ALU.add
                                      ).then_inc(hsum_ok.sem, 1)
                    dve.wait_ge(*hr_ok.at(l, w + 1))
                    r0 = 6 * w
                    t3 = tmp[:, :].rearrange("p (h d) -> p h d", h=HEADS)
                    s3 = swp[:, :].rearrange("p (h d) -> p h d", h=HEADS)
                    o3 = rot[:, n, t, :].rearrange("p (h d) -> p h d", h=HEADS)
                    dve.tensor_tensor(t3, b3, hs[:, w, 8:16].unsqueeze(2).broadcast_to([P, HEADS, DH]), ALU.mult
                                      ).then_inc(rope.sem, 1)
                    dve.wait_ge(*rope.at(l, r0 + 1))
                    cgc = cg[:, n, 0, t, :].unsqueeze(1).broadcast_to([P, HEADS, DH])
                    dve.tensor_tensor(o3, t3, cgc, ALU.mult).then_inc(rope.sem, 1)
                    for a, b in ((0, 32), (32, 0)):
                        cgs = cg[:, n, 1, t, a:a + 32].unsqueeze(1).broadcast_to([P, HEADS, 32])
                        dve.tensor_tensor(s3[:, :, a:a + 32], t3[:, :, b:b + 32], cgs, ALU.mult).then_inc(rope.sem, 1)
                    dve.wait_ge(*rope.at(l, r0 + 4))
                    dve.tensor_tensor(o3, o3, s3, ALU.add).then_inc(rope.sem, 2)

                for n in range(2):
                    for t in range(TT):
                        rope_unit(n, t)

                dve.wait_ge(*proj_free.at(l, 1))
                for c in range(2):
                    w = [pa[:, CW + 2 * j + c:CW + 2 * j + c + 1] for j in range(CONV)]
                    dve.tensor_scalar(xc[:, c, :], up[:, c, 0:SEQ], w[0], pa[:, CB + c:CB + c + 1], ALU.mult, ALU.add
                                      ).then_inc(conv_ok.sem, 1)
                for j in range(1, CONV):
                    for c in range(2):
                        dve.wait_ge(*conv_ok.at(l, 2 * j + c - 1))
                        dve.scalar_tensor_tensor(xc[:, c, :], up[:, c, j:j + SEQ], pa[:, CW + 2 * j + c:CW + 2 * j + c + 1],
                                                 xc[:, c, :], ALU.mult, ALU.add).then_inc(conv_ok.sem, 1)
                for w in (1, 3):
                    dve.wait_ge(*qkT_ps.at(l, w + 1))
                    dve.tensor_copy(qkT[:, w // 2, :, P:SEQ], bank[4 + w][:, :].rearrange("p (c s) -> p c s", c=4)
                                    ).then_inc(qkT_ok.sem, 1)

                dve.wait_ge(*lru_a.at(l, 2))
                for c in range(2):
                    dve.tensor_scalar(la[:, c, :], th_r[:, c, :], sp[:, 10, c:c + 1], sp[:, 10, c:c + 1], ALU.mult, ALU.add
                                      ).then_inc(lru_d.sem, 1)
                dve.wait_ge(*lru_a.at(l, 6))
                dve.tensor_scalar(rec[:, :, :], tn[:, :, :], 1.0, None, ALU.add).then_inc(lru_d.sem, 1)
                dve.wait_ge(*lru_d.at(l, 3))
                dve.reciprocal(rec[:, :, :], rec[:, :, :]).then_inc(lru_d.sem, 1)
                dve.scalar_tensor_tensor(th_i[:, :, :], th_i[:, :, :], 1.0, xc[:, :, :], ALU.add, ALU.mult
                                         ).then_inc(lru_d.sem, 1)
                dve.wait_ge(*lru_d.at(l, 4))
                dve.scalar_tensor_tensor(tn[:, :, :], tn[:, :, :], 2.0, rec[:, :, :], ALU.mult, ALU.mult
                                         ).then_inc(lru_d.sem, 1)
                dve.wait_ge(*pool_ps.at(l, 1))
                for c in range(2):
                    dve.tensor_scalar(pooled[:, c, :], bank[2][:, c * SEQ:c * SEQ + SEQ], pa[:, PS + c:PS + c + 1], None,
                                      ALU.mult).then_inc(pool_ok.sem, 1)
                dve.wait_ge(*pool_ok.at(l, 2))
                for c in range(2):
                    dve.tensor_scalar(yT[:, c, :], pooled[:, c, :], pa[:, OG + c:OG + c + 1], None, ALU.mult
                                      ).then_inc(lru_d.sem, 1)
                dve.wait_ge(*lru_a.at(l, 7))
                dve.memset(tn[:, :, 0:1], 1.0).then_inc(lru_d.sem, 1)
                dve.wait_ge(*lru_d.at(l, 9))
                dve.scalar_tensor_tensor(th_i[:, :, :], th_i[:, :, :], 0.5, tn[:, :, :], ALU.mult, ALU.mult
                                         ).then_inc(lru_d.sem, 1)
                dve.wait_ge(*lru_d.at(l, 10))
                for c in range(2):
                    ins = dve.tensor_tensor_scan(la[:, c, :], ea[:, c, :], th_i[:, c, :], 0.0, ALU.mult, ALU.add)
                ins.then_inc(lru_d.sem, 1)
                dve.wait_ge(*lru_d.at(l, 11))
                dve.wait_ge(*gelu_p.at(l, 5))
                dve.tensor_tensor(xc[:, :, :], la[:, :, :], gl[:, :, :], ALU.mult).then_inc(lru_d.sem, 1)
                dve.wait_ge(*lru_d.at(l, 12))
                for c in range(2):
                    dve.tensor_scalar(yT[:, 2 + c, :], xc[:, c, :], pa[:, OG + 2 + c:OG + 3 + c], None, ALU.mult
                                      ).then_inc(lru_d.sem, 1)

                def masked(h):
                    for t, (a, b) in enumerate(((0, P), (P, KEYS))):
                        if h >= 2 and t == 0:
                            dve.wait_ge(*pt_ps.at(l, h - 1))
                        if t == 0:
                            alone(dve, *s_ps.at(l, h + 1))
                        dve.tensor_tensor_reduce(prob[:, h % 2, a:b], bank[4 + h % 2][:, a:b], mask[:, a:b], -1.0, 3e38,
                                                 ALU.add, ALU.min, nmax[:, 2 * h + t:2 * h + t + 1]).then_inc(s_ok.sem, 1)

                def normalised(h):
                    dve.wait_ge(*e_ok.at(l, 2 * h + 2))
                    dve.reciprocal(rden[:, 2 * h:2 * h + 2], den[:, 2 * h:2 * h + 2]).then_inc(rd_ok.sem, 1)
                    dve.wait_ge(*rd_ok.at(l, h + 1))
                    for t, (a, b) in enumerate(((0, P), (P, KEYS))):
                        ins = dve.tensor_scalar(prob[:, h % 2, a:b], prob[:, h % 2, a:b], rden[:, 2 * h + t:2 * h + t + 1],
                                                None, ALU.mult)
                    ins.then_inc(pn_ok.sem, 1)

                def attention_y(pr):
                    dve.wait_ge(*ysq_at.at(l, pr + 1))
                    dve.tensor_scalar(yT[:, 4 + pr, :], bank[pr % 2][:, 0:SEQ], pa[:, OG + 4 + pr:OG + 5 + pr], None,
                                      ALU.mult).then_inc(o_ok.sem, 1)

                def added(n, grp):
                    t, c = (n // 2) % 2, n % 2
                    dve.wait_ge(*wo_ps.at(l, n + 1))
                    if n >= 4:
                        dve.wait_ge(*wo_ok.at(l, n - 3))
                    xs = x[:, t, c * 512:c * 512 + 512]
                    dve.scalar_tensor_tensor(xs, bank[2 + n % 2][:, :], grs[:, 2 * grp + t:2 * grp + t + 1], xs,
                                             ALU.mult, ALU.add).then_inc(wo_ok.sem, 1)

                for h in range(HEADS + 2):
                    if h < HEADS:
                        masked(h)
                    if h == 1:
                        dve.wait_ge(*st_ps.at(l, 1))
                        dve.tensor_copy(gstat[:, 0:4], bank[0][:, SEQ:SEQ + 4]).then_inc(st_ok.sem, 1)
                    if 1 <= h < HEADS + 1:
                        normalised(h - 1)
                    if h >= 3 and h % 2:
                        attention_y((h - 3) // 2)
                    if h == 2:
                        dve.wait_ge(*gr_ok.at(l, 1))
                    if h >= 2:
                        added(h - 2, 0 if h - 2 < 4 else 1)
                dve.wait_ge(*st_ps.at(l, 2))
                dve.tensor_copy(gstat[:, 4:6], bank[0][:, SEQ:SEQ + 2]).then_inc(st_ok.sem, 1)
                dve.wait_ge(*gr_ok.at(l, 2))
                for n in range(8, 12):
                    added(n, 2)

                normalise(1)
                dve.wait_ge(*pb_in.at(l, 16))
                turned(1, pb[:, G2:G2 + KD])
                dve.wait_ge(*lgT_ps.at(l, 1))
                dve.tensor_scalar(lgT[0:E, :], bank[4][0:E, 0:SEQ], pb[0:E, RB:RB + 1], None, ALU.add).then_inc(lgT_ok.sem, 1)

                rs = [0]

                def step(ins):
                    ins.then_inc(rt.sem, 1)
                    rs[0] += 1

                def settle():
                    dve.wait_ge(*rt.at(l, rs[0]))
                dve.wait_ge(*lg_ps.at(l, 1))
                step(dve.tensor_copy(lg[:, :, :], bank[5][:, 0:TT * E].rearrange("p (t e) -> p t e", t=TT)))
                alone(dve, *rt.at(l, 1))
                for t in range(TT):
                    step(dve.max(top[:, t, :], lg[:, t, :]))
                alone(dve, *rt.at(l, 3))
                for t in range(TT):
                    step(dve.max_index(tix[:, t, :], top[:, t, :], lg[:, t, :]))
                    step(dve.tensor_scalar(ntop[:, t:t + 1], top[:, t, 0:1], -1.0, None, ALU.mult))
                settle()
                step(dve.tensor_copy(tif[:, :, :], tix[:, :, :]))
                dve.wait_ge(*rt_act.at(l, 2))
                step(dve.reciprocal(rp4[:, :], psum4[:, :]))
                settle()
                for t in range(TT):
                    step(dve.tensor_scalar(ptop[:, t, :], ptop[:, t, :], rp4[:, t:t + 1], None, ALU.mult))
                settle()
                for t in range(TT):
                    for k in range(TOPK):
                        step(dve.tensor_scalar(hot[:, t, k, :], iota_e, tif[:, t, k:k + 1], ptop[:, t, k:k + 1],
                                               ALU.is_equal, ALU.mult))
                settle()
                step(dve.tensor_tensor(hot[:, :, 0:2, :], hot[:, :, 0:2, :], hot[:, :, 2:4, :], ALU.add))
                settle()
                step(dve.tensor_tensor(gates[:, :, :], hot[:, :, 0, :], hot[:, :, 1, :], ALU.add))
                ins = dve.wait_ge(*rt.at(l, rs[0]))
                dve.sem_inc(rt.sem, 40 - rs[0])

                def swiglu_in(e, q):
                    dve.wait_ge(*gu_ps.at(l, e + 1))
                    for f in range(2):
                        dve.tensor_scalar(g[:, q, f, :], bank[2 * q][:, f * SEQ:f * SEQ + SEQ],
                                          pb[:, bass.ds(BGU + e * 4 + f, 1)], LIMIT, ALU.add, ALU.min)
                    for f in range(2):
                        ins = dve.tensor_scalar(u[:, q, f, :], bank[2 * q + 1][:, f * SEQ:f * SEQ + SEQ],
                                                pb[:, bass.ds(BGU + e * 4 + 2 + f, 1)], LIMIT, ALU.add, ALU.min)
                    ins.then_inc(gu_rd.sem, 1)
                    dve.wait_ge(*gu_rd.at(l, e + 1))
                    dve.tensor_scalar(u[:, q, :, :], u[:, q, :, :], -LIMIT, 1.0, ALU.max, ALU.add).then_inc(gclip.sem, 1)

                def swiglu_out(e, q):
                    dve.wait_ge(*sg_ok.at(l, e + 1))
                    dve.scalar_tensor_tensor(th[:, q, :, :], th[:, q, :, :], 1.0, g[:, q, :, :], ALU.add, ALU.mult
                                             ).then_inc(gclip.sem, 1)
                    dve.wait_ge(*gclip.at(l, 2 * e + 2))
                    dve.wait_ge(*y_ps.at(l, 2 * e))
                    dve.scalar_tensor_tensor(act_t[:, q, :, :], th[:, q, :, :], 0.5, u[:, q, :, :], ALU.mult, ALU.mult
                                             ).then_inc(act_ok.sem, 1)

                def add_bias():
                    for t in range(TT):
                        dve.wait_ge(*y_ps.at(l, t + 1))
                        for c in range(2):
                            xs = x[:, t, c * 512:c * 512 + 512]
                            dve.tensor_tensor(xs, bank[4 + 2 * t + c][:, :], xs, ALU.add).then_inc(y_ok.sem, 1)

                def add_expert(e):
                    for t in range(TT):
                        dve.wait_ge(*y_ps.at(l, 2 * (e + 1) + t + 1))
                        for c in range(2):
                            dve.wait_ge(*y_ok.at(l, 4 * e + 2 * t + c + 1))
                            xs = x[:, t, c * 512:c * 512 + 512]
                            dve.scalar_tensor_tensor(xs, bank[4 + 2 * t + c][:, :], gates[:, t, bass.ds(e, 1)], xs,
                                                     ALU.mult, ALU.add).then_inc(y_ok.sem, 1)

                swiglu_in(0, 0)
                dve.wait_ge(*gT_ps.at(l, 1))
                dve.tensor_copy(gT[0:E, :], bank[6][0:E, 0:SEQ]).then_inc(gT_ok.sem, 1)
                swiglu_out(0, 0)
                add_bias()
                swiglu_in(1, 1)
                swiglu_out(1, 1)
                with dve.Fori(0, (E - 2) // 2) as i:
                    for q in range(2):
                        add_expert(2 * i + q)
                        swiglu_in(2 * i + 2 + q, q)
                        swiglu_out(2 * i + 2 + q, q)
                add_expert(E - 2)
                add_expert(E - 1)

        @block.scalar
        def _(act):
            act.wait_ge(once.sem, 32)
            with act.Fori(0, DEPTH) as l:
                def squares(c):
                    for t in range(TT):
                        act.activation(xn[:, t, :], x[:, t, :], ACT.Square, accum_out=ms[:, 2 * c + t:2 * c + t + 1]
                                       ).then_inc(ms_ok.sem, 1)

                def turned(c, gain):
                    for b in (0, 2):
                        act.wait_ge(*tr_ok.at(l, 4 * c + b + 1))
                        for dt in range(2):
                            k = 2 * b + dt
                            act.activation(hT[:, k, :], bank[b][:, dt * SEQ:dt * SEQ + SEQ], ACT.Copy,
                                           scale=gain[:, k:k + 1]).then_inc(hT_act.sem, 1)

                act.wait_ge(*y_ok.at(l, 0))
                squares(0)
                act.wait_ge(*pa_in.at(l, 16))
                turned(0, pa[:, G1:G1 + KD])
                act.wait_ge(*sp_dve.at(l, 2))
                act.activation(sp[:, 2, :], sp[:, 1, :], ACT.Exp, scale=-1.0).then_inc(sp_act.sem, 1)
                for w in range(4):
                    act.wait_ge(*proj_ok.at(l, w + 1))
                    if w:
                        act.wait_ge(*hsum_ok.at(l, w))
                    act.activation(sq[:, :], bank[4 + w][:, :], ACT.Square).then_inc(sq_ok.sem, 1)
                for n, dst in enumerate((up[:, :, CONV - 1:], gt[:, :, :], pp[:, :, PAD:])):
                    act.wait_ge(*proj_ok.at(l, 5 + n))
                    act.copy(dst, bank[n][:, :].rearrange("p (c s) -> p c s", c=2)).then_inc(proj_free.sem, 1)
                for w in (0, 2):
                    act.wait_ge(*qkT_ps.at(l, w + 1))
                    act.copy(qkT[:, w // 2, :, 0:P], bank[4 + w][:, :].rearrange("p (c s) -> p c s", c=4)
                             ).then_inc(qkT_ok.sem, 1)
                act.wait_ge(*proj_ok.at(l, 8))
                act.copy(vt[:, 0, :], bank[3][:, :]).then_inc(proj_free.sem, 1)
                for b, dst in enumerate((th_r, th_i)):
                    act.wait_ge(*lru_ps.at(l, b + 1))
                    if b == 0:
                        act.wait_ge(*sp_dve.at(l, 3))
                    for c in range(2):
                        act.activation(dst[:, c, :], bank[b][:, c * SEQ:c * SEQ + SEQ], ACT.Tanh,
                                       bias=hb[:, 2 * b + c:2 * b + c + 1], scale=0.5).then_inc(lru_a.sem, 1)
                act.wait_ge(*lru_d.at(l, 2))
                act.activation(ea[:, :, :], la[:, :, :], ACT.Exp).then_inc(lru_a.sem, 1)
                act.activation(tn[:, :, :], la[:, :, :], ACT.Tanh, scale=-1.0).then_inc(lru_a.sem, 1)
                act.wait_ge(*gelu_p.at(l, 3))
                act.activation(gl[:, :, :], gl[:, :, :], ACT.Tanh, scale=0.7978845608028654).then_inc(gelu_a.sem, 1)
                act.wait_ge(*lru_d.at(l, 6))
                act.activation(tn[:, :, :], tn[:, :, :], ACT.Sqrt).then_inc(lru_a.sem, 1)
                act.wait_ge(*proj_ok.at(l, 9))
                act.copy(vt[:, 1, :], bank[3][:, :]).then_inc(proj_free.sem, 1)

                for h in range(HEADS + 2):
                    if h < HEADS:
                        for t, (a, b) in enumerate(((0, P), (P, KEYS))):
                            act.wait_ge(*s_ok.at(l, 2 * h + t + 1))
                            act.activation(prob[:, h % 2, a:b], prob[:, h % 2, a:b], ACT.Exp,
                                           bias=nmax[:, 2 * h + t:2 * h + t + 1], scale=-1.0,
                                           accum_out=den[:, 2 * h + t:2 * h + t + 1]).then_inc(e_ok.sem, 1)
                    if 1 <= h < HEADS + 1:
                        act.wait_ge(*pt_ps.at(l, h))
                        act.copy(probT[:, (h - 1) % 2, :], bank[6 + (h - 1) % 2][:, 0:KEYS]).then_inc(pt_ok.sem, 1)
                    if h >= 3 and h % 2:
                        pr = (h - 3) // 2
                        act.wait_ge(*o_ps.at(l, pr + 1))
                        act.activation(ysq[:, 4 + pr, :], bank[pr % 2][:, 0:SEQ], ACT.Square).then_inc(ysq_at.sem, 1)

                act.wait_ge(*wo_ok.at(l, 12))
                squares(1)
                act.wait_ge(*pb_in.at(l, 16))
                turned(1, pb[:, G2:G2 + KD])
                act.wait_ge(*rt.at(l, 7))
                for t in range(TT):
                    act.activation(ptop[:, t, :], top[:, t, 0:TOPK], ACT.Exp, bias=ntop[:, t:t + 1],
                                   accum_out=psum4[:, t:t + 1]).then_inc(rt_act.sem, 1)

                with act.Fori(0, E // 2) as i:
                    for q in range(2):
                        e = 2 * i + q
                        act.wait_ge(*gu_rd.at(l, e + 1))
                        act.wait_ge(*act_ok.at(l, 2 * i))
                        act.activation(th[:, q, :, :], g[:, q, :, :], ACT.Tanh, scale=0.5 * ALPHA).then_inc(sg_ok.sem, 1)

        @block.gpsimd
        def _(pool):
            pool.wait_ge(once.sem, 32)
            pool.wait_ge(zeroed.sem, 1)
            with pool.Fori(0, DEPTH) as l:
                def inverse_roots(dst, src, n, scale, after, mid, ok, k):
                    alone(pool, *after)
                    pool.tensor_scalar(dst, src, scale, EPS, ALU.mult, ALU.add).then_inc(mid.sem, 1)
                    pool.wait_ge(*mid.at(l, k))
                    pool.tensor_tensor(dst, dst, half[:, 0:n], ALU.pow).then_inc(ok.sem, 1)

                def token_roots(c):
                    for t in range(TT):
                        a = 2 * c + t
                        inverse_roots(rstd[:, a:a + 1], ms[:, a:a + 1], 1, 1.0 / D, ms_ok.at(l, a + 1), rstd_mid, rstd_ok, a + 1)
                token_roots(0)
                for w in range(4):
                    inverse_roots(hs[:, w, 8:16], hs[:, w, 0:8], 8, 1.0 / DH, hsum_ok.at(l, w + 1), hr_mid, hr_ok, w + 1)

                pool.wait_ge(*proj_free.at(l, 2))
                pool.tensor_tensor(gl[:, :, :], gt[:, :, :], gt[:, :, :], ALU.mult).then_inc(gelu_p.sem, 1)
                alone(pool, *gelu_p.at(l, 1))
                pool.tensor_scalar(gl[:, :, :], gl[:, :, :], 0.044715, 1.0, ALU.mult, ALU.add).then_inc(gelu_p.sem, 1)
                pool.wait_ge(*gelu_p.at(l, 2))
                pool.tensor_tensor(gl[:, :, :], gl[:, :, :], gt[:, :, :], ALU.mult).then_inc(gelu_p.sem, 1)

                pool.wait_ge(*proj_free.at(l, 3))
                N = PAD + SEQ
                steps = [0]

                def turn(out_, in0, in1, op):
                    pool.tensor_tensor(out_, in0, in1, op).then_inc(pool_p.sem, 1)
                    steps[0] += 1
                    pool.wait_ge(*pool_p.at(l, steps[0]))
                turn(p2[:, :, 1:N], pp[:, :, 1:N], pp[:, :, 0:N - 1], ALU.add)
                turn(p4[:, :, 3:N], p2[:, :, 3:N], p2[:, :, 1:N - 2], ALU.add)
                pool.wait_ge(*rope.at(l, 24))
                turn(pooled[0:64, 0, :], p2[0:64, 0, PAD:], invc[0:64, 0, :], ALU.mult)
                turn(pooled[64:P, 0, :], p4[64:P, 0, PAD:], invc[64:P, 0, :], ALU.mult)
                turn(p2[:, 1, 7:N], p4[:, 1, 7:N], p4[:, 1, 3:N - 4], ALU.add)
                turn(pooled[0:64, 1, :], p2[0:64, 1, PAD:], invc[0:64, 1, :], ALU.mult)
                turn(p4[64:P, 1, PAD:N], p2[64:P, 1, PAD:N], p2[64:P, 1, PAD - 8:N - 8], ALU.add)
                turn(pooled[64:P, 1, :], p4[64:P, 1, PAD:], invc[64:P, 1, :], ALU.mult)
                turn(pooled[:, :, :], pooled[:, :, :], pp[:, :, PAD:], ALU.subtract)

                alone(pool, *gelu_a.at(l, 1))
                pool.tensor_scalar(gl[:, :, :], gl[:, :, :], 0.5, 0.5, ALU.mult, ALU.add).then_inc(gelu_p.sem, 1)
                pool.wait_ge(*gelu_p.at(l, 4))
                pool.tensor_tensor(gl[:, :, :], gl[:, :, :], gt[:, :, :], ALU.mult).then_inc(gelu_p.sem, 1)
                pool.wait_ge(*pool_ok.at(l, 2))
                pool.tensor_tensor(ysq[:, 0:2, :], pooled[:, :, :], pooled[:, :, :], ALU.mult).then_inc(ysq_pl.sem, 2)
                pool.wait_ge(*lru_d.at(l, 12))
                pool.tensor_tensor(ysq[:, 2:4, :], xc[:, :, :], xc[:, :, :], ALU.mult).then_inc(ysq_pl.sem, 2)
                inverse_roots(grs[:, 0:4], gstat[:, 0:4], 4, 1.0 / 256, st_ok.at(l, 1), gr_mid, gr_ok, 1)
                inverse_roots(grs[:, 4:6], gstat[:, 4:6], 2, 1.0 / ATT, st_ok.at(l, 2), gr_mid, gr_ok, 2)
                token_roots(1)


def kernel(x, norm1_g, w_in, pool_w, pool_scale, conv_w, conv_b, lru_wa, lru_ba, lru_wx, lru_bx, lru_lambda,
           q_norm_g, k_norm_g, out_norm_g, w_out, norm2_g, router_w, router_b, w_gate_up, b_gate_up, w_down, b_down):
    import numpy as np
    import concourse.bacc as bacc
    from concourse.bass_utils import run_bass_kernel_spmd

    A = np.asarray

    def columns(a, n):
        a = A(a).reshape(DEPTH, -1, n, P)
        return a.transpose(0, 3, 1, 2).reshape(DEPTH, P, -1)

    def block_diagonal(w):
        m = np.zeros((DEPTH, P, 2, P), np.float32)
        for b in range(4):
            r = slice(64 * (b % 2), 64 * (b % 2) + 64)
            m[:, r, b // 2, r] = A(w)[:, b]
        return m.reshape(DEPTH, P, 2 * P)

    def spread(a):
        return np.broadcast_to(A(a)[:, None, :], (DEPTH, P, a.shape[-1]))

    small_a = np.concatenate([
        columns(norm1_g, 8), columns(out_norm_g, 8), columns(pool_scale, 2), columns(conv_w, 2), columns(conv_b, 2),
        columns(lru_ba, 2), columns(lru_bx, 2), columns(lru_lambda, 2), block_diagonal(lru_wa), block_diagonal(lru_wx),
        block_diagonal(pool_w), spread(q_norm_g), spread(k_norm_g)], axis=2)
    rw = A(router_w).reshape(DEPTH, KD, P, E).transpose(0, 2, 1, 3).reshape(DEPTH, P, KD * E)
    bgu = A(b_gate_up).reshape(DEPTH, E, 4, P).transpose(0, 3, 1, 2).reshape(DEPTH, P, E * 4)
    rb = np.zeros((DEPTH, P, 1), np.float32)
    rb[:, 0:E, 0] = A(router_b)
    small_b = np.concatenate([columns(norm2_g, 8), rw, bgu, rb], axis=2)
    w_in_p = A(w_in).reshape(DEPTH, KD, P, IN_W).transpose(0, 2, 1, 3)
    w_out_p = A(w_out).reshape(DEPTH, KD, P, D).transpose(0, 2, 1, 3)
    gu = A(w_gate_up).reshape(DEPTH * E, KD, P, 2 * FF).transpose(0, 2, 1, 3).reshape(DEPTH * E, P, GU)
    dn = A(w_down).reshape(DEPTH * E, 2, P, D).transpose(0, 2, 1, 3).reshape(DEPTH * E, P, DN)
    experts = np.concatenate([gu, dn], axis=2)

    pos = np.arange(SEQ, dtype=np.float32)
    inv_freq = (np.float32(10000.0) ** (-np.arange(0, DH, 2, dtype=np.float32) / np.float32(DH))).astype(np.float32)
    ang = (pos[:, None] * inv_freq[None, :]).astype(np.float32)
    cos = np.concatenate([np.cos(ang), np.cos(ang)], axis=1)
    sin = np.concatenate([-np.sin(ang), np.sin(ang)], axis=1)

    def by_token(a):
        return a.reshape(TT, P, -1).transpose(1, 0, 2).reshape(P, -1)
    dist = np.arange(SEQ)[:, None] - np.arange(SEQ)[None, :]
    seen = (dist >= 0) * ((dist <= 128).astype(np.float64) + (dist % 4 == 0) + (dist % 16 == 0))
    bias = np.where(seen > 0, np.log(np.maximum(seen, 1.0)), -1e30)
    windows = np.array([[2, 4], [8, 16]])
    length = np.minimum(np.arange(1, SEQ + 1)[None, None, :], np.repeat(windows, 64, axis=1)[:, :, None])
    consts = np.concatenate([
        np.eye(P), by_token(cos), by_token(sin), bias[0:P, 0:P], bias[P:SEQ, :],
        (1.0 / length).transpose(1, 0, 2).reshape(P, -1), np.broadcast_to(np.arange(E), (P, E)),
        np.full((P, 16), -0.5), np.ones((P, 1))], axis=1).astype(np.float32)

    arrays = {
        "x_in": A(x).reshape(TT, P, D).transpose(1, 0, 2), "small_a": small_a, "small_b": small_b, "w_in": w_in_p,
        "w_out": w_out_p, "experts": experts, "b_down": A(b_down), "consts": consts,
    }
    arrays = {k: np.ascontiguousarray(v) for k, v in arrays.items()}
    nc = bacc.Bacc("TRN2", target_bir_lowering=False, num_devices=1)
    args = [nc.dram_tensor(k, v.shape, mybir.dt.from_np(v.dtype), kind="ExternalInput").ap() for k, v in arrays.items()]
    out = nc.dram_tensor("out", (P, TT, D), F32, kind="ExternalOutput").ap()
    build(nc, *args, out)
    r = run_bass_kernel_spmd(nc, [arrays], core_ids=[0])
    return r.results[0]["out"].transpose(1, 0, 2).reshape(1, SEQ, D)
```

```python
from contextlib import ExitStack

import concourse.bass as bass
from concourse import mybir

P = 128
F32 = mybir.dt.float32
BF16 = mybir.dt.bfloat16
F32R = mybir.dt.float32r
U32 = mybir.dt.uint32
I32 = mybir.dt.int32
ALU = mybir.AluOpType
ACT = mybir.ActivationFunctionType
AX = mybir.AxisListType

DEPTH, SEQ, D = 2, 256, 1024
TT = SEQ // P
KD = D // P
IN_W = 2304
HEADS, DH = 8, 64
ATT = HEADS * DH
E, FF, TOPK = 32, 256, 4
CONV = 4
PAD = 16
KEYS = P + 2 * P
EPS = 1e-6
LIMIT, ALPHA = 7.0, 1.702
GU = KD * 2 * FF
DN = (FF // P) * D
SLOT = GU + DN
RING = 4
G1, OG, PS, CW, CB, BA, BX, LAM, BD, QG, KG = 0, 8, 16, 18, 26, 28, 30, 32, 34, 802, 866
NA = 930
G2, RW, BGU, RB = 0, 8, 264, 392
NB = 393
CAP = 64
PAIRS, QUADS = E // 2, E // 4
JOBS = SEQ * TOPK // (CAP + 1)
ROUTER_STEPS = 22
ATANH_TERMS = 9


class Counter:

    def __init__(self, sem, per, base=0):
        self.sem, self.per, self.base = sem, per, base

    def at(self, layer, k):
        return self.sem, layer * self.per + k + self.base


class Pair:

    def __init__(self, i, off):
        self.n, self.quad, self.place = 4 * i + off, 2 * i + off // 2, off % 4
        self.first = off % 2 == 0
        self.par = off // 2 % 2
        self.slot = 2 * (off % 2)


def build(nc, x_in, small_a, small_b, w_in, w_out, experts, b_gate_up, b_down, consts, consts_b, out):
    with ExitStack() as ctx:
        def sb(name, *shape, dt=F32):
            return ctx.enter_context(nc.sbuf_tensor(name, [P, *shape], dt))

        def counter(name, per, base=0):
            return Counter(ctx.enter_context(nc.semaphore(name)), per, base)

        bank = [ctx.enter_context(nc.psum_tensor(f"bank{i}", [P, 512], F32)) for i in range(8)]

        x = sb("x", TT, D)
        ring = sb("ring", RING, SLOT)
        with ExitStack() as mixing:
            def shared(name, *shape):
                return mixing.enter_context(nc.sbuf_tensor(name, [P, *shape], F32))
            mixed = shared("mixed", 4096)
            vt = shared("vt", TT, ATT)
            gt = shared("gt", 2, SEQ)
            area = shared("area", KD * D)
        rot = mixed[:, 0:2048].rearrange("p (n t d) -> p n t d", n=2, t=TT)
        qkT = mixed[:, 2048:4096].rearrange("p (n c s) -> p n c s", n=2, c=4)
        wout = area[:, :].rearrange("p (k c) -> p k c", k=KD)
        xs2 = sb("token_parts", 2, TT, D, dt=F32R)
        sm = sb("selection", 2, TT, SEQ, dt=F32R)
        y_lo1 = sb("down_rest_b", FF * 2, dt=F32R)
        tokens = sb("tokens", 4 * D)
        xn = tokens[:, 0:TT * D].rearrange("p (t d) -> p t d", t=TT)
        xT = tokens[:, :].rearrange("p (q k s) -> p q k s", q=2, k=KD)
        jg, ju, jth, jact = (tokens[:, 2 * FF * n:2 * FF * n + 2 * FF].rearrange("p (f s) -> p f s", f=2) for n in range(4))
        y_hi = sb("down_part", D, dt=F32R)
        gm = sb("gates_by_slot", 2, TT, SEQ)
        ag = sb("act_turned", 2, P)
        home = sb("slot_home", SEQ, dt=F32R)
        y_lo = [sb("down_rest_a", FF * 2, dt=F32R), y_lo1]
        units = sb("units", 4 * FF)
        b_src, b_rest = units[:, 0:2 * FF], units[:, 2 * FF:4 * FF]
        g, u, th, act_e = (units[:, FF * n:FF * n + FF] for n in range(4))
        cst = sb("cst", consts.shape[1])
        cstb = sb("cstb", consts_b.shape[1], dt=BF16)
        pa = sb("pa", NA)
        pb = sb("pb", NB)
        ysq = sb("ysq", KD, SEQ)
        hT = sb("hT", KD, SEQ)
        yT = hT
        gcol = sb("gcol", 1)
        ms = sb("ms", 8)
        rstd = sb("rstd", 8)
        tmp = sb("tmp", ATT)
        b_rows = ysq[:, 2, :].bitcast(BF16)
        pick = ysq[:, 3, 0:P // 2].bitcast(BF16)
        cg = sb("cg", 2, 2, TT, DH)
        hs = sb("hs", 4, 16)
        probs = sb("probs", 4, KEYS)
        prob, probT = probs[:, 0:2, :], probs[:, 2:4, :]
        before = probs[:, :, :].rearrange("p a b -> p (a b)")
        sq, swp = before[:, 0:ATT], before[:, ATT:2 * ATT]
        nmax = sb("nmax", 16)
        den = sb("den", 16)
        rden = sb("rden", 16)
        gstat = sb("gstat", 8)
        grs = sb("grs", 8)
        up = sb("up", 2, CONV - 1 + SEQ)
        gl = sb("gl", 2, SEQ)
        hb = sb("hb", 4)
        sp = sb("sp", 12, 2)
        pp = sb("pp", 2, PAD + SEQ)
        ps = sb("ps", 2, 2, PAD + SEQ)
        p2, p4 = ps[:, 0], ps[:, 1]
        pooled = cg[:, :, :, :, :].rearrange("p a b t d -> p (a b t d)").rearrange("p (c s) -> p c s", c=2)

        def two(ap):
            return ap.rearrange("p (c s) -> p c s", c=2)
        th_r, th_i, la, tn = (two(rot[:, n, t, :]) for n in range(2) for t in range(TT))
        ea = th_r
        xc = two(tmp[:, :])
        rec = two(sq[:, :])
        g_dump = up[:, 0, CONV - 1:]
        pflat = ps[:, :, :, :].rearrange("p a b c -> p (a b c)")
        lgT = pflat[:, 0:SEQ]
        gT = pflat[:, SEQ:2 * SEQ]
        hot = pflat[:, 2 * SEQ:2 * SEQ + TT * TOPK * E].rearrange("p (t k e) -> p t k e", t=TT, k=TOPK)
        bdn = probs[:, :, :].rearrange("p a b -> p (a b)")[:, 0:D]
        top = sb("top", TT, 8)
        tix = sb("tix", TT, 8, dt=U32)
        tif = sb("tif", TT, 8)
        ntop = sb("ntop", TT)
        ptop = sb("ptop", TT, TOPK)
        psum4 = sb("psum4", TT)
        rp4 = sb("rp4", TT)
        by_expert = gl[:, :, :].rearrange("p a (b e) -> p (a b) e", e=E)
        gates, halfg, rank, over_g = (by_expert[:, TT * n:TT * n + TT, :] for n in range(4))
        sel = by_expert[:, 8, :].bitcast(BF16).rearrange("p (t e) -> p t e", t=TT)
        count, over, place, over_e = (by_expert[:, 9 + n, :] for n in range(4))
        lg = by_expert[:, 13:15, :]
        job_f = sb("job_f", 3 + JOBS)
        job = sb("job", 3 + JOBS, dt=I32)
        is_job = tmp[:, 0:JOBS * E].rearrange("p (j e) -> p j e", j=JOBS)

        ident = cst[:, 0:128]
        cos_t = cst[:, 128:256].rearrange("p (t d) -> p t d", t=TT)
        sin_t = cst[:, 256:384].rearrange("p (t d) -> p t d", t=TT)
        mask = cst[:, 384:768]
        invc = cst[:, 768:1280].rearrange("p (t s) -> p t s", t=2)
        iota_e = cst[:, 1280:1312]
        half = cst[:, 1312:1328]
        ones = cst[:, 1328:1329]
        slots = cst[:, 1329:1329 + P]
        owner = cst[:, 1457:1457 + P]
        one_row = cst[:, 1585:1585 + E]
        before_b, all_b = cstb[:, 0:P], cstb[:, P:2 * P]
        win = ring[:, 1:4, :].rearrange("p r c -> p (r c)").rearrange("p (k c) -> p k c", k=KD)

        passed = counter("waits_passed", 0)
        once, zeroed = counter("once_landed", 0), counter("pads_zeroed", 0)
        pa_in, pb_in = counter("params_a_landed", 16), counter("params_b_landed", 16)
        bdn_in = counter("b_down_landed", 16)
        win_in = [counter(f"w_in_{n}_landed", 16) for n in range(3)]
        wout_in = counter("w_out_landed", 16)
        up_in = [counter(f"gate_up_slot{j}_landed", 16 * (E // RING)) for j in range(RING)]
        down_in = [counter(f"down_slot{j}_landed", 16 * (E // RING)) for j in range(RING)]
        ms_ok = counter("squares_summed", 4)
        rstd_ok = counter("rstd_ready", 4)
        rstd_mid = counter("rstd_half", 4)
        xn_ok = counter("tokens_normalised", 4)
        tr_ok = counter("h_transposed", 8)
        hT_act, hT_dve = counter("hT_by_act", 8), counter("hT_by_dve", 8)
        proj_ok = counter("projected", 9)
        proj_free = counter("projection_copied", 5)
        sq_ok = counter("qk_squared", 4)
        hsum_ok = counter("qk_head_sums", 4)
        hr_mid, hr_ok = counter("qk_rstd_half", 4), counter("qk_rstd_ready", 4)
        rope = counter("rope_steps", 24)
        qkT_ps, qkT_ok = counter("qk_transposed", 4), counter("qkT_ready", 4)
        sp_dve, sp_act = counter("softplus_steps", 19), counter("softplus_exp", 1)
        conv_ok = counter("conv_steps", 8)
        lru_ps = counter("lru_gates_product", 2)
        lru_a = counter("lru_activations", 7)
        lru_d = counter("lru_steps", 14)
        gelu_p, gelu_a = counter("gelu_steps", 5), counter("gelu_tanh", 1)
        pool_p, pool_ps, pool_ok = counter("pool_steps", 9), counter("pool_product", 1), counter("pool_out", 2)
        ysq_pl, ysq_at = counter("y_squares", 4), counter("attention_squares", 4)
        st_ps, st_ok = counter("group_sums", 2), counter("group_sums_copied", 2)
        gr_mid, gr_ok = counter("group_rstd_half", 2), counter("group_rstd_ready", 2)
        s_ps, s_ok, e_ok = counter("scores", 8), counter("scores_masked", 16), counter("exp_done", 16)
        rd_ok, pn_ok = counter("den_reciprocal", 8), counter("probs_normalised", 8)
        pt_ps, pt_ok = counter("probs_transposed", 8), counter("probsT_copied", 8)
        o_ps, o_ok = counter("attention_out", 4), counter("attention_yT", 4)
        wo_ps, wo_ok = counter("w_out_product", 12), counter("w_out_added", 12)
        lgT_ps, lgT_ok = counter("logitsT", 1), counter("logitsT_copied", 1)
        lg_ps, rt = counter("logits", 1), counter("router_steps", ROUTER_STEPS)
        rt_act = counter("router_exp", 2)
        gT_ps, gT_ok = counter("gates_transposed", 1), counter("gatesT_copied", 1)
        x0_ok, x1_ok = counter("x_first_part", 2), counter("x_second_part", 2)
        bsrc_in, brow_ok = counter("b_gate_up_landed", 16), counter("bias_rows_steps", 6)
        rk_ps, rk_ok = counter("ranks_product", 1), counter("ranks_steps", 3)
        sm_ok, gm_ok = counter("selection_built", QUADS), counter("gates_spread", QUADS)
        pick_ok = counter("owners_built", PAIRS)
        gth_ps = counter("tokens_gathered", 4 * QUADS)
        xT_dve, xT_act = counter("xT_by_dve", 2 * QUADS), counter("xT_by_act", 2 * QUADS)
        gu_ps, gu_rd = counter("gate_up_product", PAIRS), counter("gate_up_read", PAIRS, base=1)
        sg_ok, am_ok, act_ok = counter("tanh_done", PAIRS), counter("swiglu_half", PAIRS), counter("swiglu_done", PAIRS, base=1)
        ag_ps, ag_ok = counter("act_turned", PAIRS), counter("act_turned_copied", PAIRS, base=1)
        gc_ok, home_ok = counter("slot_gates", PAIRS, base=1), counter("slot_homes", PAIRS, base=1)
        ylo_ok = counter("down_second_part", 2 * PAIRS, base=1)
        dn_ps, y_rd = counter("down_product", 2 * PAIRS, base=3), counter("down_first_part", 2 * PAIRS, base=1)
        acc_ps, x_ok = counter("combined", PAIRS, base=1), counter("x_added", 4, base=1)
        list_ok = counter("job_list_steps", 9)
        job_in, job_gu = counter("job_weights_landed", 16), counter("job_gate_up_product", 2)
        job_step, job_th = counter("job_swiglu_steps", 5), counter("job_tanh_done", 1)
        job_dn, job_x = counter("job_down_product", 4, base=1), counter("job_added", 4, base=1)
        stored = counter("out_stored", 0)

        def alone(eng, sem, value):
            eng.wait_ge(sem, value)
            eng.sem_inc(passed.sem, 1)

        def entry(eng, k, most):
            return eng.value_load(job[0:1, bass.ds(k, 1)], min_val=0, max_val=most)

        def for_jobs(eng, number, body):
            with eng.If(number > 0):
                body(0)
            with eng.If(number > 1):
                with eng.Fori(1, JOBS) as j:
                    with eng.If(number > j):
                        body(j)

        block = ctx.enter_context(nc.Block())

        def one(a, n):
            return a[bass.ds(n, 1)].rearrange("o p c -> (o p) c")

        @block.sync
        def _(sp_):
            sp_.dma_start(x[:, :, :], x_in).then_inc(once.sem, 16)
            sp_.dma_start(cst[:, :], consts).then_inc(once.sem, 16)
            sp_.dma_start(cstb[:, :], consts_b).then_inc(once.sem, 16)
            sp_.wait_ge(zeroed.sem, 2)
            with sp_.Fori(0, DEPTH) as l:
                for n in range(3):
                    sp_.wait_ge(*dn_ps.at(l, -2 if n == 0 else 0))
                    if n == 0:
                        sp_.dma_start(pa[:, :], one(small_a, l)).then_inc(pa_in.sem, 16)
                    sp_.dma_start(ring[:, 1 + n, :], one(w_in, l)[:, n * SLOT:n * SLOT + SLOT]).then_inc(win_in[n].sem, 16)
                done = entry(sp_, 2, DEPTH * JOBS)
                sp_.wait_ge(*job_dn.at(done, 0))
                sp_.dma_start(pb[:, :], one(small_b, l)).then_inc(pb_in.sem, 16)
                sp_.wait_ge(*tr_ok.at(l, 4))
                sp_.dma_start(area[:, :], one(w_out, l)).then_inc(wout_in.sem, 16)
                for j in range(RING):
                    if j == 1:
                        sp_.wait_ge(*proj_ok.at(l, 9))
                    sp_.dma_start(ring[:, j, 0:GU], one(experts, l * E + j)[:, 0:GU]).then_inc(up_in[j].sem, 16)
                    sp_.dma_start(ring[:, j, GU:SLOT], one(experts, l * E + j)[:, GU:SLOT]).then_inc(down_in[j].sem, 16)

                def load_gate_up(p, odd=None):
                    s0 = 2 * ((p if odd is None else odd) % 2)
                    sp_.wait_ge(*gu_ps.at(l, p - 1))
                    for s in range(2):
                        sp_.dma_start(ring[:, s0 + s, 0:GU], one(experts, l * E + 2 * p + s)[:, 0:GU]).then_inc(up_in[s0 + s].sem, 16)

                def load_down(p, odd=None):
                    s0 = 2 * ((p if odd is None else odd) % 2)
                    sp_.wait_ge(*dn_ps.at(l, 2 * (p - 1)))
                    for s in range(2):
                        sp_.dma_start(ring[:, s0 + s, GU:SLOT], one(experts, l * E + 2 * p + s)[:, GU:SLOT]).then_inc(down_in[s0 + s].sem, 16)
                sp_.wait_ge(*o_ps.at(l, 4))
                sp_.dma_start(bdn[0:E, :], one(b_down, l)).then_inc(bdn_in.sem, 16)
                sp_.wait_ge(*wo_ps.at(l, 12))
                sp_.dma_start(b_src[0:3 * E, :], one(b_gate_up, l)).then_inc(bsrc_in.sem, 16)
                load_gate_up(2)
                with sp_.Fori(1, PAIRS // 2 - 1) as i:
                    for n in (1, 2):
                        load_gate_up(2 * i + n, n)
                        load_down(2 * i + n - 1, n - 1)
                load_gate_up(PAIRS - 1)
                load_down(PAIRS - 2)
                load_down(PAIRS - 1)

                def load_job(j):
                    alone(sp_, *job_dn.at(seen + j, 0))
                    e = entry(sp_, 3 + j, E - 1)
                    sp_.dma_start(ring[:, 0, :], one(experts, l * E + e)).then_inc(job_in.sem, 16)
                alone(sp_, *list_ok.at(l, 9))
                number, seen = entry(sp_, 0, JOBS), entry(sp_, 1, DEPTH * JOBS)
                alone(sp_, *dn_ps.at(l, 2 * PAIRS - 2))
                for_jobs(sp_, number, load_job)
            alone(sp_, *x_ok.at(DEPTH, 0))
            sp_.wait_ge(*job_x.at(entry(sp_, 2, DEPTH * JOBS), 0))
            sp_.dma_start(out, x[:, :, :]).then_inc(stored.sem, 16)
            sp_.wait_ge(stored.sem, 16)

        @block.tensor
        def _(pe):
            pe.sem_inc(dn_ps.sem, 3)
            pe.sem_inc(job_dn.sem, 1)
            pe.sem_inc(acc_ps.sem, 1)
            pe.wait_ge(once.sem, 48)
            with pe.Fori(0, DEPTH) as l:
                def transpose_tokens(c):
                    for t in range(TT):
                        pe.wait_ge(*xn_ok.at(l, 2 * c + t + 1))
                        for b in range(4):
                            for dt in range(2):
                                k = 2 * b + dt
                                mm = pe.transpose(bank[b][:, dt * SEQ + t * P:dt * SEQ + t * P + P],
                                                  xn[:, t, k * P:k * P + P], ident)
                            if t == TT - 1:
                                mm.then_inc(tr_ok.sem, 1)

                transpose_tokens(0)

                pe.wait_ge(*hT_act.at(l, 4))
                pe.wait_ge(*hT_dve.at(l, 4))
                for k in range(KD):
                    if k in (0, 2, 5):
                        pe.wait_ge(*win_in[(0, 2, 5).index(k)].at(l, 16))
                    for n in range(2):
                        for t in range(TT):
                            mm = pe.matmul(bank[4 + 2 * n + t][:, :], hT[:, k, t * P:t * P + P],
                                           win[:, k, 768 + 512 * n:1280 + 512 * n], start=(k == 0), stop=(k == KD - 1))
                            if k == KD - 1:
                                mm.then_inc(proj_ok.sem, 1)
                for b, c0 in enumerate((256, 512, 0)):
                    for c in range(2):
                        for k in range(KD):
                            mm = pe.matmul(bank[b][:, c * SEQ:c * SEQ + SEQ], win[:, k, c0 + c * P:c0 + c * P + P],
                                           hT[:, k, :], start=(k == 0), stop=(k == KD - 1))
                    mm.then_inc(proj_ok.sem, 1)
                for n in range(2):
                    for t in range(TT):
                        pe.wait_ge(*rope.at(l, 6 * (2 * n + t + 1)))
                        for c in range(4):
                            mm = pe.transpose(bank[4 + 2 * n + t][:, c * P:c * P + P], rot[:, n, t, c * P:c * P + P], ident)
                        mm.then_inc(qkT_ps.sem, 1)

                def project_v(t):
                    for k in range(KD):
                        mm = pe.matmul(bank[3][:, :], hT[:, k, t * P:t * P + P], win[:, k, 1792:2304],
                                       start=(k == 0), stop=(k == KD - 1))
                    mm.then_inc(proj_ok.sem, 1)
                project_v(0)
                pe.wait_ge(*conv_ok.at(l, 8))
                pe.wait_ge(*proj_free.at(l, 2))
                for b in range(2):
                    for c in range(2):
                        w = pa[:, BD + (2 * b + c) * P:BD + (2 * b + c + 1) * P]
                        mm = pe.matmul(bank[b][:, c * SEQ:c * SEQ + SEQ], w, xc[:, c, :], start=True, stop=True)
                    mm.then_inc(lru_ps.sem, 1)
                pe.wait_ge(*proj_free.at(l, 4))
                project_v(1)
                pe.wait_ge(*pool_p.at(l, 9))
                pe.wait_ge(*proj_free.at(l, 3))
                for c in range(2):
                    mm = pe.matmul(bank[2][:, c * SEQ:c * SEQ + SEQ], pa[:, BD + (4 + c) * P:BD + (5 + c) * P],
                                   pooled[:, c, :], start=True, stop=True)
                mm.then_inc(pool_ps.sem, 1)

                def scores(h):
                    if h == 0:
                        pe.wait_ge(*qkT_ok.at(l, 4))
                    if h >= 2:
                        pe.wait_ge(*s_ok.at(l, 2 * h - 2))
                    s, r = bank[4 + h % 2], slice(DH * (h % 2), DH * (h % 2) + DH)
                    pe.matmul(s[:, 0:P], qkT[r, 0, h // 2, 0:P], qkT[r, 1, h // 2, 0:P], start=True, stop=True)
                    pe.matmul(s[:, P:KEYS], qkT[r, 0, h // 2, P:SEQ], qkT[r, 1, h // 2, :], start=True,
                              stop=True).then_inc(s_ps.sem, 1)

                def turn_probs(h):
                    pe.wait_ge(*pn_ok.at(l, h + 1))
                    if h == 0:
                        pe.wait_ge(*qkT_ok.at(l, 4))
                    if h >= 2:
                        pe.wait_ge(*pt_ok.at(l, h - 1))
                    for c in range(3):
                        mm = pe.transpose(bank[6 + h % 2][:, c * P:c * P + P], prob[:, h % 2, c * P:c * P + P], ident)
                    mm.then_inc(pt_ps.sem, 1)

                def values(h):
                    pr = h // 2
                    pe.wait_ge(*pt_ok.at(l, h + 1))
                    if h == 0:
                        pe.wait_ge(*proj_free.at(l, 5))
                        pe.wait_ge(*st_ok.at(l, 1))
                    if h == 2:
                        pe.wait_ge(*lru_a.at(l, 4))
                    if h >= 4 and h % 2 == 0:
                        pe.wait_ge(*o_ok.at(l, pr - 1))
                    o = bank[pr % 2][DH * (h % 2):DH * (h % 2) + DH, :]
                    pe.matmul(o[:, 0:SEQ], vt[:, 0, h * DH:h * DH + DH], probT[:, h % 2, 0:SEQ],
                              start=True, stop=False)
                    mm = pe.matmul(o[:, P:SEQ], vt[:, 1, h * DH:h * DH + DH], probT[:, h % 2, SEQ:KEYS],
                                   start=False, stop=True)
                    if h % 2:
                        mm.then_inc(o_ps.sem, 1)

                def group_sums(b, groups):
                    for n, (k0, k1) in enumerate(groups):
                        for t in range(TT):
                            c = SEQ + 2 * n + t
                            for k in range(k0, k1):
                                mm = pe.matmul(bank[b][:, c:c + 1], ysq[:, k, t * P:t * P + P], ones,
                                               start=(k == k0), stop=(k == k1 - 1))
                    mm.then_inc(st_ps.sem, 1)

                def out_unit(n, k0, k1):
                    t, c = (n // 2) % 2, n % 2
                    if n == 0:
                        pe.wait_ge(*wout_in.at(l, 16))
                        pe.wait_ge(*pool_ok.at(l, 2))
                    if n == 1:
                        pe.wait_ge(*proj_free.at(l, 5))
                    if n >= 2:
                        pe.wait_ge(*wo_ok.at(l, n - 1))
                    for k in range(k0, k1):
                        mm = pe.matmul(bank[2 + n % 2][:, :], yT[:, k, t * P:t * P + P], wout[:, k, c * 512:c * 512 + 512],
                                       start=(k == k0), stop=(k == k1 - 1))
                    mm.then_inc(wo_ps.sem, 1)

                for h in range(HEADS + 2):
                    if h < HEADS:
                        scores(h)
                    if h == 1:
                        pe.wait_ge(*ysq_pl.at(l, 4))
                        pe.wait_ge(*lru_a.at(l, 2))
                        group_sums(0, ((0, 2), (2, 4)))
                    if h >= 2:
                        values(h - 2)
                        if h - 2 < 4:
                            out_unit(h - 2, 0, 2)
                        else:
                            if h - 2 == 4:
                                pe.wait_ge(*lru_d.at(l, 14))
                            out_unit(h - 2, 2, 4)
                    if 1 <= h < HEADS + 1:
                        turn_probs(h - 1)
                pe.wait_ge(*ysq_at.at(l, 4))
                pe.wait_ge(*o_ok.at(l, 4))
                group_sums(0, ((4, 8),))
                for n in range(8, 12):
                    out_unit(n, 4, 8)

                pe.wait_ge(*st_ok.at(l, 2))
                pe.wait_ge(*wo_ok.at(l, 12))
                transpose_tokens(1)
                pe.wait_ge(*pb_in.at(l, 16))
                pe.wait_ge(*hT_act.at(l, 8))
                pe.wait_ge(*hT_dve.at(l, 8))
                for k in range(KD):
                    mm = pe.matmul(bank[4][0:E, 0:SEQ], pb[:, RW + k * E:RW + k * E + E], hT[:, k, :],
                                   start=(k == 0), stop=(k == KD - 1))
                mm.then_inc(lgT_ps.sem, 1)

                alone(pe, *lgT_ok.at(l, 1))
                for t in range(TT):
                    mm = pe.transpose(bank[5][:, t * E:t * E + E], lgT[0:E, t * P:t * P + P], ident[0:E, 0:E])
                mm.then_inc(lg_ps.sem, 1)
                pe.wait_ge(*rk_ok.at(l, 1))
                pe.matmul(bank[6][:, 0:E], before_b, sel[:, 0, :], start=True, stop=True)
                pe.matmul(bank[6][:, E:2 * E], all_b, sel[:, 0, :], start=True, stop=False)
                pe.matmul(bank[6][:, E:2 * E], before_b, sel[:, 1, :], start=False, stop=True)
                pe.matmul(bank[6][:, 2 * E:3 * E], all_b, sel[:, 0, :], start=True, stop=False)
                pe.matmul(bank[6][:, 2 * E:3 * E], all_b, sel[:, 1, :], start=False, stop=True).then_inc(rk_ps.sem, 1)
                for t in range(TT):
                    mm = pe.transpose(bank[7][0:E, t * P:t * P + P], gates[:, t, :], ident)
                mm.then_inc(gT_ps.sem, 1)

                def gather(quad, par, c, b=3):
                    if b == 3 and par is not None:
                        pe.wait_ge(*(xT_act.at(l, 2 * quad + (c + 1) // 2) if c % 2 else xT_dve.at(l, 2 * quad + c // 2)))
                    for dt in range(2):
                        k = 2 * c + dt
                        for t in range(TT):
                            for n in range(2):
                                mm = pe.matmul(bank[b][:, dt * SEQ:dt * SEQ + SEQ], xs2[:, n, t, k * P:k * P + P],
                                               sm[:, par or 0, t, :], start=(t == 0 and n == 0),
                                               stop=(t == 1 and n == 1))
                    mm.then_inc(gth_ps.sem, 1)

                def gate_up(p):
                    for s in range(2):
                        pe.wait_ge(*up_in[p.slot + s].at(l, 16 * (p.quad + 1)))
                    pe.wait_ge(*pick_ok.at(l, p.n + 1))
                    pe.wait_ge(*gu_rd.at(l, p.n))
                    if p.first:
                        pe.wait_ge(*xT_dve.at(l, 2 * p.quad + 2))
                        pe.wait_ge(*xT_act.at(l, 2 * p.quad + 2))
                    pe.matmul(bank[0][:, :], pick[0:3 * E, :], b_rows[0:3 * E, :], start=True, stop=False,
                              skip_group_check=True)
                    for k in range(KD):
                        for s in range(2):
                            c = (p.slot + s) * CAP
                            mm = pe.matmul(bank[0][s * CAP:s * CAP + CAP, :], xT[:, p.par, k, c:c + CAP],
                                           ring[:, p.slot + s, k * 2 * FF:(k + 1) * 2 * FF], start=False,
                                           stop=(k == KD - 1), skip_group_check=True)
                    mm.then_inc(gu_ps.sem, 1)

                def turn(p):
                    pe.wait_ge(*act_ok.at(l, p.n + 1))
                    pe.wait_ge(*gm_ok.at(l, p.quad + 1))
                    pe.wait_ge(*y_rd.at(l, 2 * p.n))
                    pe.wait_ge(*ylo_ok.at(l, 2 * p.n))
                    for f in range(2):
                        pe.transpose(bank[1][:, f * P:f * P + P], act_e[:, f * P:f * P + P], ident)
                    for t in range(TT):
                        c = p.slot * CAP
                        mm = pe.transpose(bank[2][:, t * P:t * P + P], gm[:, p.par, t, c:c + P], ident)
                    mm.then_inc(ag_ps.sem, 1)

                def down(p):
                    pe.wait_ge(*ag_ok.at(l, p.n + 1))
                    for s in range(2):
                        pe.wait_ge(*down_in[p.slot + s].at(l, 16 * (p.quad + 1)))
                    for h in range(2):
                        if h:
                            pe.wait_ge(*gc_ok.at(l, p.n + 1))
                        for k in range(2):
                            for s in range(2):
                                mm = pe.matmul(bank[1 + h][s * CAP:s * CAP + CAP, :], ag[:, k, s * CAP:s * CAP + CAP],
                                               ring[:, p.slot + s, GU + k * D + h * 512:GU + k * D + h * 512 + 512],
                                               start=(k == 0), stop=(k == 1), skip_group_check=True)
                        mm.then_inc(dn_ps.sem, 1)

                def combine(p):
                    for h in range(2):
                        pe.wait_ge(*y_rd.at(l, 2 * p.n + h + 1))
                        pe.wait_ge(*ylo_ok.at(l, 2 * p.n + h + 1))
                        for t in range(TT):
                            for part in (y_hi[:, h * 512:h * 512 + 512], y_lo[h][:, :]):
                                mm = pe.matmul(bank[4 + 2 * t + h][:, :], home[:, t * P:t * P + P], part,
                                               start=False, stop=False, skip_group_check=True)
                    mm.then_inc(acc_ps.sem, 1)

                pe.wait_ge(*x0_ok.at(l, 2))
                pe.wait_ge(*x1_ok.at(l, 2))
                pe.wait_ge(*sm_ok.at(l, 1))
                for c in range(4):
                    gather(0, None, c, b=c)
                pe.wait_ge(*gT_ok.at(l, 1))
                pe.wait_ge(*rk_ok.at(l, 3))
                pe.wait_ge(*bdn_in.at(l, 16))
                for t in range(TT):
                    for h in range(2):
                        pe.matmul(bank[4 + 2 * t + h][:, :], gT[0:E, t * P:t * P + P], bdn[0:E, h * 512:h * 512 + 512],
                                  start=True, stop=False, skip_group_check=True)
                pe.wait_ge(*brow_ok.at(l, 6))

                def pair_turn(p, before, more=True):
                    gate_up(p)
                    if before:
                        turn(before)
                    if more:
                        if p.first:
                            pe.wait_ge(*sm_ok.at(l, p.quad + 2))
                        gather(p.quad + 1, 1 - p.par, p.slot)
                    if before:
                        down(before)
                    if more:
                        gather(p.quad + 1, 1 - p.par, p.slot + 1)
                    if before:
                        combine(before)

                pair_turn(Pair(0, 0), None)
                with pe.Fori(0, PAIRS // 4 - 1) as i:
                    for n in range(4):
                        pair_turn(Pair(i, n + 1), Pair(i, n))
                for n in range(PAIRS - 3, PAIRS):
                    pair_turn(Pair(0, n), Pair(0, n - 1), more=n < PAIRS - 2)
                turn(Pair(0, PAIRS - 1))
                down(Pair(0, PAIRS - 1))
                combine(Pair(0, PAIRS - 1))

                alone(pe, *list_ok.at(l, 9))
                number, seen = entry(pe, 0, JOBS), entry(pe, 1, DEPTH * JOBS)

                def expert_job(j):
                    pe.wait_ge(*job_in.at(seen + j, 16))
                    for b in range(2):
                        for f in range(2):
                            for k in range(KD):
                                c = k * 2 * FF + b * FF + f * P
                                mm = pe.matmul(bank[3 * b][:, f * SEQ:f * SEQ + SEQ], ring[:, 0, c:c + P], hT[:, k, :],
                                               start=(k == 0), stop=(k == KD - 1))
                        mm.then_inc(job_gu.sem, 1)
                    pe.wait_ge(*job_step.at(seen + j, 5))
                    pe.wait_ge(*x_ok.at(l, 4))
                    pe.wait_ge(*job_x.at(seen + j, 0))
                    for t in range(TT):
                        for h in range(2):
                            for f in range(2):
                                c = GU + f * D + h * 512
                                mm = pe.matmul(bank[4 + 2 * t + h][:, :], jact[:, f, t * P:t * P + P],
                                               ring[:, 0, c:c + 512], start=(f == 0), stop=(f == 1))
                            mm.then_inc(job_dn.sem, 1)
                for_jobs(pe, number, expert_job)

        @block.vector
        def _(dve):
            for c in (gu_rd, act_ok, x_ok, job_x, home_ok, ylo_ok):
                dve.sem_inc(c.sem, 1)
            dve.memset(up[:, :, 0:CONV - 1], 0.0)
            dve.memset(pp[:, :, 0:PAD], 0.0).then_inc(zeroed.sem, 1)
            dve.memset(job_f[:, :], 0.0)
            dve.memset(job[:, :], 0).then_inc(zeroed.sem, 1)
            dve.wait_ge(once.sem, 48)
            dve.wait_ge(zeroed.sem, 2)
            with dve.Fori(0, DEPTH) as l:
                def normalise(c):
                    for t in range(TT):
                        dve.wait_ge(*rstd_ok.at(l, 2 * c + t + 1))
                        dve.tensor_scalar(xn[:, t, :], x[:, t, :], rstd[:, 2 * c + t:2 * c + t + 1], None, ALU.mult
                                          ).then_inc(xn_ok.sem, 1)

                def turned(c, gain):
                    for b in (1, 3):
                        dve.wait_ge(*tr_ok.at(l, 4 * c + b + 1))
                        for dt in range(2):
                            k = 2 * b + dt
                            dve.tensor_scalar(hT[:, k, :], bank[b][:, dt * SEQ:dt * SEQ + SEQ], gain[:, k:k + 1], None,
                                              ALU.mult).then_inc(hT_dve.sem, 1)

                normalise(0)
                dve.wait_ge(*pa_in.at(l, 16))
                turned(0, pa[:, G1:G1 + KD])

                steps = [0]

                def tiny(ins):
                    ins.then_inc(sp_dve.sem, 1)
                    steps[0] += 1
                    dve.wait_ge(*sp_dve.at(l, steps[0]))
                lam = pa[:, LAM:LAM + 2]
                tiny(dve.tensor_scalar(sp[:, 0, :], lam, -1.0, None, ALU.mult))
                tiny(dve.tensor_tensor(sp[:, 1, :], lam, sp[:, 0, :], ALU.max))
                tiny(dve.tensor_scalar(hb[:, :], pa[:, BA:BA + 4], 0.5, None, ALU.mult))
                dve.wait_ge(*sp_act.at(l, 1))
                tiny(dve.tensor_scalar(sp[:, 3, :], sp[:, 2, :], 2.0, None, ALU.add))
                tiny(dve.reciprocal(sp[:, 4, :], sp[:, 3, :]))
                tiny(dve.tensor_tensor(sp[:, 5, :], sp[:, 2, :], sp[:, 4, :], ALU.mult))
                tiny(dve.tensor_tensor(sp[:, 6, :], sp[:, 5, :], sp[:, 5, :], ALU.mult))
                tiny(dve.tensor_scalar(sp[:, 7, :], sp[:, 6, :], 1.0 / (2 * ATANH_TERMS - 1), None, ALU.mult))
                for k in range(ATANH_TERMS - 2, 0, -1):
                    tiny(dve.scalar_tensor_tensor(sp[:, 7, :], sp[:, 7, :], 1.0 / (2 * k + 1), sp[:, 6, :], ALU.add, ALU.mult))
                tiny(dve.scalar_tensor_tensor(sp[:, 8, :], sp[:, 7, :], 1.0, sp[:, 5, :], ALU.add, ALU.mult))
                tiny(dve.tensor_scalar(sp[:, 9, :], sp[:, 0, :], 0.0, -4.0, ALU.max, ALU.mult))
                tiny(dve.scalar_tensor_tensor(sp[:, 10, :], sp[:, 8, :], -8.0, sp[:, 9, :], ALU.mult, ALU.add))
                for n, (g0, scale) in enumerate(((QG, DH ** -0.5), (KG, 1.0))):
                    gain = pa[:, g0:g0 + DH].unsqueeze(1).broadcast_to([P, TT, DH])
                    dve.scalar_tensor_tensor(cg[:, n, 0, :, :], cos_t, scale, gain, ALU.mult, ALU.mult)
                    for a, b in ((0, 32), (32, 0)):
                        gs = pa[:, g0 + b:g0 + b + 32].unsqueeze(1).broadcast_to([P, TT, 32])
                        ins = dve.scalar_tensor_tensor(cg[:, n, 1, :, a:a + 32], sin_t[:, :, a:a + 32], scale, gs,
                                                       ALU.mult, ALU.mult)
                tiny(ins)
                assert steps[0] == 19

                def rope_unit(n, t):
                    w = 2 * n + t
                    b3 = bank[4 + w][:, :].rearrange("p (h d) -> p h d", h=HEADS)
                    dve.wait_ge(*sq_ok.at(l, w + 1))
                    dve.tensor_reduce(hs[:, w, 0:8], sq[:, :].rearrange("p (h d) -> p h d", h=HEADS), AX.X, ALU.add
                                      ).then_inc(hsum_ok.sem, 1)
                    dve.wait_ge(*hr_ok.at(l, w + 1))
                    r0 = 6 * w
                    t3 = tmp[:, :].rearrange("p (h d) -> p h d", h=HEADS)
                    s3 = swp[:, :].rearrange("p (h d) -> p h d", h=HEADS)
                    o3 = rot[:, n, t, :].rearrange("p (h d) -> p h d", h=HEADS)
                    dve.tensor_tensor(t3, b3, hs[:, w, 8:16].unsqueeze(2).broadcast_to([P, HEADS, DH]), ALU.mult
                                      ).then_inc(rope.sem, 1)
                    dve.wait_ge(*rope.at(l, r0 + 1))
                    cgc = cg[:, n, 0, t, :].unsqueeze(1).broadcast_to([P, HEADS, DH])
                    dve.tensor_tensor(o3, t3, cgc, ALU.mult).then_inc(rope.sem, 1)
                    for a, b in ((0, 32), (32, 0)):
                        cgs = cg[:, n, 1, t, a:a + 32].unsqueeze(1).broadcast_to([P, HEADS, 32])
                        dve.tensor_tensor(s3[:, :, a:a + 32], t3[:, :, b:b + 32], cgs, ALU.mult).then_inc(rope.sem, 1)
                    dve.wait_ge(*rope.at(l, r0 + 4))
                    dve.tensor_tensor(o3, o3, s3, ALU.add).then_inc(rope.sem, 2)

                for n in range(2):
                    for t in range(TT):
                        rope_unit(n, t)

                dve.wait_ge(*proj_free.at(l, 1))
                for c in range(2):
                    w = [pa[:, CW + 2 * j + c:CW + 2 * j + c + 1] for j in range(CONV)]
                    dve.tensor_scalar(xc[:, c, :], up[:, c, 0:SEQ], w[0], pa[:, CB + c:CB + c + 1], ALU.mult, ALU.add
                                      ).then_inc(conv_ok.sem, 1)
                for j in range(1, CONV):
                    for c in range(2):
                        dve.wait_ge(*conv_ok.at(l, 2 * j + c - 1))
                        dve.scalar_tensor_tensor(xc[:, c, :], up[:, c, j:j + SEQ], pa[:, CW + 2 * j + c:CW + 2 * j + c + 1],
                                                 xc[:, c, :], ALU.mult, ALU.add).then_inc(conv_ok.sem, 1)
                for w in (1, 3):
                    dve.wait_ge(*qkT_ps.at(l, w + 1))
                    dve.tensor_copy(qkT[:, w // 2, :, P:SEQ], bank[4 + w][:, :].rearrange("p (c s) -> p c s", c=4)
                                    ).then_inc(qkT_ok.sem, 1)

                dve.wait_ge(*lru_a.at(l, 2))
                for c in range(2):
                    dve.tensor_scalar(la[:, c, :], th_r[:, c, :], sp[:, 10, c:c + 1], sp[:, 10, c:c + 1], ALU.mult, ALU.add
                                      ).then_inc(lru_d.sem, 1)
                dve.wait_ge(*lru_a.at(l, 6))
                dve.tensor_scalar(rec[:, :, :], tn[:, :, :], 1.0, None, ALU.add).then_inc(lru_d.sem, 1)
                dve.wait_ge(*lru_d.at(l, 3))
                dve.reciprocal(rec[:, :, :], rec[:, :, :]).then_inc(lru_d.sem, 1)
                dve.scalar_tensor_tensor(th_i[:, :, :], th_i[:, :, :], 1.0, xc[:, :, :], ALU.add, ALU.mult
                                         ).then_inc(lru_d.sem, 1)
                dve.wait_ge(*lru_d.at(l, 4))
                dve.scalar_tensor_tensor(tn[:, :, :], tn[:, :, :], 2.0, rec[:, :, :], ALU.mult, ALU.mult
                                         ).then_inc(lru_d.sem, 1)
                dve.wait_ge(*pool_ps.at(l, 1))
                for c in range(2):
                    dve.tensor_scalar(pooled[:, c, :], bank[2][:, c * SEQ:c * SEQ + SEQ], pa[:, PS + c:PS + c + 1], None,
                                      ALU.mult).then_inc(pool_ok.sem, 1)
                dve.wait_ge(*pool_ok.at(l, 2))
                for c in range(2):
                    dve.tensor_scalar(yT[:, c, :], pooled[:, c, :], pa[:, OG + c:OG + c + 1], None, ALU.mult
                                      ).then_inc(lru_d.sem, 1)
                dve.wait_ge(*lru_a.at(l, 7))
                dve.memset(tn[:, :, 0:1], 1.0).then_inc(lru_d.sem, 1)
                dve.wait_ge(*lru_d.at(l, 9))
                dve.scalar_tensor_tensor(th_i[:, :, :], th_i[:, :, :], 0.5, tn[:, :, :], ALU.mult, ALU.mult
                                         ).then_inc(lru_d.sem, 1)
                dve.wait_ge(*lru_d.at(l, 10))
                for c in range(2):
                    ins = dve.tensor_tensor_scan(la[:, c, :], ea[:, c, :], th_i[:, c, :], 0.0, ALU.mult, ALU.add)
                ins.then_inc(lru_d.sem, 1)
                dve.wait_ge(*lru_d.at(l, 11))
                dve.wait_ge(*gelu_p.at(l, 5))
                dve.tensor_tensor(xc[:, :, :], la[:, :, :], gl[:, :, :], ALU.mult).then_inc(lru_d.sem, 1)
                dve.wait_ge(*lru_d.at(l, 12))
                for c in range(2):
                    dve.tensor_scalar(yT[:, 2 + c, :], xc[:, c, :], pa[:, OG + 2 + c:OG + 3 + c], None, ALU.mult
                                      ).then_inc(lru_d.sem, 1)

                def masked(h):
                    for t, (a, b) in enumerate(((0, P), (P, KEYS))):
                        if h >= 2 and t == 0:
                            dve.wait_ge(*pt_ps.at(l, h - 1))
                        if t == 0:
                            alone(dve, *s_ps.at(l, h + 1))
                        dve.tensor_tensor_reduce(prob[:, h % 2, a:b], bank[4 + h % 2][:, a:b], mask[:, a:b], -1.0, 3e38,
                                                 ALU.add, ALU.min, nmax[:, 2 * h + t:2 * h + t + 1]).then_inc(s_ok.sem, 1)

                def normalised(h):
                    dve.wait_ge(*e_ok.at(l, 2 * h + 2))
                    dve.reciprocal(rden[:, 2 * h:2 * h + 2], den[:, 2 * h:2 * h + 2]).then_inc(rd_ok.sem, 1)
                    dve.wait_ge(*rd_ok.at(l, h + 1))
                    for t, (a, b) in enumerate(((0, P), (P, KEYS))):
                        ins = dve.tensor_scalar(prob[:, h % 2, a:b], prob[:, h % 2, a:b], rden[:, 2 * h + t:2 * h + t + 1],
                                                None, ALU.mult)
                    ins.then_inc(pn_ok.sem, 1)

                def attention_y(pr):
                    dve.wait_ge(*ysq_at.at(l, pr + 1))
                    dve.tensor_scalar(yT[:, 4 + pr, :], bank[pr % 2][:, 0:SEQ], pa[:, OG + 4 + pr:OG + 5 + pr], None,
                                      ALU.mult).then_inc(o_ok.sem, 1)

                def added(n, grp):
                    t, c = (n // 2) % 2, n % 2
                    dve.wait_ge(*wo_ps.at(l, n + 1))
                    if n >= 4:
                        dve.wait_ge(*wo_ok.at(l, n - 3))
                    xs = x[:, t, c * 512:c * 512 + 512]
                    dve.scalar_tensor_tensor(xs, bank[2 + n % 2][:, :], grs[:, 2 * grp + t:2 * grp + t + 1], xs,
                                             ALU.mult, ALU.add).then_inc(wo_ok.sem, 1)

                for h in range(HEADS + 2):
                    if h < HEADS:
                        masked(h)
                    if h == 1:
                        dve.wait_ge(*st_ps.at(l, 1))
                        dve.tensor_copy(gstat[:, 0:4], bank[0][:, SEQ:SEQ + 4]).then_inc(st_ok.sem, 1)
                    if 1 <= h < HEADS + 1:
                        normalised(h - 1)
                    if h >= 3 and h % 2:
                        attention_y((h - 3) // 2)
                    if h == 2:
                        dve.wait_ge(*gr_ok.at(l, 1))
                    if h >= 2:
                        added(h - 2, 0 if h - 2 < 4 else 1)
                dve.wait_ge(*st_ps.at(l, 2))
                dve.tensor_copy(gstat[:, 4:6], bank[0][:, SEQ:SEQ + 2]).then_inc(st_ok.sem, 1)
                dve.wait_ge(*gr_ok.at(l, 2))
                for n in range(8, 12):
                    added(n, 2)

                normalise(1)
                dve.wait_ge(*pb_in.at(l, 16))
                turned(1, pb[:, G2:G2 + KD])
                for t in range(TT):
                    dve.wait_ge(*x0_ok.at(l, t + 1))
                    dve.tensor_tensor(xs2[:, 1, t, :], xn[:, t, :], xs2[:, 0, t, :], ALU.subtract).then_inc(x1_ok.sem, 1)
                dve.wait_ge(*lgT_ps.at(l, 1))
                dve.tensor_scalar(lgT[0:E, :], bank[4][0:E, 0:SEQ], pb[0:E, RB:RB + 1], None, ALU.add).then_inc(lgT_ok.sem, 1)

                rs = [0]

                def step(ins):
                    ins.then_inc(rt.sem, 1)
                    rs[0] += 1

                def settle():
                    dve.wait_ge(*rt.at(l, rs[0]))
                dve.wait_ge(*lg_ps.at(l, 1))
                step(dve.tensor_copy(lg[:, :, :], bank[5][:, 0:TT * E].rearrange("p (t e) -> p t e", t=TT)))
                alone(dve, *rt.at(l, 1))
                for t in range(TT):
                    step(dve.max(top[:, t, :], lg[:, t, :]))
                alone(dve, *rt.at(l, 3))
                for t in range(TT):
                    step(dve.max_index(tix[:, t, :], top[:, t, :], lg[:, t, :]))
                    step(dve.tensor_scalar(ntop[:, t:t + 1], top[:, t, 0:1], -1.0, None, ALU.mult))
                settle()
                step(dve.tensor_copy(tif[:, :, :], tix[:, :, :]))
                dve.wait_ge(*rt_act.at(l, 2))
                step(dve.reciprocal(rp4[:, :], psum4[:, :]))
                settle()
                for t in range(TT):
                    step(dve.tensor_scalar(ptop[:, t, :], ptop[:, t, :], rp4[:, t:t + 1], None, ALU.mult))
                settle()
                for t in range(TT):
                    for k in range(TOPK):
                        step(dve.tensor_scalar(hot[:, t, k, :], iota_e, tif[:, t, k:k + 1], ptop[:, t, k:k + 1],
                                               ALU.is_equal, ALU.mult))
                settle()
                step(dve.tensor_tensor(hot[:, :, 0:2, :], hot[:, :, 0:2, :], hot[:, :, 2:4, :], ALU.add))
                settle()
                step(dve.tensor_tensor(gates[:, :, :], hot[:, :, 0, :], hot[:, :, 1, :], ALU.add))
                settle()
                dve.tensor_scalar(sel[:, :, :], gates[:, :, :], 0.0, None, ALU.is_gt).then_inc(rk_ok.sem, 1)
                step(dve.tensor_scalar(halfg[:, :, :], gates[:, :, :], 0.5, None, ALU.mult))
                assert rs[0] == ROUTER_STEPS

                def select(quad, par):
                    r = rank[:, :, bass.ds(4 * quad, 4)].unsqueeze(3).broadcast_to([P, TT, 4, CAP])
                    s4 = slots[:, 0:CAP].unsqueeze(1).broadcast_to([P, 4, CAP])
                    dst = sm[:, par].rearrange("p t (e s) -> p t e s", e=4)
                    for t in range(TT):
                        ins = dve.tensor_tensor(dst[:, t], r[:, t], s4, ALU.is_equal)
                    ins.then_inc(sm_ok.sem, 1)

                def spread_gates(quad, par):
                    gq = halfg[:, :, bass.ds(4 * quad, 4)].unsqueeze(3).broadcast_to([P, TT, 4, CAP])
                    src = sm[:, par].bitcast(F32).rearrange("p t (e s) -> p t e s", e=4)
                    dst = gm[:, par].rearrange("p t (e s) -> p t e s", e=4)
                    dve.wait_ge(*sm_ok.at(l, quad + 1))
                    for t in range(TT):
                        ins = dve.tensor_tensor(dst[:, t], src[:, t], gq[:, t], ALU.mult)
                    ins.then_inc(gm_ok.sem, 1)

                def owners(n):
                    dve.tensor_scalar(pick[0:3 * E, :], owner[0:3 * E, :], iota_e[0:3 * E, bass.ds(2 * n, 1)], None,
                                      ALU.is_equal).then_inc(pick_ok.sem, 1)

                def tiles_out(quad, par, c, b=3):
                    dve.wait_ge(*gth_ps.at(l, 4 * quad + c + 1))
                    for dt in range(2):
                        k = 2 * c + dt
                        ins = dve.tensor_scalar(xT[:, par, k, :], bank[b][:, dt * SEQ:dt * SEQ + SEQ],
                                                pb[:, G2 + k:G2 + k + 1], None, ALU.mult)
                    ins.then_inc(xT_dve.sem, 1)

                dve.wait_ge(*rk_ps.at(l, 1))
                dve.scalar_tensor_tensor(rank[:, :, :], bank[6][:, 0:TT * E].rearrange("p (t e) -> p t e", t=TT), 1.0,
                                         sel[:, :, :], ALU.add, ALU.mult).then_inc(rk_ok.sem, 1)
                dve.wait_ge(*rk_ok.at(l, 2))
                select(0, 0)
                dve.tensor_copy(count, bank[6][:, 2 * E:3 * E]).then_inc(rk_ok.sem, 1)
                dve.wait_ge(*gT_ps.at(l, 1))
                dve.tensor_copy(gT[0:E, :], bank[7][0:E, 0:SEQ]).then_inc(gT_ok.sem, 1)
                tiles_out(0, 0, 1, 1)
                owners(0)
                tiles_out(0, 0, 3, 3)
                select(1, 1)
                spread_gates(0, 0)

                def swiglu(p, another=True):
                    dve.wait_ge(*gu_ps.at(l, p.n + 1))
                    dve.wait_ge(*act_ok.at(l, p.n))
                    dve.tensor_scalar(g, bank[0][:, 0:FF], LIMIT, None, ALU.min)
                    dve.tensor_scalar(u, bank[0][:, FF:2 * FF], LIMIT, -LIMIT, ALU.min, ALU.max).then_inc(gu_rd.sem, 1)
                    if another:
                        owners(p.n + 1)
                    dve.wait_ge(*sg_ok.at(l, p.n + 1))
                    dve.scalar_tensor_tensor(th, th, 1.0, g, ALU.add, ALU.mult).then_inc(am_ok.sem, 1)
                    dve.wait_ge(*am_ok.at(l, p.n + 1))
                    dve.wait_ge(*ag_ps.at(l, p.n))
                    dve.scalar_tensor_tensor(act_e, u, 1.0, th, ALU.add, ALU.mult).then_inc(act_ok.sem, 1)

                def homes(p):
                    dve.wait_ge(*ag_ps.at(l, p.n + 1))
                    dve.wait_ge(*acc_ps.at(l, p.n))
                    dve.tensor_scalar(home[:, :], bank[2][:, 0:SEQ], 0.0, None, ALU.is_gt).then_inc(home_ok.sem, 1)

                def down_rest(p):
                    for h in range(2):
                        dve.wait_ge(*y_rd.at(l, 2 * p.n + h + 1))
                        dve.scalar_tensor_tensor(y_lo[h][:, :], bank[1 + h][:, :], gcol[:, 0:1], y_hi[:, h * 512:h * 512 + 512],
                                                 ALU.mult, ALU.subtract).then_inc(ylo_ok.sem, 1)

                def pair_turn(p, before=None, choose=True, spread=True, more=True, another=True):
                    if before:
                        homes(before)
                    swiglu(p, another)
                    if before:
                        down_rest(before)
                    if more:
                        tiles_out(p.quad + 1, 1 - p.par, p.slot + 1)
                    if not p.first and choose:
                        select(p.quad + 2, p.par)
                    if p.first and spread:
                        spread_gates(p.quad + 1, 1 - p.par)

                pair_turn(Pair(0, 0))
                js = [0]

                def listed(ins):
                    ins.then_inc(list_ok.sem, 1)
                    js[0] += 1
                    alone(dve, *list_ok.at(l, js[0]))
                dve.wait_ge(*rk_ok.at(l, 3))
                dve.scalar_tensor_tensor(over_g[:, :, :], rank[:, :, :], CAP + 0.5, gates[:, :, :], ALU.is_gt, ALU.mult)
                listed(dve.tensor_scalar(over, count, CAP + 0.5, None, ALU.is_gt))
                listed(dve.tensor_tensor_scan(place, one_row, over, 0.0, ALU.mult, ALU.add))
                dve.tensor_tensor(over_e, over, iota_e, ALU.mult)
                listed(dve.tensor_tensor(is_job, place.unsqueeze(1).broadcast_to([P, JOBS, E]),
                                         slots[:, 0:JOBS].unsqueeze(2).broadcast_to([P, JOBS, E]), ALU.is_equal))
                listed(dve.tensor_tensor(is_job, is_job, over_e.unsqueeze(1).broadcast_to([P, JOBS, E]), ALU.mult))
                listed(dve.tensor_copy(job_f[:, 1:2], job_f[:, 2:3]))
                listed(dve.tensor_copy(job_f[:, 0:1], by_expert[:, 11, E - 1:E]))
                listed(dve.tensor_tensor(job_f[:, 2:3], job_f[:, 1:2], job_f[:, 0:1], ALU.add))
                listed(dve.tensor_reduce(job_f[:, 3:3 + JOBS], is_job, AX.X, ALU.add))
                listed(dve.tensor_copy(job[:, :], job_f[:, :]))

                with dve.Fori(0, PAIRS // 4 - 1) as i:
                    for n in range(4):
                        pair_turn(Pair(i, n + 1), Pair(i, n))
                for n in range(PAIRS - 3, PAIRS):
                    pair_turn(Pair(0, n), Pair(0, n - 1), choose=False, spread=False, more=n < PAIRS - 2, another=n < PAIRS - 1)
                homes(Pair(0, PAIRS - 1))
                down_rest(Pair(0, PAIRS - 1))
                dve.wait_ge(*acc_ps.at(l, PAIRS))
                for t in range(TT):
                    for h in range(2):
                        xs = x[:, t, h * 512:h * 512 + 512]
                        dve.tensor_tensor(xs, bank[4 + 2 * t + h][:, :], xs, ALU.add).then_inc(x_ok.sem, 1)
                number, seen = entry(dve, 0, JOBS), entry(dve, 1, DEPTH * JOBS)

                def expert_job(j):
                    e = entry(dve, 3 + j, E - 1)
                    n = seen + j
                    dve.wait_ge(*job_gu.at(n, 1))
                    for f in range(2):
                        ins = dve.tensor_scalar(jg[:, f, :], bank[0][:, f * SEQ:f * SEQ + SEQ],
                                                pb[:, bass.ds(BGU + e * 4 + f, 1)], LIMIT, ALU.add, ALU.min)
                    ins.then_inc(job_step.sem, 1)
                    dve.wait_ge(*job_gu.at(n, 2))
                    for f in range(2):
                        ins = dve.tensor_scalar(ju[:, f, :], bank[3][:, f * SEQ:f * SEQ + SEQ],
                                                pb[:, bass.ds(BGU + e * 4 + 2 + f, 1)], LIMIT, ALU.add, ALU.min)
                    ins.then_inc(job_step.sem, 1)
                    dve.wait_ge(*job_step.at(n, 2))
                    dve.tensor_scalar(ju, ju, -LIMIT, 1.0, ALU.max, ALU.add).then_inc(job_step.sem, 1)
                    dve.wait_ge(*job_th.at(n, 1))
                    dve.scalar_tensor_tensor(jth, jth, 1.0, jg, ALU.add, ALU.mult).then_inc(job_step.sem, 1)
                    dve.wait_ge(*job_step.at(n, 4))
                    dve.wait_ge(*job_dn.at(n, 0))
                    dve.scalar_tensor_tensor(jact, jth, 0.5, ju, ALU.mult, ALU.mult).then_inc(job_step.sem, 1)
                    dve.wait_ge(*x_ok.at(l, 4))
                    dve.wait_ge(*job_x.at(n, 0))
                    for t in range(TT):
                        for h in range(2):
                            dve.wait_ge(*job_dn.at(n, 2 * t + h + 1))
                            xs = x[:, t, h * 512:h * 512 + 512]
                            dve.scalar_tensor_tensor(xs, bank[4 + 2 * t + h][:, :], over_g[:, t, bass.ds(e, 1)], xs,
                                                     ALU.mult, ALU.add).then_inc(job_x.sem, 1)
                for_jobs(dve, number, expert_job)

        @block.scalar
        def _(act):
            for c in (ag_ok, gc_ok, y_rd):
                act.sem_inc(c.sem, 1)
            act.wait_ge(once.sem, 48)
            with act.Fori(0, DEPTH) as l:
                def squares(c):
                    for t in range(TT):
                        if c:
                            act.wait_ge(*wo_ok.at(l, 10 + 2 * t))
                        act.activation(xn[:, t, :], x[:, t, :], ACT.Square, accum_out=ms[:, 2 * c + t:2 * c + t + 1]
                                       ).then_inc(ms_ok.sem, 1)

                def turned(c, gain):
                    for b in (0, 2):
                        act.wait_ge(*tr_ok.at(l, 4 * c + b + 1))
                        for dt in range(2):
                            k = 2 * b + dt
                            act.activation(hT[:, k, :], bank[b][:, dt * SEQ:dt * SEQ + SEQ], ACT.Copy,
                                           scale=gain[:, k:k + 1]).then_inc(hT_act.sem, 1)

                act.wait_ge(*x_ok.at(l, 0))
                squares(0)
                act.wait_ge(*pa_in.at(l, 16))
                turned(0, pa[:, G1:G1 + KD])
                act.wait_ge(*sp_dve.at(l, 2))
                act.activation(sp[:, 2, :], sp[:, 1, :], ACT.Exp, scale=-1.0).then_inc(sp_act.sem, 1)
                for w in range(4):
                    act.wait_ge(*proj_ok.at(l, w + 1))
                    if w:
                        act.wait_ge(*hsum_ok.at(l, w))
                    act.activation(sq[:, :], bank[4 + w][:, :], ACT.Square).then_inc(sq_ok.sem, 1)
                for n, dst in enumerate((up[:, :, CONV - 1:], gt[:, :, :], pp[:, :, PAD:])):
                    act.wait_ge(*proj_ok.at(l, 5 + n))
                    act.copy(dst, bank[n][:, :].rearrange("p (c s) -> p c s", c=2)).then_inc(proj_free.sem, 1)
                for w in (0, 2):
                    act.wait_ge(*qkT_ps.at(l, w + 1))
                    act.copy(qkT[:, w // 2, :, 0:P], bank[4 + w][:, :].rearrange("p (c s) -> p c s", c=4)
                             ).then_inc(qkT_ok.sem, 1)
                act.wait_ge(*proj_ok.at(l, 8))
                act.copy(vt[:, 0, :], bank[3][:, :]).then_inc(proj_free.sem, 1)
                for b, dst in enumerate((th_r, th_i)):
                    act.wait_ge(*lru_ps.at(l, b + 1))
                    if b == 0:
                        act.wait_ge(*sp_dve.at(l, 3))
                    for c in range(2):
                        act.activation(dst[:, c, :], bank[b][:, c * SEQ:c * SEQ + SEQ], ACT.Tanh,
                                       bias=hb[:, 2 * b + c:2 * b + c + 1], scale=0.5).then_inc(lru_a.sem, 1)
                act.wait_ge(*lru_d.at(l, 2))
                act.activation(ea[:, :, :], la[:, :, :], ACT.Exp).then_inc(lru_a.sem, 1)
                act.activation(tn[:, :, :], la[:, :, :], ACT.Tanh, scale=-1.0).then_inc(lru_a.sem, 1)
                act.wait_ge(*gelu_p.at(l, 3))
                act.activation(gl[:, :, :], gl[:, :, :], ACT.Tanh, scale=0.7978845608028654).then_inc(gelu_a.sem, 1)
                act.wait_ge(*lru_d.at(l, 6))
                act.activation(tn[:, :, :], tn[:, :, :], ACT.Sqrt).then_inc(lru_a.sem, 1)
                act.wait_ge(*proj_ok.at(l, 9))
                act.copy(vt[:, 1, :], bank[3][:, :]).then_inc(proj_free.sem, 1)

                for h in range(HEADS + 2):
                    if h < HEADS:
                        for t, (a, b) in enumerate(((0, P), (P, KEYS))):
                            act.wait_ge(*s_ok.at(l, 2 * h + t + 1))
                            act.activation(prob[:, h % 2, a:b], prob[:, h % 2, a:b], ACT.Exp,
                                           bias=nmax[:, 2 * h + t:2 * h + t + 1], scale=-1.0,
                                           accum_out=den[:, 2 * h + t:2 * h + t + 1]).then_inc(e_ok.sem, 1)
                    if 1 <= h < HEADS + 1:
                        act.wait_ge(*pt_ps.at(l, h))
                        act.copy(probT[:, (h - 1) % 2, :], bank[6 + (h - 1) % 2][:, 0:KEYS]).then_inc(pt_ok.sem, 1)
                    if h >= 3 and h % 2:
                        pr = (h - 3) // 2
                        act.wait_ge(*o_ps.at(l, pr + 1))
                        act.activation(ysq[:, 4 + pr, :], bank[pr % 2][:, 0:SEQ], ACT.Square).then_inc(ysq_at.sem, 1)

                squares(1)
                act.wait_ge(*pb_in.at(l, 16))
                turned(1, pb[:, G2:G2 + KD])
                for t in range(TT):
                    act.wait_ge(*xn_ok.at(l, 3 + t))
                    act.copy(xs2[:, 0, t, :], xn[:, t, :]).then_inc(x0_ok.sem, 1)
                act.wait_ge(*rt.at(l, 7))
                for t in range(TT):
                    act.activation(ptop[:, t, :], top[:, t, 0:TOPK], ACT.Exp, bias=ntop[:, t:t + 1],
                                   accum_out=psum4[:, t:t + 1]).then_inc(rt_act.sem, 1)

                def tiles_out(quad, par, c, b=3):
                    act.wait_ge(*gth_ps.at(l, 4 * quad + c + 1))
                    for dt in range(2):
                        k = 2 * c + dt
                        ins = act.activation(xT[:, par, k, :], bank[b][:, dt * SEQ:dt * SEQ + SEQ], ACT.Copy,
                                             scale=pb[:, G2 + k:G2 + k + 1])
                    ins.then_inc(xT_act.sem, 1)

                def turned_out(p):
                    act.wait_ge(*ag_ps.at(l, p.n + 1))
                    act.wait_ge(*dn_ps.at(l, 2 * p.n))
                    act.copy(ag[:, :, :], bank[1][:, 0:SEQ].rearrange("p (n s) -> p n s", n=2)).then_inc(ag_ok.sem, 1)
                    act.wait_ge(*ylo_ok.at(l, 2 * p.n))
                    act.wait_ge(*gc_ok.at(l, p.n))
                    act.wait_ge(*home_ok.at(l, p.n + 1))
                    act.activation(g_dump, bank[2][:, 0:SEQ], ACT.Copy, accum_out=gcol[:, 0:1]).then_inc(gc_ok.sem, 1)

                def tanh(p):
                    act.wait_ge(*gu_rd.at(l, p.n + 1))
                    act.wait_ge(*act_ok.at(l, p.n))
                    act.activation(th, g, ACT.Tanh, scale=0.5 * ALPHA).then_inc(sg_ok.sem, 1)

                def down_out(p):
                    for h in range(2):
                        act.wait_ge(*dn_ps.at(l, 2 * p.n + h + 1))
                        if h == 0:
                            act.wait_ge(*gc_ok.at(l, p.n + 1))
                            act.wait_ge(*acc_ps.at(l, p.n))
                        act.activation(y_hi[:, h * 512:h * 512 + 512], bank[1 + h][:, :], ACT.Copy, scale=gcol[:, 0:1]
                                       ).then_inc(y_rd.sem, 1)

                tiles_out(0, 0, 0, 0)
                tiles_out(0, 0, 2, 2)

                def pair_turn(p, before, more=True):
                    if before:
                        turned_out(before)
                    tanh(p)
                    if more:
                        tiles_out(p.quad + 1, 1 - p.par, p.slot)
                    if before:
                        down_out(before)
                pair_turn(Pair(0, 0), None)
                with act.Fori(0, PAIRS // 4 - 1) as i:
                    for n in range(4):
                        pair_turn(Pair(i, n + 1), Pair(i, n))
                for n in range(PAIRS - 3, PAIRS):
                    pair_turn(Pair(0, n), Pair(0, n - 1), more=n < PAIRS - 2)
                turned_out(Pair(0, PAIRS - 1))
                down_out(Pair(0, PAIRS - 1))

                alone(act, *list_ok.at(l, 9))
                number, seen = entry(act, 0, JOBS), entry(act, 1, DEPTH * JOBS)

                def expert_job(j):
                    act.wait_ge(*job_step.at(seen + j, 1))
                    act.activation(jth, jg, ACT.Tanh, scale=0.5 * ALPHA).then_inc(job_th.sem, 1)
                for_jobs(act, number, expert_job)
                alone(act, *job_x.at(seen + number, 0))

        @block.gpsimd
        def _(pool):
            pool.wait_ge(once.sem, 48)
            pool.wait_ge(zeroed.sem, 2)
            with pool.Fori(0, DEPTH) as l:
                def inverse_roots(dst, src, n, scale, after, mid, ok, k):
                    alone(pool, *after)
                    pool.tensor_scalar(dst, src, scale, EPS, ALU.mult, ALU.add).then_inc(mid.sem, 1)
                    pool.wait_ge(*mid.at(l, k))
                    pool.tensor_tensor(dst, dst, half[:, 0:n], ALU.pow).then_inc(ok.sem, 1)

                def token_roots(c):
                    for t in range(TT):
                        a = 2 * c + t
                        inverse_roots(rstd[:, a:a + 1], ms[:, a:a + 1], 1, 1.0 / D, ms_ok.at(l, a + 1), rstd_mid, rstd_ok, a + 1)
                token_roots(0)
                for w in range(4):
                    inverse_roots(hs[:, w, 8:16], hs[:, w, 0:8], 8, 1.0 / DH, hsum_ok.at(l, w + 1), hr_mid, hr_ok, w + 1)

                pool.wait_ge(*proj_free.at(l, 2))
                pool.tensor_tensor(gl[:, :, :], gt[:, :, :], gt[:, :, :], ALU.mult).then_inc(gelu_p.sem, 1)
                alone(pool, *gelu_p.at(l, 1))
                pool.tensor_scalar(gl[:, :, :], gl[:, :, :], 0.044715, 1.0, ALU.mult, ALU.add).then_inc(gelu_p.sem, 1)
                pool.wait_ge(*gelu_p.at(l, 2))
                pool.tensor_tensor(gl[:, :, :], gl[:, :, :], gt[:, :, :], ALU.mult).then_inc(gelu_p.sem, 1)

                pool.wait_ge(*proj_free.at(l, 3))
                N = PAD + SEQ
                steps = [0]

                def turn(out_, in0, in1, op):
                    pool.tensor_tensor(out_, in0, in1, op).then_inc(pool_p.sem, 1)
                    steps[0] += 1
                    pool.wait_ge(*pool_p.at(l, steps[0]))
                turn(p2[:, :, 1:N], pp[:, :, 1:N], pp[:, :, 0:N - 1], ALU.add)
                turn(p4[:, :, 3:N], p2[:, :, 3:N], p2[:, :, 1:N - 2], ALU.add)
                pool.wait_ge(*rope.at(l, 24))
                turn(pooled[0:64, 0, :], p2[0:64, 0, PAD:], invc[0:64, 0, :], ALU.mult)
                turn(pooled[64:P, 0, :], p4[64:P, 0, PAD:], invc[64:P, 0, :], ALU.mult)
                turn(p2[:, 1, 7:N], p4[:, 1, 7:N], p4[:, 1, 3:N - 4], ALU.add)
                turn(pooled[0:64, 1, :], p2[0:64, 1, PAD:], invc[0:64, 1, :], ALU.mult)
                turn(p4[64:P, 1, PAD:N], p2[64:P, 1, PAD:N], p2[64:P, 1, PAD - 8:N - 8], ALU.add)
                turn(pooled[64:P, 1, :], p4[64:P, 1, PAD:], invc[64:P, 1, :], ALU.mult)
                turn(pooled[:, :, :], pooled[:, :, :], pp[:, :, PAD:], ALU.subtract)

                alone(pool, *gelu_a.at(l, 1))
                pool.tensor_scalar(gl[:, :, :], gl[:, :, :], 0.5, 0.5, ALU.mult, ALU.add).then_inc(gelu_p.sem, 1)
                pool.wait_ge(*gelu_p.at(l, 4))
                pool.tensor_tensor(gl[:, :, :], gl[:, :, :], gt[:, :, :], ALU.mult).then_inc(gelu_p.sem, 1)
                pool.wait_ge(*pool_ok.at(l, 2))
                pool.tensor_tensor(ysq[:, 0:2, :], pooled[:, :, :], pooled[:, :, :], ALU.mult).then_inc(ysq_pl.sem, 2)
                pool.wait_ge(*lru_d.at(l, 12))
                pool.tensor_tensor(ysq[:, 2:4, :], xc[:, :, :], xc[:, :, :], ALU.mult).then_inc(ysq_pl.sem, 2)
                inverse_roots(grs[:, 0:4], gstat[:, 0:4], 4, 1.0 / 256, st_ok.at(l, 1), gr_mid, gr_ok, 1)
                inverse_roots(grs[:, 4:6], gstat[:, 4:6], 2, 1.0 / ATT, st_ok.at(l, 2), gr_mid, gr_ok, 2)
                token_roots(1)
                b_0, b_1 = (ysq[:, n, :].bitcast(BF16) for n in range(2))
                w = slice(0, 3 * E)
                alone(pool, *bsrc_in.at(l, 16))
                pool.tensor_copy(b_0[w, :], b_src[w, :]).then_inc(brow_ok.sem, 1)
                pool.wait_ge(*brow_ok.at(l, 1))
                pool.tensor_tensor(b_rest[w, :], b_src[w, :], b_0[w, :], ALU.subtract).then_inc(brow_ok.sem, 1)
                alone(pool, *brow_ok.at(l, 2))
                pool.tensor_copy(b_1[w, :], b_rest[w, :]).then_inc(brow_ok.sem, 1)
                alone(pool, *brow_ok.at(l, 3))
                pool.tensor_copy(b_rows[0:E, :], b_0[0:E, :]).then_inc(brow_ok.sem, 1)
                alone(pool, *brow_ok.at(l, 4))
                pool.tensor_copy(b_rows[E:2 * E, :], b_1[E:2 * E, :]).then_inc(brow_ok.sem, 1)
                pool.wait_ge(*brow_ok.at(l, 5))
                pool.tensor_tensor(b_rows[2 * E:3 * E, :], b_rest[2 * E:3 * E, :], b_1[2 * E:3 * E, :], ALU.subtract
                                   ).then_inc(brow_ok.sem, 1)


def kernel(x, norm1_g, w_in, pool_w, pool_scale, conv_w, conv_b, lru_wa, lru_ba, lru_wx, lru_bx, lru_lambda,
           q_norm_g, k_norm_g, out_norm_g, w_out, norm2_g, router_w, router_b, w_gate_up, b_gate_up, w_down, b_down):
    import ml_dtypes
    import numpy as np
    import concourse.bacc as bacc
    from concourse.bass_utils import run_bass_kernel_spmd

    A = np.asarray

    def columns(a, n):
        a = A(a).reshape(DEPTH, -1, n, P)
        return a.transpose(0, 3, 1, 2).reshape(DEPTH, P, -1)

    def block_diagonal(w):
        m = np.zeros((DEPTH, P, 2, P), np.float32)
        for b in range(4):
            r = slice(64 * (b % 2), 64 * (b % 2) + 64)
            m[:, r, b // 2, r] = A(w)[:, b]
        return m.reshape(DEPTH, P, 2 * P)

    def spread(a):
        return np.broadcast_to(A(a)[:, None, :], (DEPTH, P, a.shape[-1]))

    small_a = np.concatenate([
        columns(norm1_g, 8), columns(out_norm_g, 8), columns(pool_scale, 2), columns(conv_w, 2), columns(conv_b, 2),
        columns(lru_ba, 2), columns(lru_bx, 2), columns(lru_lambda, 2), block_diagonal(lru_wa), block_diagonal(lru_wx),
        block_diagonal(pool_w), spread(q_norm_g), spread(k_norm_g)], axis=2)
    rw = A(router_w).reshape(DEPTH, KD, P, E).transpose(0, 2, 1, 3).reshape(DEPTH, P, KD * E)
    bgu = A(b_gate_up).reshape(DEPTH, E, 4, P).transpose(0, 3, 1, 2).reshape(DEPTH, P, E * 4)
    rb = np.zeros((DEPTH, P, 1), np.float32)
    rb[:, 0:E, 0] = A(router_b)
    small_b = np.concatenate([columns(norm2_g, 8), rw, bgu, rb], axis=2)
    w_in_p = A(w_in).reshape(DEPTH, KD, P, IN_W).transpose(0, 2, 1, 3)
    w_out_p = A(w_out).reshape(DEPTH, KD, P, D).transpose(0, 2, 1, 3)
    gu = A(w_gate_up).reshape(DEPTH * E, KD, P, 2 * FF).transpose(0, 2, 1, 3).reshape(DEPTH * E, P, GU)
    dn = A(w_down).reshape(DEPTH * E, 2, P, D).transpose(0, 2, 1, 3).reshape(DEPTH * E, P, DN)
    experts = np.concatenate([gu, dn], axis=2)

    pos = np.arange(SEQ, dtype=np.float32)
    inv_freq = (np.float32(10000.0) ** (-np.arange(0, DH, 2, dtype=np.float32) / np.float32(DH))).astype(np.float32)
    ang = (pos[:, None] * inv_freq[None, :]).astype(np.float32)
    cos = np.concatenate([np.cos(ang), np.cos(ang)], axis=1)
    sin = np.concatenate([-np.sin(ang), np.sin(ang)], axis=1)

    def by_token(a):
        return a.reshape(TT, P, -1).transpose(1, 0, 2).reshape(P, -1)
    dist = np.arange(SEQ)[:, None] - np.arange(SEQ)[None, :]
    seen = (dist >= 0) * ((dist <= 128).astype(np.float64) + (dist % 4 == 0) + (dist % 16 == 0))
    bias = np.where(seen > 0, np.log(np.maximum(seen, 1.0)), -1e30)
    windows = np.array([[2, 4], [8, 16]])
    length = np.minimum(np.arange(1, SEQ + 1)[None, None, :], np.repeat(windows, 64, axis=1)[:, :, None])
    consts = np.concatenate([
        np.eye(P), by_token(cos), by_token(sin), bias[0:P, 0:P], bias[P:SEQ, :],
        (1.0 / length).transpose(1, 0, 2).reshape(P, -1), np.broadcast_to(np.arange(E), (P, E)),
        np.full((P, 16), -0.5), np.ones((P, 1)), np.broadcast_to(np.arange(1, P + 1), (P, P)),
        np.arange(P)[:, None] % E - (np.arange(P)[None, :] >= CAP), np.ones((P, E))], axis=1).astype(np.float32)
    consts_b = np.concatenate([np.triu(np.ones((P, P)), 1), np.ones((P, P))], axis=1).astype(ml_dtypes.bfloat16)

    arrays = {
        "x_in": A(x).reshape(TT, P, D).transpose(1, 0, 2), "small_a": small_a, "small_b": small_b, "w_in": w_in_p.reshape(DEPTH, P, -1),
        "w_out": w_out_p.reshape(DEPTH, P, -1), "experts": experts,
        "b_gate_up": np.concatenate([A(b_gate_up)] * 3, axis=1), "b_down": A(b_down), "consts": consts, "consts_b": consts_b,
    }
    arrays = {k: np.ascontiguousarray(v) for k, v in arrays.items()}
    nc = bacc.Bacc("TRN2", target_bir_lowering=False, num_devices=1)
    args = [nc.dram_tensor(k, v.shape, mybir.dt.from_np(v.dtype), kind="ExternalInput").ap() for k, v in arrays.items()]
    out = nc.dram_tensor("out", (P, TT, D), F32, kind="ExternalOutput").ap()
    build(nc, *args, out)
    r = run_bass_kernel_spmd(nc, [arrays], core_ids=[0])
    return r.results[0]["out"].transpose(1, 0, 2).reshape(1, SEQ, D)
```

```python
from contextlib import ExitStack

import concourse.bass as bass
from concourse import mybir

P = 128
F32 = mybir.dt.float32
BF16 = mybir.dt.bfloat16
F32R = mybir.dt.float32r
U32 = mybir.dt.uint32
I32 = mybir.dt.int32
ALU = mybir.AluOpType
ACT = mybir.ActivationFunctionType
AX = mybir.AxisListType

DEPTH, SEQ, D = 2, 256, 1024
TT = SEQ // P
KD = D // P
IN_W = 2304
HEADS, DH = 8, 64
ATT = HEADS * DH
E, FF, TOPK = 32, 256, 4
CONV = 4
PAD = 16
KEYS = P + 2 * P
EPS = 1e-6
LIMIT, ALPHA = 7.0, 1.702
GU = KD * 2 * FF
DN = (FF // P) * D
SLOT = GU + DN
RING = 4
G1, OG, PS, CW, CB, BA, BX, LAM, BD, QG, KG = 0, 8, 16, 18, 26, 28, 30, 32, 34, 802, 866
NA = 930
G2, RW, RB = 0, 8, 264
NB = 265
CAP = 64
PAIRS, QUADS = E // 2, E // 4
JOBS = SEQ * TOPK // (CAP + 1)
ROUTER_STEPS = 15
LIST_STEPS = 20
ATANH_TERMS = 9


class Counter:

    def __init__(self, sem, per, base=0):
        self.sem, self.per, self.base = sem, per, base

    def at(self, layer, k):
        return self.sem, layer * self.per + k + self.base


class Pair:

    def __init__(self, i, off):
        self.n, self.quad, self.place = 4 * i + off, 2 * i + off // 2, off % 4
        self.first = off % 2 == 0
        self.par = off // 2 % 2
        self.slot = 2 * (off % 2)


def build(nc, x_in, small_a, small_b, w_in, w_out, experts, b_gate_up, b_down, consts, consts_b, out):
    with ExitStack() as ctx:
        def sb(name, *shape, dt=F32):
            return ctx.enter_context(nc.sbuf_tensor(name, [P, *shape], dt))

        def counter(name, per, base=0):
            return Counter(ctx.enter_context(nc.semaphore(name)), per, base)

        bank = [ctx.enter_context(nc.psum_tensor(f"bank{i}", [P, 512], F32)) for i in range(8)]

        x = sb("x", TT, D)
        ring = sb("ring", RING, SLOT)
        with ExitStack() as mixing:
            def shared(name, *shape):
                return mixing.enter_context(nc.sbuf_tensor(name, [P, *shape], F32))
            mixed = shared("mixed", 4096)
            vt = shared("vt", TT, ATT)
            gt = shared("gt", 2, SEQ)
            area = shared("area", KD * D)
        rot = mixed[:, 0:2048].rearrange("p (n t d) -> p n t d", n=2, t=TT)
        qkT = mixed[:, 2048:4096].rearrange("p (n c s) -> p n c s", n=2, c=4)
        wout = area[:, :].rearrange("p (k c) -> p k c", k=KD)
        xs2 = sb("token_parts", 2, TT, D, dt=F32R)
        sm = sb("selection", 2, TT, SEQ, dt=F32R)
        y_lo1 = sb("down_rest_b", FF * 2, dt=F32R)
        tokens = sb("tokens", 4 * D)
        xn = tokens[:, 0:TT * D].rearrange("p (t d) -> p t d", t=TT)
        xT = tokens[:, :].rearrange("p (q k s) -> p q k s", q=2, k=KD)
        xT_job = tokens[:, 0:KD * P].rearrange("p (k s) -> p k s", k=KD)
        y_hi = sb("down_part", D, dt=F32R)
        gm = sb("gates_by_slot", 2, TT, SEQ)
        ag = sb("act_turned", 2, P)
        home = sb("slot_home", SEQ, dt=F32R)
        y_lo = [sb("down_rest_a", FF * 2, dt=F32R), y_lo1]
        units = sb("units", 4 * FF)
        b_src, b_rest = units[:, 0:2 * FF], units[:, 2 * FF:4 * FF]
        g, u, th, act_e = (units[:, FF * n:FF * n + FF] for n in range(4))
        cst = sb("cst", consts.shape[1])
        cstb = sb("cstb", consts_b.shape[1], dt=BF16)
        pa = sb("pa", NA)
        pb = sb("pb", NB)
        ysq = sb("ysq", KD, SEQ)
        hT = sb("hT", KD, SEQ)
        yT = hT
        gcol = sb("gcol", 1)
        ms = sb("ms", 8)
        rstd = sb("rstd", 8)
        tmp = sb("tmp", ATT)
        b_rows = ysq[:, 2, :].bitcast(BF16)
        pick = ysq[:, 3, 0:P // 2].bitcast(BF16)
        job_pick = ysq[:, 3, P // 2:P].bitcast(BF16)
        cg = sb("cg", 2, 2, TT, DH)
        hs = sb("hs", 4, 16)
        probs = sb("probs", 4, KEYS)
        prob, probT = probs[:, 0:2, :], probs[:, 2:4, :]
        before = probs[:, :, :].rearrange("p a b -> p (a b)")
        sq, swp = before[:, 0:ATT], before[:, ATT:2 * ATT]
        nmax = sb("nmax", 16)
        den = sb("den", 16)
        rden = sb("rden", 16)
        gstat = sb("gstat", 8)
        grs = sb("grs", 8)
        up = sb("up", 2, CONV - 1 + SEQ)
        gl = sb("gl", 2, SEQ)
        hb = sb("hb", 4)
        sp = sb("sp", 12, 2)
        pp = sb("pp", 2, PAD + SEQ)
        ps = sb("ps", 2, 2, PAD + SEQ)
        p2, p4 = ps[:, 0], ps[:, 1]
        pooled = cg[:, :, :, :, :].rearrange("p a b t d -> p (a b t d)").rearrange("p (c s) -> p c s", c=2)

        def two(ap):
            return ap.rearrange("p (c s) -> p c s", c=2)
        th_r, th_i, la, tn = (two(rot[:, n, t, :]) for n in range(2) for t in range(TT))
        ea = th_r
        xc = two(tmp[:, :])
        rec = two(vt[:, 1, :])
        g_dump = up[:, 0, CONV - 1:]
        pflat = ps[:, :, :, :].rearrange("p a b c -> p (a b c)")
        lgT = pflat[:, 0:SEQ]
        gT = pflat[:, SEQ:2 * SEQ]
        hot = pflat[:, 2 * SEQ:2 * SEQ + TT * TOPK * E].rearrange("p (t k e) -> p t k e", t=TT, k=TOPK)
        bdn = probs[:, :, :].rearrange("p a b -> p (a b)")[:, 0:D]
        top = sb("top", TT, 8)
        tix = sb("tix", TT, 8, dt=U32)
        tif = sb("tif", TT, 8)
        ntop = sb("ntop", TT)
        ptop = sb("ptop", TT, TOPK)
        psum4 = sb("psum4", TT)
        rp4 = sb("rp4", TT)
        by_expert = gl[:, :, :].rearrange("p a (b e) -> p (a b) e", e=E)
        gates, halfg, rank = (by_expert[:, TT * n:TT * n + TT, :] for n in range(3))
        sel = by_expert[:, 8, :].bitcast(BF16).rearrange("p (t e) -> p t e", t=TT)
        count, over, over2, place, first, second = (by_expert[:, n, :] for n in (9, 10, 12, 11, 6, 7))
        lg = by_expert[:, 13:15, :]
        job_f = sb("job_f", 3 + 2 * JOBS)
        job = sb("job", 3 + JOBS, dt=I32)
        is_job = tmp[:, 0:JOBS * E].rearrange("p (j e) -> p j e", j=JOBS)

        ident = cst[:, 0:128]
        cos_t = cst[:, 128:256].rearrange("p (t d) -> p t d", t=TT)
        sin_t = cst[:, 256:384].rearrange("p (t d) -> p t d", t=TT)
        mask = cst[:, 384:768]
        invc = cst[:, 768:1280].rearrange("p (t s) -> p t s", t=2)
        iota_e = cst[:, 1280:1312]
        half = cst[:, 1312:1328]
        ones = cst[:, 1328:1329]
        slots = cst[:, 1329:1329 + P]
        owner = cst[:, 1457:1457 + P]
        one_row = cst[:, 1585:1585 + E]
        before_b, all_b = cstb[:, 0:P], cstb[:, P:2 * P]
        win = ring[:, 1:4, :].rearrange("p r c -> p (r c)").rearrange("p (k c) -> p k c", k=KD)

        passed = counter("waits_passed", 0)
        x_landed, once, zeroed = counter("x_landed", 0), counter("constants_landed", 0), counter("pads_zeroed", 0)
        pa_in, pb_in = counter("params_a_landed", 16), counter("params_b_landed", 16)
        bdn_in = counter("b_down_landed", 16)
        win_in = [counter(f"w_in_{n}_landed", 16) for n in range(3)]
        wout_in = counter("w_out_landed", 16)
        up_in = [counter(f"gate_up_slot{j}_landed", 16 * (E // RING)) for j in range(RING)]
        early_in = [counter(f"half_gate_up_slot{j}_landed", 16) for j in range(2)]
        gu_half = counter("half_gate_up_used", 1)
        down_in = [counter(f"down_slot{j}_landed", 16 * (E // RING)) for j in range(RING)]
        ms_ok = counter("squares_summed", 4)
        rstd_ok = counter("rstd_ready", 4)
        rstd_mid = counter("rstd_half", 4)
        xn_ok = counter("tokens_normalised", 4)
        tr_ok = counter("h_transposed", 8)
        hT_act, hT_dve = counter("hT_by_act", 8), counter("hT_by_dve", 8)
        proj_ok = counter("projected", 9)
        proj_free = counter("projection_copied", 5)
        sq_ok = counter("qk_squared", 4)
        hsum_ok = counter("qk_head_sums", 4)
        hr_mid, hr_ok = counter("qk_rstd_half", 4), counter("qk_rstd_ready", 4)
        rope = counter("rope_steps", 24)
        qkT_ps, qkT_ok = counter("qk_transposed", 4), counter("qkT_ready", 4)
        sp_dve, sp_act = counter("softplus_steps", 19), counter("softplus_exp", 1)
        conv_ok = counter("conv_steps", 8)
        lru_ps = counter("lru_gates_product", 2)
        lru_a = counter("lru_activations", 7)
        lru_d = counter("lru_steps", 14)
        gelu_p, gelu_a = counter("gelu_steps", 5), counter("gelu_tanh", 1)
        pool_p, pool_ps, pool_ok = counter("pool_steps", 9), counter("pool_product", 1), counter("pool_out", 2)
        ysq_pl, ysq_at = counter("y_squares", 4), counter("attention_squares", 4)
        st_ps, st_ok = counter("group_sums", 2), counter("group_sums_copied", 2)
        gr_mid, gr_ok = counter("group_rstd_half", 2), counter("group_rstd_ready", 2)
        s_ps, s_ok, e_ok = counter("scores", 8), counter("scores_masked", 16), counter("exp_done", 16)
        rd_ok, pn_ok = counter("den_reciprocal", 8), counter("probs_normalised", 8)
        pt_ps, pt_ok = counter("probs_transposed", 8), counter("probsT_copied", 8)
        o_ps, o_ok = counter("attention_out", 4), counter("attention_yT", 4)
        wo_ps, wo_ok = counter("w_out_product", 12), counter("w_out_added", 12)
        lgT_ps, lgT_ok = counter("logitsT", 1), counter("logitsT_copied", 1)
        lg_ps, rt = counter("logits", 1), counter("router_steps", ROUTER_STEPS)
        rt_act = counter("router_exp", 2)
        gT_ps, gT_ok = counter("gates_transposed", 1), counter("gatesT_copied", 1)
        x0_ok, x1_ok = counter("x_first_part", 2), counter("x_second_part", 2)
        bsrc_in, brow_ok = counter("b_gate_up_landed", 16), counter("bias_rows_steps", 6)
        rk_ps, rk_ok = counter("ranks_product", 1), counter("ranks_steps", 3)
        sm_ok, gm_ok = counter("selection_built", QUADS), counter("gates_spread", QUADS)
        pick_ok = counter("owners_built", PAIRS)
        gth_ps = counter("tokens_gathered", 4 * QUADS)
        xT_dve, xT_act = counter("xT_by_dve", 2 * QUADS), counter("xT_by_act", 2 * QUADS)
        gu_ps, gu_rd = counter("gate_up_product", PAIRS), counter("gate_up_read", PAIRS, base=1)
        sg_ok, am_ok, act_ok = counter("tanh_done", PAIRS), counter("swiglu_half", PAIRS), counter("swiglu_done", PAIRS, base=1)
        ag_ps, ag_ok = counter("act_turned", PAIRS), counter("act_turned_copied", PAIRS, base=1)
        gc_ok, home_ok = counter("slot_gates", PAIRS, base=1), counter("slot_homes", PAIRS, base=1)
        ylo_ok = counter("down_second_part", 2 * PAIRS, base=1)
        dn_ps, y_rd = counter("down_product", 2 * PAIRS, base=3), counter("down_first_part", 2 * PAIRS, base=1)
        acc_ps, x_ok = counter("combined", PAIRS, base=1), counter("x_added", 4, base=3)
        list_ok = counter("job_list_steps", LIST_STEPS)
        job_in, job_down_in = counter("job_gate_up_landed", 16), counter("job_down_landed", 16)
        job_sm, job_gth = counter("job_selection_built", 1), counter("job_tokens_gathered", 4)
        job_xa, job_xd = counter("job_xT_by_act", 2), counter("job_xT_by_dve", 2)
        job_gu, job_step, job_th = counter("job_gate_up_product", 1, base=1), counter("job_swiglu_steps", 3, base=1), counter("job_tanh_done", 1)
        job_tr, job_ag, job_home, job_gc = (counter("job_turned", 1, base=1), counter("job_turned_copied", 1),
                                            counter("job_slot_homes", 1), counter("job_slot_gates", 1))
        job_dn, job_hi, job_lo = (counter("job_down_product", 2, base=1), counter("job_down_first_part", 2),
                                  counter("job_down_second_part", 2, base=1))
        job_acc = counter("job_combined", 1, base=1)
        stored = counter("out_stored", 0)

        def alone(eng, sem, value):
            eng.wait_ge(sem, value)
            eng.sem_inc(passed.sem, 1)

        def entry(eng, k, most):
            return eng.value_load(job[0:1, bass.ds(k, 1)], min_val=0, max_val=most)

        def for_jobs(eng, number, tail, body):
            with eng.If(number > 0):
                tail(True)
            with eng.Else():
                tail(False)
            with eng.If(number > 1):
                with eng.Fori(1, JOBS) as j:
                    with eng.If(number > j):
                        body(j)

        block = ctx.enter_context(nc.Block())

        def one(a, n):
            return a[bass.ds(n, 1)].rearrange("o p c -> (o p) c")

        @block.sync
        def _(sp_):
            sp_.dma_start(x[:, :, :], x_in).then_inc(x_landed.sem, 16)
            sp_.dma_start(cst[:, :], consts).then_inc(once.sem, 16)
            sp_.dma_start(cstb[:, :], consts_b).then_inc(once.sem, 16)
            sp_.wait_ge(zeroed.sem, 2)
            with sp_.Fori(0, DEPTH) as l:
                for n in range(3):
                    sp_.wait_ge(*dn_ps.at(l, -2 if n == 0 else 0))
                    if n == 0:
                        sp_.dma_start(pa[:, :], one(small_a, l)).then_inc(pa_in.sem, 16)
                    sp_.dma_start(ring[:, 1 + n, :], one(w_in, l)[:, n * SLOT:n * SLOT + SLOT]).then_inc(win_in[n].sem, 16)
                sp_.wait_ge(*x_ok.at(l, 0))
                sp_.dma_start(pb[:, :], one(small_b, l)).then_inc(pb_in.sem, 16)
                sp_.wait_ge(*tr_ok.at(l, 4))
                sp_.dma_start(area[:, :], one(w_out, l)).then_inc(wout_in.sem, 16)
                for j in range(RING):
                    if j == 1:
                        sp_.wait_ge(*proj_ok.at(l, 9))
                    sp_.dma_start(ring[:, j, 0:GU], one(experts, l * E + j)[:, 0:GU]).then_inc(up_in[j].sem, 16)
                    sp_.dma_start(ring[:, j, GU:SLOT], one(experts, l * E + j)[:, GU:SLOT]).then_inc(down_in[j].sem, 16)

                def load_gate_up(p, odd=None):
                    s0 = 2 * ((p if odd is None else odd) % 2)
                    sp_.wait_ge(*gu_ps.at(l, p - 1))
                    for s in range(2):
                        sp_.dma_start(ring[:, s0 + s, 0:GU], one(experts, l * E + 2 * p + s)[:, 0:GU]).then_inc(up_in[s0 + s].sem, 16)

                def load_down(p, odd=None):
                    s0 = 2 * ((p if odd is None else odd) % 2)
                    sp_.wait_ge(*dn_ps.at(l, 2 * (p - 1)))
                    for s in range(2):
                        sp_.dma_start(ring[:, s0 + s, GU:SLOT], one(experts, l * E + 2 * p + s)[:, GU:SLOT]).then_inc(down_in[s0 + s].sem, 16)
                sp_.wait_ge(*o_ps.at(l, 4))
                sp_.dma_start(bdn[0:E, :], one(b_down, l)).then_inc(bdn_in.sem, 16)
                sp_.wait_ge(*wo_ps.at(l, 12))
                sp_.dma_start(b_src[0:3 * E, :], one(b_gate_up, l)).then_inc(bsrc_in.sem, 16)
                sp_.wait_ge(*gu_half.at(l, 1))
                for s in range(2):
                    sp_.dma_start(ring[:, s, 0:GU // 2], one(experts, l * E + 4 + s)[:, 0:GU // 2]).then_inc(early_in[s].sem, 16)
                sp_.wait_ge(*gu_ps.at(l, 1))
                for s in range(2):
                    sp_.dma_start(ring[:, s, GU // 2:GU], one(experts, l * E + 4 + s)[:, GU // 2:GU]).then_inc(up_in[s].sem, 16)
                with sp_.Fori(1, PAIRS // 2 - 1) as i:
                    for n in (1, 2):
                        load_gate_up(2 * i + n, n)
                        load_down(2 * i + n - 1, n - 1)
                load_gate_up(PAIRS - 1)
                load_down(PAIRS - 2)

                def load_job_up(j):
                    alone(sp_, *job_gu.at(seen + j, 0))
                    e = entry(sp_, 3 + j, E - 1)
                    sp_.dma_start(ring[:, 0, 0:GU], one(experts, l * E + e)[:, 0:GU]).then_inc(job_in.sem, 16)
                    return e

                def load_job_down(j, e):
                    sp_.wait_ge(*dn_ps.at(l, 2 * PAIRS - 2))
                    sp_.wait_ge(*job_dn.at(seen + j, 0))
                    sp_.dma_start(ring[:, 0, GU:SLOT], one(experts, l * E + e)[:, GU:SLOT]).then_inc(job_down_in.sem, 16)

                def tail(job):
                    if job:
                        e = load_job_up(0)
                    load_down(PAIRS - 1)
                    if job:
                        load_job_down(0, e)
                alone(sp_, *list_ok.at(l, LIST_STEPS))
                number, seen = entry(sp_, 0, JOBS), entry(sp_, 1, DEPTH * JOBS)
                alone(sp_, *gu_ps.at(l, PAIRS - 1))
                for_jobs(sp_, number, tail, lambda j: load_job_down(j, load_job_up(j)))
            sp_.wait_ge(*x_ok.at(DEPTH, 0))
            sp_.dma_start(out, x[:, :, :]).then_inc(stored.sem, 16)
            sp_.wait_ge(stored.sem, 16)

        @block.tensor
        def _(pe):
            pe.sem_inc(dn_ps.sem, 3)
            for c in (job_gu, job_tr, job_dn, job_acc):
                pe.sem_inc(c.sem, 1)
            pe.sem_inc(acc_ps.sem, 1)
            pe.wait_ge(once.sem, 32)
            with pe.Fori(0, DEPTH) as l:
                def keep_warm(b, n):
                    for _ in range(n):
                        pe.matmul(bank[b][:, 0:2 * P], before_b, cstb[:, 0:2 * P], start=True, stop=True)

                def transpose_tokens(c):
                    for t in range(TT):
                        if c and t:
                            keep_warm(7, 16)
                        pe.wait_ge(*xn_ok.at(l, 2 * c + t + 1))
                        for b in range(4):
                            for dt in range(2):
                                k = 2 * b + dt
                                mm = pe.transpose(bank[b][:, dt * SEQ + t * P:dt * SEQ + t * P + P],
                                                  xn[:, t, k * P:k * P + P], ident)
                            if t == TT - 1:
                                mm.then_inc(tr_ok.sem, 1)

                keep_warm(3, 44)
                transpose_tokens(0)

                pe.wait_ge(*hT_act.at(l, 4))
                pe.wait_ge(*hT_dve.at(l, 4))
                for k in range(KD):
                    if k in (0, 2, 5):
                        pe.wait_ge(*win_in[(0, 2, 5).index(k)].at(l, 16))
                    for n in range(2):
                        for t in range(TT):
                            mm = pe.matmul(bank[4 + 2 * n + t][:, :], hT[:, k, t * P:t * P + P],
                                           win[:, k, 768 + 512 * n:1280 + 512 * n], start=(k == 0), stop=(k == KD - 1))
                            if k == KD - 1:
                                mm.then_inc(proj_ok.sem, 1)
                for b, c0 in enumerate((256, 512, 0)):
                    for c in range(2):
                        for k in range(KD):
                            mm = pe.matmul(bank[b][:, c * SEQ:c * SEQ + SEQ], win[:, k, c0 + c * P:c0 + c * P + P],
                                           hT[:, k, :], start=(k == 0), stop=(k == KD - 1))
                    mm.then_inc(proj_ok.sem, 1)
                for n in range(2):
                    for t in range(TT):
                        pe.wait_ge(*rope.at(l, 6 * (2 * n + t + 1)))
                        for c in range(4):
                            mm = pe.transpose(bank[4 + 2 * n + t][:, c * P:c * P + P], rot[:, n, t, c * P:c * P + P], ident)
                        mm.then_inc(qkT_ps.sem, 1)

                def project_v(t, k0, k1):
                    for k in range(k0, k1):
                        mm = pe.matmul(bank[3][:, :], hT[:, k, t * P:t * P + P], win[:, k, 1792:2304],
                                       start=(k == 0), stop=(k == KD - 1))
                    if k1 == KD:
                        mm.then_inc(proj_ok.sem, 1)
                project_v(0, 0, KD // 2)
                pe.wait_ge(*conv_ok.at(l, 8))
                pe.wait_ge(*proj_free.at(l, 2))
                for b in range(2):
                    for c in range(2):
                        w = pa[:, BD + (2 * b + c) * P:BD + (2 * b + c + 1) * P]
                        mm = pe.matmul(bank[b][:, c * SEQ:c * SEQ + SEQ], w, xc[:, c, :], start=True, stop=True)
                    mm.then_inc(lru_ps.sem, 1)
                project_v(0, KD // 2, KD)
                def scores(h):
                    if h == 0:
                        pe.wait_ge(*qkT_ok.at(l, 4))
                    if h >= 2:
                        pe.wait_ge(*s_ok.at(l, 2 * h - 2))
                    s, r = bank[4 + h % 2], slice(DH * (h % 2), DH * (h % 2) + DH)
                    pe.matmul(s[:, 0:P], qkT[r, 0, h // 2, 0:P], qkT[r, 1, h // 2, 0:P], start=True, stop=True)
                    pe.matmul(s[:, P:KEYS], qkT[r, 0, h // 2, P:SEQ], qkT[r, 1, h // 2, :], start=True,
                              stop=True).then_inc(s_ps.sem, 1)

                def turn_probs(h):
                    pe.wait_ge(*pn_ok.at(l, h + 1))
                    if h == 0:
                        pe.wait_ge(*qkT_ok.at(l, 4))
                    if h >= 2:
                        pe.wait_ge(*pt_ok.at(l, h - 1))
                    for c in range(3):
                        mm = pe.transpose(bank[6 + h % 2][:, c * P:c * P + P], prob[:, h % 2, c * P:c * P + P], ident)
                    mm.then_inc(pt_ps.sem, 1)

                def values(h):
                    pr = h // 2
                    pe.wait_ge(*pt_ok.at(l, h + 1))
                    if h == 0:
                        pe.wait_ge(*proj_free.at(l, 5))
                        pe.wait_ge(*lru_a.at(l, 2))
                    if h == 2:
                        pe.wait_ge(*st_ok.at(l, 1))
                    if h >= 4 and h % 2 == 0:
                        pe.wait_ge(*o_ok.at(l, pr - 1))
                    o = bank[pr % 2][DH * (h % 2):DH * (h % 2) + DH, :]
                    pe.matmul(o[:, 0:SEQ], vt[:, 0, h * DH:h * DH + DH], probT[:, h % 2, 0:SEQ],
                              start=True, stop=False)
                    mm = pe.matmul(o[:, P:SEQ], vt[:, 1, h * DH:h * DH + DH], probT[:, h % 2, SEQ:KEYS],
                                   start=False, stop=True)
                    if h % 2:
                        mm.then_inc(o_ps.sem, 1)

                def group_sums(b, groups):
                    for n, (k0, k1) in enumerate(groups):
                        for t in range(TT):
                            c = SEQ + 2 * n + t
                            for k in range(k0, k1):
                                mm = pe.matmul(bank[b][:, c:c + 1], ysq[:, k, t * P:t * P + P], ones,
                                               start=(k == k0), stop=(k == k1 - 1))
                    mm.then_inc(st_ps.sem, 1)

                def out_unit(n, k0, k1):
                    t, c = (n // 2) % 2, n % 2
                    if n == 0:
                        pe.wait_ge(*wout_in.at(l, 16))
                        pe.wait_ge(*lru_d.at(l, 8))
                    if n == 1:
                        pe.wait_ge(*proj_free.at(l, 5))
                    if n >= 2:
                        pe.wait_ge(*wo_ok.at(l, n - 1))
                    for k in range(k0, k1):
                        mm = pe.matmul(bank[2 + n % 2][:, :], yT[:, k, t * P:t * P + P], wout[:, k, c * 512:c * 512 + 512],
                                       start=(k == k0), stop=(k == k1 - 1))
                    mm.then_inc(wo_ps.sem, 1)

                scores(0)
                scores(1)
                pe.wait_ge(*pool_p.at(l, 9))
                pe.wait_ge(*proj_free.at(l, 3))
                for c in range(2):
                    mm = pe.matmul(bank[2][:, c * SEQ:c * SEQ + SEQ], pa[:, BD + (4 + c) * P:BD + (5 + c) * P],
                                   pooled[:, c, :], start=True, stop=True)
                mm.then_inc(pool_ps.sem, 1)

                pe.wait_ge(*proj_free.at(l, 4))
                project_v(1, 0, KD)
                turn_probs(0)
                for h in range(2, HEADS + 2):
                    if h < HEADS:
                        scores(h)
                    values(h - 2)
                    if h == 6:
                        pe.wait_ge(*lru_d.at(l, 14))
                    out_unit(h - 2, 0 if h < 6 else 2, 2 if h < 6 else 4)
                    if h < HEADS + 1:
                        turn_probs(h - 1)
                    if h == 3:
                        pe.wait_ge(*ysq_pl.at(l, 4))
                        pe.wait_ge(*lru_a.at(l, 4))
                        group_sums(1, ((0, 2), (2, 4)))
                pe.wait_ge(*ysq_at.at(l, 4))
                pe.wait_ge(*o_ok.at(l, 4))
                group_sums(0, ((4, 8),))
                for n in range(8, 12):
                    out_unit(n, 4, 8)

                pe.wait_ge(*st_ok.at(l, 2))
                pe.wait_ge(*wo_ok.at(l, 12))
                transpose_tokens(1)
                pe.wait_ge(*pb_in.at(l, 16))
                pe.wait_ge(*hT_act.at(l, 8))
                pe.wait_ge(*hT_dve.at(l, 8))
                for k in range(KD):
                    mm = pe.matmul(bank[4][0:E, 0:SEQ], pb[:, RW + k * E:RW + k * E + E], hT[:, k, :],
                                   start=(k == 0), stop=(k == KD - 1))
                mm.then_inc(lgT_ps.sem, 1)

                keep_warm(7, 5)
                alone(pe, *lgT_ok.at(l, 1))
                for t in range(TT):
                    mm = pe.transpose(bank[5][:, t * E:t * E + E], lgT[0:E, t * P:t * P + P], ident[0:E, 0:E])
                mm.then_inc(lg_ps.sem, 1)
                keep_warm(7, 34)
                pe.wait_ge(*rk_ok.at(l, 1))
                pe.matmul(bank[6][:, 0:E], before_b, sel[:, 0, :], start=True, stop=True)
                pe.matmul(bank[6][:, E:2 * E], all_b, sel[:, 0, :], start=True, stop=False)
                pe.matmul(bank[6][:, E:2 * E], before_b, sel[:, 1, :], start=False, stop=True)
                pe.matmul(bank[6][:, 2 * E:3 * E], all_b, sel[:, 0, :], start=True, stop=False)
                pe.matmul(bank[6][:, 2 * E:3 * E], all_b, sel[:, 1, :], start=False, stop=True).then_inc(rk_ps.sem, 1)
                for t in range(TT):
                    mm = pe.transpose(bank[7][0:E, t * P:t * P + P], gates[:, t, :], ident)
                mm.then_inc(gT_ps.sem, 1)

                def gather(quad, par, c, b=3):
                    if b == 3 and par is not None:
                        pe.wait_ge(*(xT_act.at(l, 2 * quad + (c + 1) // 2) if c % 2 else xT_dve.at(l, 2 * quad + c // 2)))
                    for dt in range(2):
                        k = 2 * c + dt
                        for t in range(TT):
                            for n in range(2):
                                mm = pe.matmul(bank[b][:, dt * SEQ:dt * SEQ + SEQ], xs2[:, n, t, k * P:k * P + P],
                                               sm[:, par or 0, t, :], start=(t == 0 and n == 0),
                                               stop=(t == 1 and n == 1))
                    mm.then_inc(gth_ps.sem, 1)

                def gate_up(p, first):
                    pe.wait_ge(*pick_ok.at(l, p.n + 1))
                    pe.wait_ge(*gu_rd.at(l, p.n))
                    if first:
                        pe.wait_ge(*xT_act.at(l, 1))
                    elif p.first:
                        pe.wait_ge(*xT_dve.at(l, 2 * p.quad + 2))
                        pe.wait_ge(*xT_act.at(l, 2 * p.quad + 2))
                    for s in range(2):
                        if p.place == 2:
                            pe.wait_ge(*early_in[s].at(l, 16))
                        pe.wait_ge(*up_in[p.slot + s].at(l, 16 * (p.quad + 1)))
                    pe.matmul(bank[0][:, :], pick[0:3 * E, :], b_rows[0:3 * E, :], start=True, stop=False,
                              skip_group_check=True)
                    for k in range(KD):
                        if first and k in (2, 6):
                            pe.wait_ge(*xT_dve.at(l, k // 4 + 1))
                        if first and k == 4:
                            pe.wait_ge(*xT_act.at(l, 2))
                        for s in range(2):
                            c = (p.slot + s) * CAP
                            mm = pe.matmul(bank[0][s * CAP:s * CAP + CAP, :], xT[:, p.par, k, c:c + CAP],
                                           ring[:, p.slot + s, k * 2 * FF:(k + 1) * 2 * FF], start=False,
                                           stop=(k == KD - 1), skip_group_check=True)
                        if first and k == KD // 2 - 1:
                            mm.then_inc(gu_half.sem, 1)
                    mm.then_inc(gu_ps.sem, 1)

                def turn(p):
                    pe.wait_ge(*act_ok.at(l, p.n + 1))
                    pe.wait_ge(*gm_ok.at(l, p.quad + 1))
                    pe.wait_ge(*y_rd.at(l, 2 * p.n))
                    pe.wait_ge(*ylo_ok.at(l, 2 * p.n))
                    for f in range(2):
                        pe.transpose(bank[1][:, f * P:f * P + P], act_e[:, f * P:f * P + P], ident)
                    for t in range(TT):
                        c = p.slot * CAP
                        mm = pe.transpose(bank[2][:, t * P:t * P + P], gm[:, p.par, t, c:c + P], ident)
                    mm.then_inc(ag_ps.sem, 1)

                def down(p):
                    pe.wait_ge(*ag_ok.at(l, p.n + 1))
                    for s in range(2):
                        pe.wait_ge(*down_in[p.slot + s].at(l, 16 * (p.quad + 1)))
                    for h in range(2):
                        if h:
                            pe.wait_ge(*gc_ok.at(l, p.n + 1))
                        for k in range(2):
                            for s in range(2):
                                mm = pe.matmul(bank[1 + h][s * CAP:s * CAP + CAP, :], ag[:, k, s * CAP:s * CAP + CAP],
                                               ring[:, p.slot + s, GU + k * D + h * 512:GU + k * D + h * 512 + 512],
                                               start=(k == 0), stop=(k == 1), skip_group_check=True)
                        mm.then_inc(dn_ps.sem, 1)

                def combine(p):
                    for h in range(2):
                        pe.wait_ge(*y_rd.at(l, 2 * p.n + h + 1))
                        pe.wait_ge(*ylo_ok.at(l, 2 * p.n + h + 1))
                        for t in range(TT):
                            for part in (y_hi[:, h * 512:h * 512 + 512], y_lo[h][:, :]):
                                mm = pe.matmul(bank[4 + 2 * t + h][:, :], home[:, t * P:t * P + P], part,
                                               start=False, stop=False, skip_group_check=True)
                    mm.then_inc(acc_ps.sem, 1)

                pe.wait_ge(*x0_ok.at(l, 2))
                pe.wait_ge(*x1_ok.at(l, 2))
                pe.wait_ge(*sm_ok.at(l, 1))
                for c in range(4):
                    gather(0, None, c, b=c)
                pe.wait_ge(*brow_ok.at(l, 6))

                def open_sums():
                    pe.wait_ge(*gT_ok.at(l, 1))
                    pe.wait_ge(*rk_ok.at(l, 3))
                    pe.wait_ge(*bdn_in.at(l, 16))
                    for t in range(TT):
                        for h in range(2):
                            pe.matmul(bank[4 + 2 * t + h][:, :], gT[0:E, t * P:t * P + P], bdn[0:E, h * 512:h * 512 + 512],
                                      start=True, stop=False, skip_group_check=True)

                def pair_turn(p, before, more=True, job=None):
                    gate_up(p, not before)
                    if before:
                        turn(before)
                    else:
                        open_sums()
                    if more:
                        if p.first:
                            pe.wait_ge(*sm_ok.at(l, p.quad + 2))
                        gather(p.quad + 1, 1 - p.par, p.slot)
                    if job is not None:
                        gather_job(0, job)
                    if before:
                        down(before)
                    if more:
                        gather(p.quad + 1, 1 - p.par, p.slot + 1)
                    if job is not None:
                        gather_job(0, job + 1)
                    if before:
                        combine(before)

                pair_turn(Pair(0, 0), None)
                with pe.Fori(0, PAIRS // 4 - 1) as i:
                    for n in range(4):
                        pair_turn(Pair(i, n + 1), Pair(i, n))
                pair_turn(Pair(0, PAIRS - 3), Pair(0, PAIRS - 4))
                alone(pe, *list_ok.at(l, LIST_STEPS))
                number, seen = entry(pe, 0, JOBS), entry(pe, 1, DEPTH * JOBS)

                def gather_job(j, c):
                    n = seen + j
                    if c == 0:
                        pe.wait_ge(*job_sm.at(n, 1))
                    else:
                        pe.wait_ge(*(job_xa if c % 2 else job_xd).at(n, (c + 1) // 2))
                    for dt in range(2):
                        k = 2 * c + dt
                        for t in range(TT):
                            twice = sm[:, 0, t, 0:P].unsqueeze(1).broadcast_to([P, 2, P])
                            for i in range(2):
                                dst = bank[3][:, dt * SEQ:dt * SEQ + SEQ].rearrange("p (a s) -> p a s", a=2)
                                mm = pe.matmul(dst, xs2[:, i, t, k * P:k * P + P], twice, start=(t == 0 and i == 0),
                                               stop=(t == 1 and i == 1))
                    mm.then_inc(job_gth.sem, 1)

                def start(j):
                    n = seen + j
                    pe.wait_ge(*job_xa.at(n, 2))
                    pe.wait_ge(*job_xd.at(n, 2))
                    pe.wait_ge(*gu_rd.at(l, PAIRS))
                    pe.wait_ge(*job_step.at(n, 0))
                    pe.wait_ge(*job_in.at(n, 16))
                    pe.matmul(bank[0][:, :], job_pick[0:3 * E, :], b_rows[0:3 * E, :], start=True, stop=False)
                    for k in range(KD):
                        mm = pe.matmul(bank[0][:, :], xT_job[:, k, :], ring[:, 0, k * 2 * FF:(k + 1) * 2 * FF], start=False,
                                       stop=(k == KD - 1))
                    mm.then_inc(job_gu.sem, 1)

                def finish(j):
                    n = seen + j
                    pe.wait_ge(*job_step.at(n, 3))
                    pe.wait_ge(*y_rd.at(l, 2 * PAIRS))
                    pe.wait_ge(*ylo_ok.at(l, 2 * PAIRS))
                    pe.wait_ge(*job_lo.at(n, 0))
                    for f in range(2):
                        pe.transpose(bank[1][:, f * P:f * P + P], act_e[:, f * P:f * P + P], ident)
                    for t in range(TT):
                        mm = pe.transpose(bank[2][:, t * P:t * P + P], gm[:, 0, t, 0:P], ident)
                    mm.then_inc(job_tr.sem, 1)
                    pe.wait_ge(*job_ag.at(n, 1))
                    pe.wait_ge(*job_down_in.at(n, 16))
                    for h in range(2):
                        if h:
                            pe.wait_ge(*job_gc.at(n, 1))
                        for k in range(2):
                            mm = pe.matmul(bank[1 + h][:, :], ag[:, k, :], ring[:, 0, GU + k * D + h * 512:GU + k * D + h * 512 + 512],
                                           start=(k == 0), stop=(k == 1))
                        mm.then_inc(job_dn.sem, 1)
                    for h in range(2):
                        pe.wait_ge(*job_hi.at(n, h + 1))
                        pe.wait_ge(*job_lo.at(n, h + 1))
                        for t in range(TT):
                            for part in (y_hi[:, h * 512:h * 512 + 512], y_lo[h][:, :]):
                                mm = pe.matmul(bank[4 + 2 * t + h][:, :], home[:, t * P:t * P + P], part,
                                               start=False, stop=False, skip_group_check=True)
                    mm.then_inc(job_acc.sem, 1)
                def tail(job):
                    pair_turn(Pair(0, PAIRS - 2), Pair(0, PAIRS - 3), more=False, job=0 if job else None)
                    pair_turn(Pair(0, PAIRS - 1), Pair(0, PAIRS - 2), more=False, job=2 if job else None)
                    if job:
                        start(0)
                    turn(Pair(0, PAIRS - 1))
                    down(Pair(0, PAIRS - 1))
                    combine(Pair(0, PAIRS - 1))
                    if job:
                        finish(0)

                def another_job(j):
                    for c in range(4):
                        gather_job(j, c)
                    start(j)
                    finish(j)
                for_jobs(pe, number, tail, another_job)

        @block.vector
        def _(dve):
            dve.sem_inc(x_ok.sem, 3)
            for c in (gu_rd, act_ok, home_ok, ylo_ok, job_step, job_lo):
                dve.sem_inc(c.sem, 1)
            dve.memset(up[:, :, 0:CONV - 1], 0.0)
            dve.memset(pp[:, :, 0:PAD], 0.0).then_inc(zeroed.sem, 1)
            dve.memset(job_f[:, :], 0.0)
            dve.memset(job[:, :], 0).then_inc(zeroed.sem, 1)
            dve.wait_ge(once.sem, 32)
            dve.wait_ge(zeroed.sem, 2)
            with dve.Fori(0, DEPTH) as l:
                def normalise(c):
                    for t in range(TT):
                        dve.wait_ge(*rstd_ok.at(l, 2 * c + t + 1))
                        dve.tensor_scalar(xn[:, t, :], x[:, t, :], rstd[:, 2 * c + t:2 * c + t + 1], None, ALU.mult
                                          ).then_inc(xn_ok.sem, 1)

                def turned(c, gain):
                    for b in (1, 3):
                        dve.wait_ge(*tr_ok.at(l, 4 * c + b + 1))
                        for dt in range(2):
                            k = 2 * b + dt
                            dve.tensor_scalar(hT[:, k, :], bank[b][:, dt * SEQ:dt * SEQ + SEQ], gain[:, k:k + 1], None,
                                              ALU.mult).then_inc(hT_dve.sem, 1)

                normalise(0)
                dve.wait_ge(*pa_in.at(l, 16))
                turned(0, pa[:, G1:G1 + KD])

                steps = [0]

                def tiny(ins):
                    ins.then_inc(sp_dve.sem, 1)
                    steps[0] += 1
                    dve.wait_ge(*sp_dve.at(l, steps[0]))
                lam = pa[:, LAM:LAM + 2]
                tiny(dve.tensor_scalar(sp[:, 0, :], lam, -1.0, None, ALU.mult))
                tiny(dve.tensor_tensor(sp[:, 1, :], lam, sp[:, 0, :], ALU.max))
                tiny(dve.tensor_scalar(hb[:, :], pa[:, BA:BA + 4], 0.5, None, ALU.mult))
                dve.wait_ge(*sp_act.at(l, 1))
                tiny(dve.tensor_scalar(sp[:, 3, :], sp[:, 2, :], 2.0, None, ALU.add))
                tiny(dve.reciprocal(sp[:, 4, :], sp[:, 3, :]))
                tiny(dve.tensor_tensor(sp[:, 5, :], sp[:, 2, :], sp[:, 4, :], ALU.mult))
                tiny(dve.tensor_tensor(sp[:, 6, :], sp[:, 5, :], sp[:, 5, :], ALU.mult))
                tiny(dve.tensor_scalar(sp[:, 7, :], sp[:, 6, :], 1.0 / (2 * ATANH_TERMS - 1), None, ALU.mult))
                for k in range(ATANH_TERMS - 2, 0, -1):
                    tiny(dve.scalar_tensor_tensor(sp[:, 7, :], sp[:, 7, :], 1.0 / (2 * k + 1), sp[:, 6, :], ALU.add, ALU.mult))
                tiny(dve.scalar_tensor_tensor(sp[:, 8, :], sp[:, 7, :], 1.0, sp[:, 5, :], ALU.add, ALU.mult))
                tiny(dve.tensor_scalar(sp[:, 9, :], sp[:, 0, :], 0.0, -4.0, ALU.max, ALU.mult))
                tiny(dve.scalar_tensor_tensor(sp[:, 10, :], sp[:, 8, :], -8.0, sp[:, 9, :], ALU.mult, ALU.add))
                for n, (g0, scale) in enumerate(((QG, DH ** -0.5), (KG, 1.0))):
                    gain = pa[:, g0:g0 + DH].unsqueeze(1).broadcast_to([P, TT, DH])
                    dve.scalar_tensor_tensor(cg[:, n, 0, :, :], cos_t, scale, gain, ALU.mult, ALU.mult)
                    for a, b in ((0, 32), (32, 0)):
                        gs = pa[:, g0 + b:g0 + b + 32].unsqueeze(1).broadcast_to([P, TT, 32])
                        ins = dve.scalar_tensor_tensor(cg[:, n, 1, :, a:a + 32], sin_t[:, :, a:a + 32], scale, gs,
                                                       ALU.mult, ALU.mult)
                tiny(ins)
                assert steps[0] == 19

                def rope_unit(n, t):
                    w = 2 * n + t
                    b3 = bank[4 + w][:, :].rearrange("p (h d) -> p h d", h=HEADS)
                    dve.wait_ge(*sq_ok.at(l, w + 1))
                    dve.tensor_reduce(hs[:, w, 0:8], sq[:, :].rearrange("p (h d) -> p h d", h=HEADS), AX.X, ALU.add
                                      ).then_inc(hsum_ok.sem, 1)
                    dve.wait_ge(*hr_ok.at(l, w + 1))
                    r0 = 6 * w
                    t3 = tmp[:, :].rearrange("p (h d) -> p h d", h=HEADS)
                    s3 = swp[:, :].rearrange("p (h d) -> p h d", h=HEADS)
                    o3 = rot[:, n, t, :].rearrange("p (h d) -> p h d", h=HEADS)
                    dve.tensor_tensor(t3, b3, hs[:, w, 8:16].unsqueeze(2).broadcast_to([P, HEADS, DH]), ALU.mult
                                      ).then_inc(rope.sem, 1)
                    dve.wait_ge(*rope.at(l, r0 + 1))
                    cgc = cg[:, n, 0, t, :].unsqueeze(1).broadcast_to([P, HEADS, DH])
                    dve.tensor_tensor(o3, t3, cgc, ALU.mult).then_inc(rope.sem, 1)
                    for a, b in ((0, 32), (32, 0)):
                        cgs = cg[:, n, 1, t, a:a + 32].unsqueeze(1).broadcast_to([P, HEADS, 32])
                        dve.tensor_tensor(s3[:, :, a:a + 32], t3[:, :, b:b + 32], cgs, ALU.mult).then_inc(rope.sem, 1)
                    dve.wait_ge(*rope.at(l, r0 + 4))
                    dve.tensor_tensor(o3, o3, s3, ALU.add).then_inc(rope.sem, 2)

                for n in range(2):
                    for t in range(TT):
                        rope_unit(n, t)

                dve.wait_ge(*proj_free.at(l, 1))
                for c in range(2):
                    w = [pa[:, CW + 2 * j + c:CW + 2 * j + c + 1] for j in range(CONV)]
                    dve.tensor_scalar(xc[:, c, :], up[:, c, 0:SEQ], w[0], pa[:, CB + c:CB + c + 1], ALU.mult, ALU.add
                                      ).then_inc(conv_ok.sem, 1)
                for j in range(1, CONV):
                    for c in range(2):
                        dve.wait_ge(*conv_ok.at(l, 2 * j + c - 1))
                        dve.scalar_tensor_tensor(xc[:, c, :], up[:, c, j:j + SEQ], pa[:, CW + 2 * j + c:CW + 2 * j + c + 1],
                                                 xc[:, c, :], ALU.mult, ALU.add).then_inc(conv_ok.sem, 1)
                for w in (1, 3):
                    dve.wait_ge(*qkT_ps.at(l, w + 1))
                    dve.tensor_copy(qkT[:, w // 2, :, P:SEQ], bank[4 + w][:, :].rearrange("p (c s) -> p c s", c=4)
                                    ).then_inc(qkT_ok.sem, 1)

                def masked(h):
                    for t, (a, b) in enumerate(((0, P), (P, KEYS))):
                        if h >= 2 and t == 0:
                            dve.wait_ge(*pt_ps.at(l, h - 1))
                        if t == 0:
                            alone(dve, *s_ps.at(l, h + 1))
                        dve.tensor_tensor_reduce(prob[:, h % 2, a:b], bank[4 + h % 2][:, a:b], mask[:, a:b], -1.0, 3e38,
                                                 ALU.add, ALU.min, nmax[:, 2 * h + t:2 * h + t + 1]).then_inc(s_ok.sem, 1)

                def normalised(h):
                    dve.wait_ge(*e_ok.at(l, 2 * h + 2))
                    dve.reciprocal(rden[:, 2 * h:2 * h + 2], den[:, 2 * h:2 * h + 2]).then_inc(rd_ok.sem, 1)
                    dve.wait_ge(*rd_ok.at(l, h + 1))
                    for t, (a, b) in enumerate(((0, P), (P, KEYS))):
                        ins = dve.tensor_scalar(prob[:, h % 2, a:b], prob[:, h % 2, a:b], rden[:, 2 * h + t:2 * h + t + 1],
                                                None, ALU.mult)
                    ins.then_inc(pn_ok.sem, 1)

                dve.wait_ge(*lru_a.at(l, 2))
                for c in range(2):
                    dve.tensor_scalar(la[:, c, :], th_r[:, c, :], sp[:, 10, c:c + 1], sp[:, 10, c:c + 1], ALU.mult, ALU.add
                                      ).then_inc(lru_d.sem, 1)
                masked(0)
                masked(1)
                dve.wait_ge(*lru_a.at(l, 6))
                dve.tensor_scalar(rec[:, :, :], tn[:, :, :], 1.0, None, ALU.add).then_inc(lru_d.sem, 1)
                dve.wait_ge(*lru_d.at(l, 3))
                dve.reciprocal(rec[:, :, :], rec[:, :, :]).then_inc(lru_d.sem, 1)
                dve.scalar_tensor_tensor(th_i[:, :, :], th_i[:, :, :], 1.0, xc[:, :, :], ALU.add, ALU.mult
                                         ).then_inc(lru_d.sem, 1)
                dve.wait_ge(*lru_d.at(l, 4))
                dve.scalar_tensor_tensor(tn[:, :, :], tn[:, :, :], 2.0, rec[:, :, :], ALU.mult, ALU.mult
                                         ).then_inc(lru_d.sem, 1)
                dve.wait_ge(*pool_ps.at(l, 1))
                for c in range(2):
                    dve.tensor_scalar(pooled[:, c, :], bank[2][:, c * SEQ:c * SEQ + SEQ], pa[:, PS + c:PS + c + 1], None,
                                      ALU.mult).then_inc(pool_ok.sem, 1)
                normalised(0)
                dve.wait_ge(*pool_ok.at(l, 2))
                dve.wait_ge(*proj_ok.at(l, 9))
                for c in range(2):
                    dve.tensor_scalar(yT[:, c, :], pooled[:, c, :], pa[:, OG + c:OG + c + 1], None, ALU.mult
                                      ).then_inc(lru_d.sem, 1)
                masked(2)
                normalised(1)
                dve.wait_ge(*lru_a.at(l, 7))
                dve.memset(tn[:, :, 0:1], 1.0).then_inc(lru_d.sem, 1)
                dve.wait_ge(*lru_d.at(l, 9))
                dve.scalar_tensor_tensor(th_i[:, :, :], th_i[:, :, :], 0.5, tn[:, :, :], ALU.mult, ALU.mult
                                         ).then_inc(lru_d.sem, 1)
                dve.wait_ge(*lru_d.at(l, 10))
                for c in range(2):
                    ins = dve.tensor_tensor_scan(la[:, c, :], ea[:, c, :], th_i[:, c, :], 0.0, ALU.mult, ALU.add)
                ins.then_inc(lru_d.sem, 1)
                dve.wait_ge(*lru_d.at(l, 11))
                dve.wait_ge(*gelu_p.at(l, 5))
                dve.tensor_tensor(xc[:, :, :], la[:, :, :], gl[:, :, :], ALU.mult).then_inc(lru_d.sem, 1)
                dve.wait_ge(*lru_d.at(l, 12))
                for c in range(2):
                    dve.tensor_scalar(yT[:, 2 + c, :], xc[:, c, :], pa[:, OG + 2 + c:OG + 3 + c], None, ALU.mult
                                      ).then_inc(lru_d.sem, 1)

                def attention_y(pr):
                    dve.wait_ge(*ysq_at.at(l, pr + 1))
                    dve.tensor_scalar(yT[:, 4 + pr, :], bank[pr % 2][:, 0:SEQ], pa[:, OG + 4 + pr:OG + 5 + pr], None,
                                      ALU.mult).then_inc(o_ok.sem, 1)

                def added(n, grp):
                    t, c = (n // 2) % 2, n % 2
                    dve.wait_ge(*wo_ps.at(l, n + 1))
                    if n >= 4:
                        dve.wait_ge(*wo_ok.at(l, n - 3))
                    xs = x[:, t, c * 512:c * 512 + 512]
                    dve.scalar_tensor_tensor(xs, bank[2 + n % 2][:, :], grs[:, 2 * grp + t:2 * grp + t + 1], xs,
                                             ALU.mult, ALU.add).then_inc(wo_ok.sem, 1)

                for h in range(3, HEADS + 2):
                    if h == 4:
                        dve.wait_ge(*st_ps.at(l, 1))
                        dve.tensor_copy(gstat[:, 0:4], bank[1][:, SEQ:SEQ + 4]).then_inc(st_ok.sem, 1)
                    if h < HEADS:
                        masked(h)
                    if h < HEADS + 1:
                        normalised(h - 1)
                    if h % 2:
                        attention_y((h - 3) // 2)
                    if h == 4:
                        dve.wait_ge(*gr_ok.at(l, 1))
                        added(0, 0)
                        added(1, 0)
                    if h >= 4:
                        added(h - 2, 0 if h - 2 < 4 else 1)
                dve.wait_ge(*st_ps.at(l, 2))
                dve.tensor_copy(gstat[:, 4:6], bank[0][:, SEQ:SEQ + 2]).then_inc(st_ok.sem, 1)
                dve.wait_ge(*gr_ok.at(l, 2))
                for n in range(8, 12):
                    added(n, 2)

                normalise(1)
                dve.wait_ge(*pb_in.at(l, 16))
                turned(1, pb[:, G2:G2 + KD])
                for t in range(TT):
                    dve.wait_ge(*x0_ok.at(l, t + 1))
                    dve.tensor_tensor(xs2[:, 1, t, :], xn[:, t, :], xs2[:, 0, t, :], ALU.subtract).then_inc(x1_ok.sem, 1)
                dve.wait_ge(*lgT_ps.at(l, 1))
                dve.tensor_scalar(lgT[0:E, :], bank[4][0:E, 0:SEQ], pb[0:E, RB:RB + 1], None, ALU.add).then_inc(lgT_ok.sem, 1)

                rs = [0]

                def step(ins):
                    ins.then_inc(rt.sem, 1)
                    rs[0] += 1

                def settle():
                    dve.wait_ge(*rt.at(l, rs[0]))
                dve.wait_ge(*lg_ps.at(l, 1))
                step(dve.tensor_copy(lg[:, :, :], bank[5][:, 0:TT * E].rearrange("p (t e) -> p t e", t=TT)))
                alone(dve, *rt.at(l, 1))
                for t in range(TT):
                    step(dve.max(top[:, t, :], lg[:, t, :]))
                alone(dve, *rt.at(l, 3))
                for t in range(TT):
                    step(dve.max_index(tix[:, t, :], top[:, t, :], lg[:, t, :]))
                    step(dve.tensor_scalar(ntop[:, t:t + 1], top[:, t, 0:1], -1.0, None, ALU.mult))
                settle()
                step(dve.tensor_copy(tif[:, :, :], tix[:, :, :]))
                settle()
                step(dve.tensor_tensor(hot, iota_e.unsqueeze(1).unsqueeze(1).broadcast_to([P, TT, TOPK, E]),
                                       tif[:, :, 0:TOPK].unsqueeze(3).broadcast_to([P, TT, TOPK, E]), ALU.is_equal))
                dve.wait_ge(*rt_act.at(l, 2))
                step(dve.reciprocal(rp4[:, :], psum4[:, :]))
                settle()
                step(dve.tensor_tensor(ptop[:, :, :], ptop[:, :, :], rp4[:, :].unsqueeze(2).broadcast_to([P, TT, TOPK]), ALU.mult))
                settle()
                step(dve.tensor_tensor(hot, hot, ptop[:, :, :].unsqueeze(3).broadcast_to([P, TT, TOPK, E]), ALU.mult))
                settle()
                step(dve.tensor_tensor(hot[:, :, 0:2, :], hot[:, :, 0:2, :], hot[:, :, 2:4, :], ALU.add))
                settle()
                step(dve.tensor_tensor(gates[:, :, :], hot[:, :, 0, :], hot[:, :, 1, :], ALU.add))
                settle()
                dve.tensor_scalar(sel[:, :, :], gates[:, :, :], 0.0, None, ALU.is_gt).then_inc(rk_ok.sem, 1)
                step(dve.tensor_scalar(halfg[:, :, :], gates[:, :, :], 0.5, None, ALU.mult))
                assert rs[0] == ROUTER_STEPS

                def select(quad, par):
                    r = rank[:, :, bass.ds(4 * quad, 4)].unsqueeze(3).broadcast_to([P, TT, 4, CAP])
                    s4 = slots[:, 0:CAP].unsqueeze(1).broadcast_to([P, 4, CAP])
                    dst = sm[:, par].rearrange("p t (e s) -> p t e s", e=4)
                    for t in range(TT):
                        ins = dve.tensor_tensor(dst[:, t], r[:, t], s4, ALU.is_equal)
                    ins.then_inc(sm_ok.sem, 1)

                def spread_gates(quad, par):
                    gq = halfg[:, :, bass.ds(4 * quad, 4)].unsqueeze(3).broadcast_to([P, TT, 4, CAP])
                    src = sm[:, par].bitcast(F32).rearrange("p t (e s) -> p t e s", e=4)
                    dst = gm[:, par].rearrange("p t (e s) -> p t e s", e=4)
                    dve.wait_ge(*sm_ok.at(l, quad + 1))
                    for t in range(TT):
                        ins = dve.tensor_tensor(dst[:, t], src[:, t], gq[:, t], ALU.mult)
                    ins.then_inc(gm_ok.sem, 1)

                def owners(n):
                    dve.tensor_scalar(pick[0:3 * E, :], owner[0:3 * E, :], iota_e[0:3 * E, bass.ds(2 * n, 1)], None,
                                      ALU.is_equal).then_inc(pick_ok.sem, 1)

                def tiles_out(quad, par, c, b=3):
                    dve.wait_ge(*gth_ps.at(l, 4 * quad + c + 1))
                    for dt in range(2):
                        k = 2 * c + dt
                        ins = dve.tensor_scalar(xT[:, par, k, :], bank[b][:, dt * SEQ:dt * SEQ + SEQ],
                                                pb[:, G2 + k:G2 + k + 1], None, ALU.mult)
                    ins.then_inc(xT_dve.sem, 1)

                dve.wait_ge(*rk_ps.at(l, 1))
                dve.scalar_tensor_tensor(rank[:, :, :], bank[6][:, 0:TT * E].rearrange("p (t e) -> p t e", t=TT), 1.0,
                                         sel[:, :, :], ALU.add, ALU.mult).then_inc(rk_ok.sem, 1)
                dve.wait_ge(*rk_ok.at(l, 2))
                select(0, 0)
                dve.tensor_copy(count, bank[6][:, 2 * E:3 * E]).then_inc(rk_ok.sem, 1)
                dve.wait_ge(*gT_ps.at(l, 1))
                dve.tensor_copy(gT[0:E, :], bank[7][0:E, 0:SEQ]).then_inc(gT_ok.sem, 1)
                tiles_out(0, 0, 1, 1)
                owners(0)
                tiles_out(0, 0, 3, 3)
                select(1, 1)
                spread_gates(0, 0)

                def swiglu(p, another=True):
                    dve.wait_ge(*gu_ps.at(l, p.n + 1))
                    dve.wait_ge(*act_ok.at(l, p.n))
                    dve.tensor_scalar(g, bank[0][:, 0:FF], LIMIT, None, ALU.min)
                    dve.tensor_scalar(u, bank[0][:, FF:2 * FF], LIMIT, -LIMIT, ALU.min, ALU.max).then_inc(gu_rd.sem, 1)
                    if another:
                        owners(p.n + 1)
                    dve.wait_ge(*sg_ok.at(l, p.n + 1))
                    dve.scalar_tensor_tensor(th, th, 1.0, g, ALU.add, ALU.mult).then_inc(am_ok.sem, 1)
                    dve.wait_ge(*am_ok.at(l, p.n + 1))
                    dve.wait_ge(*ag_ps.at(l, p.n))
                    dve.scalar_tensor_tensor(act_e, u, 1.0, th, ALU.add, ALU.mult).then_inc(act_ok.sem, 1)

                def homes(p):
                    dve.wait_ge(*ag_ps.at(l, p.n + 1))
                    dve.wait_ge(*acc_ps.at(l, p.n))
                    dve.tensor_scalar(home[:, :], bank[2][:, 0:SEQ], 0.0, None, ALU.is_gt).then_inc(home_ok.sem, 1)

                def down_rest(p):
                    for h in range(2):
                        dve.wait_ge(*y_rd.at(l, 2 * p.n + h + 1))
                        dve.scalar_tensor_tensor(y_lo[h][:, :], bank[1 + h][:, :], gcol[:, 0:1], y_hi[:, h * 512:h * 512 + 512],
                                                 ALU.mult, ALU.subtract).then_inc(ylo_ok.sem, 1)

                def pair_turn(p, before=None, choose=True, spread=True, more=True, another=True, job=None):
                    if before:
                        homes(before)
                    swiglu(p, another)
                    if before:
                        down_rest(before)
                    if more:
                        tiles_out(p.quad + 1, 1 - p.par, p.slot + 1)
                    if job is not None:
                        job_tiles_out(0, job)
                    if not p.first and choose:
                        select(p.quad + 2, p.par)
                    if p.first and spread:
                        spread_gates(p.quad + 1, 1 - p.par)

                js = [0]

                def listed(ins):
                    ins.then_inc(list_ok.sem, 1)
                    js[0] += 1
                    dve.wait_ge(*list_ok.at(l, js[0]))
                dve.wait_ge(*rk_ok.at(l, 3))
                listed(dve.tensor_scalar(over, count, CAP + 0.5, None, ALU.is_gt))
                listed(dve.tensor_scalar(over2, count, CAP + P + 0.5, None, ALU.is_gt))
                listed(dve.tensor_tensor(first, over, over2, ALU.add))
                listed(dve.tensor_tensor_scan(place, one_row, first, 0.0, ALU.mult, ALU.add))
                listed(dve.tensor_tensor(first, place, over2, ALU.subtract))
                listed(dve.tensor_tensor(first, first, over, ALU.mult))
                listed(dve.tensor_tensor(second, place, over2, ALU.mult))
                listed(dve.tensor_copy(job_f[:, 1:2], job_f[:, 2:3]))
                listed(dve.tensor_copy(job_f[:, 0:1], by_expert[:, 11, E - 1:E]))
                listed(dve.tensor_tensor(job_f[:, 2:3], job_f[:, 1:2], job_f[:, 0:1], ALU.add))
                pair_turn(Pair(0, 0))
                job_e, job_low = job_f[:, 3:3 + JOBS], job_f[:, 3 + JOBS:3 + 2 * JOBS]
                numbers = slots[:, 0:JOBS].unsqueeze(2).broadcast_to([P, JOBS, E])
                listed(dve.tensor_tensor(is_job, second.unsqueeze(1).broadcast_to([P, JOBS, E]), numbers, ALU.is_equal))
                listed(dve.tensor_reduce(job_low, is_job, AX.X, ALU.add))
                listed(dve.tensor_scalar(job_low, job_low, float(P), float(CAP), ALU.mult, ALU.add))
                experts_of = by_expert[:, 15, 0:JOBS]
                by_iota = iota_e.unsqueeze(1).broadcast_to([P, JOBS, E])
                listed(dve.tensor_tensor(is_job, is_job, by_iota, ALU.mult))
                listed(dve.tensor_reduce(job_e, is_job, AX.X, ALU.add))
                listed(dve.tensor_tensor(is_job, first.unsqueeze(1).broadcast_to([P, JOBS, E]), numbers, ALU.is_equal))
                listed(dve.tensor_tensor(is_job, is_job, by_iota, ALU.mult))
                listed(dve.tensor_reduce(experts_of, is_job, AX.X, ALU.add))
                listed(dve.tensor_tensor(job_e, job_e, experts_of, ALU.add))
                listed(dve.tensor_copy(job[:, :], job_f[:, 0:3 + JOBS]))
                assert js[0] == LIST_STEPS
                dve.sem_inc(passed.sem, 1)
                with dve.Fori(0, PAIRS // 4 - 1) as i:
                    for n in range(4):
                        pair_turn(Pair(i, n + 1), Pair(i, n))
                pair_turn(Pair(0, PAIRS - 3), Pair(0, PAIRS - 4), choose=False, spread=False)
                number, seen = entry(dve, 0, JOBS), entry(dve, 1, DEPTH * JOBS)

                def select_job(j):
                    n = seen + j
                    e = entry(dve, 3 + j, E - 1)
                    dve.wait_ge(*gth_ps.at(l, 4 * QUADS))
                    dve.wait_ge(*gm_ok.at(l, QUADS))
                    dve.wait_ge(*job_tr.at(n, 0))
                    for t in range(TT):
                        dve.tensor_scalar(sm[:, 0, t, 0:P], slots, job_f[:, bass.ds(3 + JOBS + j, 1)],
                                          rank[:, t, bass.ds(e, 1)], ALU.add, ALU.is_equal)
                    for s in (0, CAP):
                        ins = dve.tensor_scalar(job_pick[0:3 * E, s:s + CAP], owner[0:3 * E, 0:CAP],
                                                iota_e[0:3 * E, bass.ds(e, 1)], None, ALU.is_equal)
                    ins.then_inc(job_sm.sem, 1)
                    return e

                def spread_job(j, e):
                    dve.wait_ge(*ag_ps.at(l, PAIRS - 2))
                    dve.wait_ge(*job_sm.at(seen + j, 1))
                    for t in range(TT):
                        dve.tensor_scalar(gm[:, 0, t, 0:P], sm[:, 0, t, 0:P].bitcast(F32), halfg[:, t, bass.ds(e, 1)], None,
                                          ALU.mult)

                def job_tiles_out(j, c):
                    dve.wait_ge(*job_gth.at(seen + j, c + 1))
                    for dt in range(2):
                        k = 2 * c + dt
                        ins = dve.tensor_scalar(xT_job[:, k, :], bank[3][:, dt * SEQ:dt * SEQ + P],
                                                pb[:, G2 + k:G2 + k + 1], None, ALU.mult)
                    ins.then_inc(job_xd.sem, 1)

                def start(j):
                    n = seen + j
                    dve.wait_ge(*job_gu.at(n, 1))
                    dve.wait_ge(*act_ok.at(l, PAIRS))
                    dve.wait_ge(*job_step.at(n, 0))
                    dve.tensor_scalar(g, bank[0][:, 0:FF], LIMIT, None, ALU.min)
                    dve.tensor_scalar(u, bank[0][:, FF:2 * FF], LIMIT, -LIMIT, ALU.min, ALU.max).then_inc(job_step.sem, 1)
                    dve.wait_ge(*job_th.at(n, 1))
                    dve.scalar_tensor_tensor(th, th, 1.0, g, ALU.add, ALU.mult).then_inc(job_step.sem, 1)
                    dve.wait_ge(*job_step.at(n, 2))
                    dve.wait_ge(*ag_ps.at(l, PAIRS))
                    dve.wait_ge(*job_tr.at(n, 0))
                    dve.scalar_tensor_tensor(act_e, u, 1.0, th, ALU.add, ALU.mult).then_inc(job_step.sem, 1)

                def finish(j):
                    n = seen + j
                    dve.wait_ge(*job_tr.at(n, 1))
                    dve.wait_ge(*acc_ps.at(l, PAIRS))
                    dve.wait_ge(*job_acc.at(n, 0))
                    dve.tensor_scalar(home[:, :], bank[2][:, 0:SEQ], 0.0, None, ALU.is_gt).then_inc(job_home.sem, 1)
                    for h in range(2):
                        dve.wait_ge(*job_hi.at(n, h + 1))
                        dve.scalar_tensor_tensor(y_lo[h][:, :], bank[1 + h][:, :], gcol[:, 0:1], y_hi[:, h * 512:h * 512 + 512],
                                                 ALU.mult, ALU.subtract).then_inc(job_lo.sem, 1)

                def tail(job):
                    if job:
                        e = select_job(0)
                    pair_turn(Pair(0, PAIRS - 2), Pair(0, PAIRS - 3), choose=False, spread=False, more=False, job=1 if job else None)
                    if job:
                        spread_job(0, e)
                    pair_turn(Pair(0, PAIRS - 1), Pair(0, PAIRS - 2), choose=False, spread=False, more=False, another=False,
                              job=3 if job else None)
                    homes(Pair(0, PAIRS - 1))
                    if job:
                        start(0)
                    down_rest(Pair(0, PAIRS - 1))
                    if job:
                        finish(0)

                def another_job(j):
                    spread_job(j, select_job(j))
                    job_tiles_out(j, 1)
                    job_tiles_out(j, 3)
                    start(j)
                    finish(j)
                for_jobs(dve, number, tail, another_job)
                dve.wait_ge(*acc_ps.at(l, PAIRS))
                dve.wait_ge(*job_acc.at(seen + number, 0))
                for t in range(TT):
                    for h in range(2):
                        xs = x[:, t, h * 512:h * 512 + 512]
                        dve.tensor_tensor(xs, bank[4 + 2 * t + h][:, :], xs, ALU.add).then_inc(x_ok.sem, 1)

        @block.scalar
        def _(act):
            for c in (ag_ok, gc_ok, y_rd):
                act.sem_inc(c.sem, 1)
            act.wait_ge(x_landed.sem, 16)
            with act.Fori(0, DEPTH) as l:
                def squares(c):
                    for t in range(TT):
                        act.wait_ge(*(wo_ok.at(l, 10 + 2 * t) if c else x_ok.at(l, 2 * t - 2)))
                        act.activation(xn[:, t, :], x[:, t, :], ACT.Square, accum_out=ms[:, 2 * c + t:2 * c + t + 1]
                                       ).then_inc(ms_ok.sem, 1)

                def turned(c, gain):
                    for b in (0, 2):
                        act.wait_ge(*tr_ok.at(l, 4 * c + b + 1))
                        for dt in range(2):
                            k = 2 * b + dt
                            act.activation(hT[:, k, :], bank[b][:, dt * SEQ:dt * SEQ + SEQ], ACT.Copy,
                                           scale=gain[:, k:k + 1]).then_inc(hT_act.sem, 1)

                squares(0)
                act.wait_ge(*pa_in.at(l, 16))
                turned(0, pa[:, G1:G1 + KD])
                act.wait_ge(*sp_dve.at(l, 2))
                act.activation(sp[:, 2, :], sp[:, 1, :], ACT.Exp, scale=-1.0).then_inc(sp_act.sem, 1)
                for w in range(4):
                    act.wait_ge(*proj_ok.at(l, w + 1))
                    if w:
                        act.wait_ge(*hsum_ok.at(l, w))
                    act.activation(sq[:, :], bank[4 + w][:, :], ACT.Square).then_inc(sq_ok.sem, 1)
                for n, dst in enumerate((up[:, :, CONV - 1:], gt[:, :, :], pp[:, :, PAD:])):
                    act.wait_ge(*proj_ok.at(l, 5 + n))
                    act.copy(dst, bank[n][:, :].rearrange("p (c s) -> p c s", c=2)).then_inc(proj_free.sem, 1)
                for w in (0, 2):
                    act.wait_ge(*qkT_ps.at(l, w + 1))
                    act.copy(qkT[:, w // 2, :, 0:P], bank[4 + w][:, :].rearrange("p (c s) -> p c s", c=4)
                             ).then_inc(qkT_ok.sem, 1)
                act.wait_ge(*proj_ok.at(l, 8))
                act.copy(vt[:, 0, :], bank[3][:, :]).then_inc(proj_free.sem, 1)
                for b, dst in enumerate((th_r, th_i)):
                    act.wait_ge(*lru_ps.at(l, b + 1))
                    if b == 0:
                        act.wait_ge(*sp_dve.at(l, 3))
                    for c in range(2):
                        act.activation(dst[:, c, :], bank[b][:, c * SEQ:c * SEQ + SEQ], ACT.Tanh,
                                       bias=hb[:, 2 * b + c:2 * b + c + 1], scale=0.5).then_inc(lru_a.sem, 1)
                act.wait_ge(*lru_d.at(l, 2))
                act.activation(ea[:, :, :], la[:, :, :], ACT.Exp).then_inc(lru_a.sem, 1)
                act.activation(tn[:, :, :], la[:, :, :], ACT.Tanh, scale=-1.0).then_inc(lru_a.sem, 1)
                act.wait_ge(*gelu_p.at(l, 3))
                act.activation(gl[:, :, :], gl[:, :, :], ACT.Tanh, scale=0.7978845608028654).then_inc(gelu_a.sem, 1)

                def exponentials(h):
                    for t, (a, b) in enumerate(((0, P), (P, KEYS))):
                        act.wait_ge(*s_ok.at(l, 2 * h + t + 1))
                        act.activation(prob[:, h % 2, a:b], prob[:, h % 2, a:b], ACT.Exp,
                                       bias=nmax[:, 2 * h + t:2 * h + t + 1], scale=-1.0,
                                       accum_out=den[:, 2 * h + t:2 * h + t + 1]).then_inc(e_ok.sem, 1)

                def probs_out(h):
                    act.wait_ge(*pt_ps.at(l, h + 1))
                    act.copy(probT[:, h % 2, :], bank[6 + h % 2][:, 0:KEYS]).then_inc(pt_ok.sem, 1)
                exponentials(0)
                exponentials(1)
                act.wait_ge(*lru_d.at(l, 6))
                act.activation(tn[:, :, :], tn[:, :, :], ACT.Sqrt).then_inc(lru_a.sem, 1)
                act.wait_ge(*proj_ok.at(l, 9))
                act.copy(vt[:, 1, :], bank[3][:, :]).then_inc(proj_free.sem, 1)

                probs_out(0)
                for h in range(2, HEADS + 2):
                    if h < HEADS:
                        exponentials(h)
                    if h % 2:
                        pr = (h - 3) // 2
                        act.wait_ge(*o_ps.at(l, pr + 1))
                        act.activation(ysq[:, 4 + pr, :], bank[pr % 2][:, 0:SEQ], ACT.Square).then_inc(ysq_at.sem, 1)
                    if h < HEADS + 1:
                        probs_out(h - 1)

                squares(1)
                act.wait_ge(*pb_in.at(l, 16))
                turned(1, pb[:, G2:G2 + KD])
                for t in range(TT):
                    act.wait_ge(*xn_ok.at(l, 3 + t))
                    act.copy(xs2[:, 0, t, :], xn[:, t, :]).then_inc(x0_ok.sem, 1)
                act.wait_ge(*rt.at(l, 7))
                for t in range(TT):
                    act.activation(ptop[:, t, :], top[:, t, 0:TOPK], ACT.Exp, bias=ntop[:, t:t + 1],
                                   accum_out=psum4[:, t:t + 1]).then_inc(rt_act.sem, 1)

                def tiles_out(quad, par, c, b=3):
                    act.wait_ge(*gth_ps.at(l, 4 * quad + c + 1))
                    for dt in range(2):
                        k = 2 * c + dt
                        ins = act.activation(xT[:, par, k, :], bank[b][:, dt * SEQ:dt * SEQ + SEQ], ACT.Copy,
                                             scale=pb[:, G2 + k:G2 + k + 1])
                    ins.then_inc(xT_act.sem, 1)

                def turned_out(p):
                    act.wait_ge(*ag_ps.at(l, p.n + 1))
                    act.wait_ge(*dn_ps.at(l, 2 * p.n))
                    act.copy(ag[:, :, :], bank[1][:, 0:SEQ].rearrange("p (n s) -> p n s", n=2)).then_inc(ag_ok.sem, 1)
                    act.wait_ge(*ylo_ok.at(l, 2 * p.n))
                    act.wait_ge(*gc_ok.at(l, p.n))
                    act.wait_ge(*home_ok.at(l, p.n + 1))
                    act.activation(g_dump, bank[2][:, 0:SEQ], ACT.Copy, accum_out=gcol[:, 0:1]).then_inc(gc_ok.sem, 1)

                def tanh(p):
                    act.wait_ge(*gu_rd.at(l, p.n + 1))
                    act.wait_ge(*act_ok.at(l, p.n))
                    act.activation(th, g, ACT.Tanh, scale=0.5 * ALPHA).then_inc(sg_ok.sem, 1)

                def down_out(p):
                    for h in range(2):
                        act.wait_ge(*dn_ps.at(l, 2 * p.n + h + 1))
                        if h == 0:
                            act.wait_ge(*gc_ok.at(l, p.n + 1))
                            act.wait_ge(*acc_ps.at(l, p.n))
                        act.activation(y_hi[:, h * 512:h * 512 + 512], bank[1 + h][:, :], ACT.Copy, scale=gcol[:, 0:1]
                                       ).then_inc(y_rd.sem, 1)

                tiles_out(0, 0, 0, 0)
                tiles_out(0, 0, 2, 2)

                def pair_turn(p, before, more=True, job=None):
                    if before:
                        turned_out(before)
                    tanh(p)
                    if job is not None:
                        job_tiles_out(0, job)
                    if more:
                        tiles_out(p.quad + 1, 1 - p.par, p.slot)
                    if before:
                        down_out(before)
                pair_turn(Pair(0, 0), None)
                with act.Fori(0, PAIRS // 4 - 1) as i:
                    for n in range(4):
                        pair_turn(Pair(i, n + 1), Pair(i, n))
                pair_turn(Pair(0, PAIRS - 3), Pair(0, PAIRS - 4))
                alone(act, *list_ok.at(l, LIST_STEPS))
                number, seen = entry(act, 0, JOBS), entry(act, 1, DEPTH * JOBS)

                def job_tiles_out(j, c):
                    act.wait_ge(*job_gth.at(seen + j, c + 1))
                    for dt in range(2):
                        k = 2 * c + dt
                        ins = act.activation(xT_job[:, k, :], bank[3][:, dt * SEQ:dt * SEQ + P], ACT.Copy,
                                             scale=pb[:, G2 + k:G2 + k + 1])
                    ins.then_inc(job_xa.sem, 1)

                def start(j):
                    act.wait_ge(*job_step.at(seen + j, 1))
                    act.activation(th, g, ACT.Tanh, scale=0.5 * ALPHA).then_inc(job_th.sem, 1)

                def finish(j):
                    n = seen + j
                    act.wait_ge(*job_tr.at(n, 1))
                    act.wait_ge(*job_dn.at(n, 0))
                    act.copy(ag[:, :, :], bank[1][:, 0:SEQ].rearrange("p (n s) -> p n s", n=2)).then_inc(job_ag.sem, 1)
                    act.wait_ge(*ylo_ok.at(l, 2 * PAIRS))
                    act.wait_ge(*gc_ok.at(l, PAIRS))
                    act.wait_ge(*job_lo.at(n, 0))
                    act.wait_ge(*job_home.at(n, 1))
                    act.activation(g_dump, bank[2][:, 0:SEQ], ACT.Copy, accum_out=gcol[:, 0:1]).then_inc(job_gc.sem, 1)
                    for h in range(2):
                        act.wait_ge(*job_dn.at(n, h + 1))
                        if h == 0:
                            act.wait_ge(*job_gc.at(n, 1))
                            act.wait_ge(*acc_ps.at(l, PAIRS))
                            act.wait_ge(*job_acc.at(n, 0))
                        act.activation(y_hi[:, h * 512:h * 512 + 512], bank[1 + h][:, :], ACT.Copy, scale=gcol[:, 0:1]
                                       ).then_inc(job_hi.sem, 1)

                def tail(job):
                    pair_turn(Pair(0, PAIRS - 2), Pair(0, PAIRS - 3), more=False, job=0 if job else None)
                    pair_turn(Pair(0, PAIRS - 1), Pair(0, PAIRS - 2), more=False, job=2 if job else None)
                    turned_out(Pair(0, PAIRS - 1))
                    if job:
                        start(0)
                    down_out(Pair(0, PAIRS - 1))
                    if job:
                        finish(0)

                def another_job(j):
                    job_tiles_out(j, 0)
                    job_tiles_out(j, 2)
                    start(j)
                    finish(j)
                for_jobs(act, number, tail, another_job)

        @block.gpsimd
        def _(pool):
            pool.wait_ge(once.sem, 32)
            pool.wait_ge(zeroed.sem, 2)
            with pool.Fori(0, DEPTH) as l:
                def inverse_roots(dst, src, n, scale, after, mid, ok, k):
                    alone(pool, *after)
                    pool.tensor_scalar(dst, src, scale, EPS, ALU.mult, ALU.add).then_inc(mid.sem, 1)
                    pool.wait_ge(*mid.at(l, k))
                    pool.tensor_tensor(dst, dst, half[:, 0:n], ALU.pow).then_inc(ok.sem, 1)

                def token_roots(c):
                    for t in range(TT):
                        a = 2 * c + t
                        inverse_roots(rstd[:, a:a + 1], ms[:, a:a + 1], 1, 1.0 / D, ms_ok.at(l, a + 1), rstd_mid, rstd_ok, a + 1)
                token_roots(0)
                for w in range(4):
                    inverse_roots(hs[:, w, 8:16], hs[:, w, 0:8], 8, 1.0 / DH, hsum_ok.at(l, w + 1), hr_mid, hr_ok, w + 1)

                pool.wait_ge(*proj_free.at(l, 2))
                pool.tensor_tensor(gl[:, :, :], gt[:, :, :], gt[:, :, :], ALU.mult).then_inc(gelu_p.sem, 1)
                alone(pool, *gelu_p.at(l, 1))
                pool.tensor_scalar(gl[:, :, :], gl[:, :, :], 0.044715, 1.0, ALU.mult, ALU.add).then_inc(gelu_p.sem, 1)
                pool.wait_ge(*gelu_p.at(l, 2))
                pool.tensor_tensor(gl[:, :, :], gl[:, :, :], gt[:, :, :], ALU.mult).then_inc(gelu_p.sem, 1)

                pool.wait_ge(*proj_free.at(l, 3))
                N = PAD + SEQ
                steps = [0]

                def turn(out_, in0, in1, op):
                    pool.tensor_tensor(out_, in0, in1, op).then_inc(pool_p.sem, 1)
                    steps[0] += 1
                    pool.wait_ge(*pool_p.at(l, steps[0]))
                turn(p2[:, :, 1:N], pp[:, :, 1:N], pp[:, :, 0:N - 1], ALU.add)
                turn(p4[:, :, 3:N], p2[:, :, 3:N], p2[:, :, 1:N - 2], ALU.add)
                pool.wait_ge(*rope.at(l, 24))
                turn(pooled[0:64, 0, :], p2[0:64, 0, PAD:], invc[0:64, 0, :], ALU.mult)
                turn(pooled[64:P, 0, :], p4[64:P, 0, PAD:], invc[64:P, 0, :], ALU.mult)
                turn(p2[:, 1, 7:N], p4[:, 1, 7:N], p4[:, 1, 3:N - 4], ALU.add)
                turn(pooled[0:64, 1, :], p2[0:64, 1, PAD:], invc[0:64, 1, :], ALU.mult)
                turn(p4[64:P, 1, PAD:N], p2[64:P, 1, PAD:N], p2[64:P, 1, PAD - 8:N - 8], ALU.add)
                turn(pooled[64:P, 1, :], p4[64:P, 1, PAD:], invc[64:P, 1, :], ALU.mult)
                turn(pooled[:, :, :], pooled[:, :, :], pp[:, :, PAD:], ALU.subtract)

                alone(pool, *gelu_a.at(l, 1))
                pool.tensor_scalar(gl[:, :, :], gl[:, :, :], 0.5, 0.5, ALU.mult, ALU.add).then_inc(gelu_p.sem, 1)
                pool.wait_ge(*gelu_p.at(l, 4))
                pool.tensor_tensor(gl[:, :, :], gl[:, :, :], gt[:, :, :], ALU.mult).then_inc(gelu_p.sem, 1)
                pool.wait_ge(*pool_ok.at(l, 2))
                pool.tensor_tensor(ysq[:, 0:2, :], pooled[:, :, :], pooled[:, :, :], ALU.mult).then_inc(ysq_pl.sem, 2)
                pool.wait_ge(*lru_d.at(l, 12))
                pool.tensor_tensor(ysq[:, 2:4, :], xc[:, :, :], xc[:, :, :], ALU.mult).then_inc(ysq_pl.sem, 2)
                inverse_roots(grs[:, 0:4], gstat[:, 0:4], 4, 1.0 / 256, st_ok.at(l, 1), gr_mid, gr_ok, 1)
                inverse_roots(grs[:, 4:6], gstat[:, 4:6], 2, 1.0 / ATT, st_ok.at(l, 2), gr_mid, gr_ok, 2)
                token_roots(1)
                b_0, b_1 = (ysq[:, n, :].bitcast(BF16) for n in range(2))
                w = slice(0, 3 * E)
                alone(pool, *bsrc_in.at(l, 16))
                pool.tensor_copy(b_0[w, :], b_src[w, :]).then_inc(brow_ok.sem, 1)
                pool.wait_ge(*brow_ok.at(l, 1))
                pool.tensor_tensor(b_rest[w, :], b_src[w, :], b_0[w, :], ALU.subtract).then_inc(brow_ok.sem, 1)
                alone(pool, *brow_ok.at(l, 2))
                pool.tensor_copy(b_1[w, :], b_rest[w, :]).then_inc(brow_ok.sem, 1)
                alone(pool, *brow_ok.at(l, 3))
                pool.tensor_copy(b_rows[0:E, :], b_0[0:E, :]).then_inc(brow_ok.sem, 1)
                alone(pool, *brow_ok.at(l, 4))
                pool.tensor_copy(b_rows[E:2 * E, :], b_1[E:2 * E, :]).then_inc(brow_ok.sem, 1)
                pool.wait_ge(*brow_ok.at(l, 5))
                pool.tensor_tensor(b_rows[2 * E:3 * E, :], b_rest[2 * E:3 * E, :], b_1[2 * E:3 * E, :], ALU.subtract
                                   ).then_inc(brow_ok.sem, 1)


def kernel(x, norm1_g, w_in, pool_w, pool_scale, conv_w, conv_b, lru_wa, lru_ba, lru_wx, lru_bx, lru_lambda,
           q_norm_g, k_norm_g, out_norm_g, w_out, norm2_g, router_w, router_b, w_gate_up, b_gate_up, w_down, b_down):
    import ml_dtypes
    import numpy as np
    import concourse.bacc as bacc
    from concourse.bass_utils import run_bass_kernel_spmd

    A = np.asarray

    def columns(a, n):
        a = A(a).reshape(DEPTH, -1, n, P)
        return a.transpose(0, 3, 1, 2).reshape(DEPTH, P, -1)

    def block_diagonal(w):
        m = np.zeros((DEPTH, P, 2, P), np.float32)
        for b in range(4):
            r = slice(64 * (b % 2), 64 * (b % 2) + 64)
            m[:, r, b // 2, r] = A(w)[:, b]
        return m.reshape(DEPTH, P, 2 * P)

    def spread(a):
        return np.broadcast_to(A(a)[:, None, :], (DEPTH, P, a.shape[-1]))

    small_a = np.concatenate([
        columns(norm1_g, 8), columns(out_norm_g, 8), columns(pool_scale, 2), columns(conv_w, 2), columns(conv_b, 2),
        columns(lru_ba, 2), columns(lru_bx, 2), columns(lru_lambda, 2), block_diagonal(lru_wa), block_diagonal(lru_wx),
        block_diagonal(pool_w), spread(q_norm_g), spread(k_norm_g)], axis=2)
    rw = A(router_w).reshape(DEPTH, KD, P, E).transpose(0, 2, 1, 3).reshape(DEPTH, P, KD * E)
    rb = np.zeros((DEPTH, P, 1), np.float32)
    rb[:, 0:E, 0] = A(router_b)
    small_b = np.concatenate([columns(norm2_g, 8), rw, rb], axis=2)
    w_in_p = A(w_in).reshape(DEPTH, KD, P, IN_W).transpose(0, 2, 1, 3)
    w_out_p = A(w_out).reshape(DEPTH, KD, P, D).transpose(0, 2, 1, 3)
    gu = A(w_gate_up).reshape(DEPTH * E, KD, P, 2 * FF).transpose(0, 2, 1, 3).reshape(DEPTH * E, P, GU)
    dn = A(w_down).reshape(DEPTH * E, 2, P, D).transpose(0, 2, 1, 3).reshape(DEPTH * E, P, DN)
    experts = np.concatenate([gu, dn], axis=2)

    pos = np.arange(SEQ, dtype=np.float32)
    inv_freq = (np.float32(10000.0) ** (-np.arange(0, DH, 2, dtype=np.float32) / np.float32(DH))).astype(np.float32)
    ang = (pos[:, None] * inv_freq[None, :]).astype(np.float32)
    cos = np.concatenate([np.cos(ang), np.cos(ang)], axis=1)
    sin = np.concatenate([-np.sin(ang), np.sin(ang)], axis=1)

    def by_token(a):
        return a.reshape(TT, P, -1).transpose(1, 0, 2).reshape(P, -1)
    dist = np.arange(SEQ)[:, None] - np.arange(SEQ)[None, :]
    seen = (dist >= 0) * ((dist <= 128).astype(np.float64) + (dist % 4 == 0) + (dist % 16 == 0))
    bias = np.where(seen > 0, np.log(np.maximum(seen, 1.0)), -1e30)
    windows = np.array([[2, 4], [8, 16]])
    length = np.minimum(np.arange(1, SEQ + 1)[None, None, :], np.repeat(windows, 64, axis=1)[:, :, None])
    consts = np.concatenate([
        np.eye(P), by_token(cos), by_token(sin), bias[0:P, 0:P], bias[P:SEQ, :],
        (1.0 / length).transpose(1, 0, 2).reshape(P, -1), np.broadcast_to(np.arange(E), (P, E)),
        np.full((P, 16), -0.5), np.ones((P, 1)), np.broadcast_to(np.arange(1, P + 1), (P, P)),
        np.arange(P)[:, None] % E - (np.arange(P)[None, :] >= CAP), np.ones((P, E))], axis=1).astype(np.float32)
    consts_b = np.concatenate([np.triu(np.ones((P, P)), 1), np.ones((P, P))], axis=1).astype(ml_dtypes.bfloat16)

    arrays = {
        "x_in": A(x).reshape(TT, P, D).transpose(1, 0, 2), "small_a": small_a, "small_b": small_b, "w_in": w_in_p.reshape(DEPTH, P, -1),
        "w_out": w_out_p.reshape(DEPTH, P, -1), "experts": experts,
        "b_gate_up": np.concatenate([A(b_gate_up)] * 3, axis=1), "b_down": A(b_down), "consts": consts, "consts_b": consts_b,
    }
    arrays = {k: np.ascontiguousarray(v) for k, v in arrays.items()}
    nc = bacc.Bacc("TRN2", target_bir_lowering=False, num_devices=1)
    args = [nc.dram_tensor(k, v.shape, mybir.dt.from_np(v.dtype), kind="ExternalInput").ap() for k, v in arrays.items()]
    out = nc.dram_tensor("out", (P, TT, D), F32, kind="ExternalOutput").ap()
    build(nc, *args, out)
    r = run_bass_kernel_spmd(nc, [arrays], core_ids=[0])
    return r.results[0]["out"].transpose(1, 0, 2).reshape(1, SEQ, D)
```
